# Optimizing a Trainium2 kernel written in Bass

```python
import jax, jax.numpy as jnp
from jax import lax
import numpy as np

D_MODEL = 1024
BATCH = 1
SEQ = 256
DEPTH = 1

MEM_LEN = 256
N_MIXERS = 4
GROUP_WIDTH = D_MODEL // N_MIXERS
N_HEADS = 4
HEAD_DIM = GROUP_WIDTH // N_HEADS
GLA_KEY_DIM = HEAD_DIM // 2
GLA_LOWRANK = 16
GLA_GATE_NORM = 16.0
GDN_CONV = 4
CHUNK = 64
ROPE_BASE = 10000.0
XATTN_HEADS = 4
XATTN_HEAD_DIM = D_MODEL // XATTN_HEADS
D_FF = 2816
FFN_CONV = 3
EPS = 1e-6

IN_SPLITS = (
    GROUP_WIDTH, GROUP_WIDTH, GROUP_WIDTH, GROUP_WIDTH,
    GROUP_WIDTH, GROUP_WIDTH, GROUP_WIDTH, N_HEADS, N_HEADS, GROUP_WIDTH,
    N_HEADS * GLA_KEY_DIM, N_HEADS * GLA_KEY_DIM, GROUP_WIDTH, GLA_LOWRANK, GROUP_WIDTH,
    GROUP_WIDTH, GROUP_WIDTH, GROUP_WIDTH, GROUP_WIDTH,
)
IN_WIDTH = sum(IN_SPLITS)


def _rmsnorm(x, w):
    xf = x.astype(jnp.float32)
    y = xf * lax.rsqrt(jnp.mean(xf * xf, axis=-1, keepdims=True) + EPS)
    return (y * w.astype(jnp.float32)).astype(x.dtype)

def _norm_f32(x):
    return x * lax.rsqrt(jnp.mean(x * x, axis=-1, keepdims=True) + EPS)

def _l2norm(x):
    return x * lax.rsqrt(jnp.sum(x * x, axis=-1, keepdims=True) + EPS)

def _rope(x, positions):
    d = x.shape[-1]
    freqs = ROPE_BASE ** (-jnp.arange(0, d, 2, dtype=jnp.float32) / d)
    ang = positions.astype(jnp.float32)[..., None] * freqs
    cos, sin = jnp.cos(ang)[:, :, None, :], jnp.sin(ang)[:, :, None, :]
    x1, x2 = jnp.split(x, 2, axis=-1)
    return jnp.concatenate([x1 * cos - x2 * sin, x1 * sin + x2 * cos], axis=-1)

def _causal_dwconv(x, w):
    k, c = w.shape
    return lax.conv_general_dilated(
        x, w[:, None, :].astype(x.dtype), window_strides=(1,), padding=[(k - 1, 0)],
        dimension_numbers=('NWC', 'WIO', 'NWC'), feature_group_count=c)

def _to_chunks(t):
    b, tt, h = t.shape[:3]
    t = t.reshape((b, tt // CHUNK, CHUNK, h) + t.shape[3:])
    return jnp.moveaxis(t, 3, 1)

def _from_chunks(t):
    b, h, n, c, d = t.shape
    return jnp.moveaxis(t, 1, 3).reshape(b, n * c, h, d)

def _retention_chunked(q, k, v, log_gamma):
    c = q.shape[3]
    idx = jnp.arange(c, dtype=jnp.float32)
    lg = log_gamma[:, None]
    rel = idx[:, None] - idx[None, :]
    decay = jnp.where(rel >= 0, jnp.exp(lg[:, :, None] * jnp.maximum(rel, 0.0)), 0.0)
    scores = jnp.einsum('bhncd,bhnsd->bhncs', q, k) * decay[None, :, None]
    o_intra = jnp.einsum('bhncs,bhnsv->bhncv', scores, v)
    q_decay = jnp.exp(lg * (idx + 1.0))
    k_decay = jnp.exp(lg * (c - 1.0 - idx))
    chunk_decay = jnp.exp(log_gamma * c)
    kv = jnp.einsum('bhncd,bhncv->bhndv', k * k_decay[None, :, None, :, None], v)

    def step(state, inp):
        kv_n, q_n = inp
        o = jnp.einsum('bhcd,bhdv->bhcv', q_n, state) * q_decay[None, :, :, None]
        state = state * chunk_decay[None, :, None, None] + kv_n
        return state, o

    b, h, _, _, dk = q.shape
    s0 = jnp.zeros((b, h, dk, v.shape[-1]), jnp.float32)
    _, o_inter = lax.scan(step, s0, (jnp.moveaxis(kv, 2, 0), jnp.moveaxis(q, 2, 0)))
    return o_intra + jnp.moveaxis(o_inter, 0, 2)

def _gated_delta_chunked(q, k, v, beta, g):
    c = q.shape[3]
    gc = jnp.cumsum(g, axis=-1)
    causal = jnp.tril(jnp.ones((c, c), dtype=bool))
    strict = jnp.tril(jnp.ones((c, c), dtype=bool), k=-1)
    ratio = jnp.exp(jnp.where(causal, gc[..., :, None] - gc[..., None, :], -jnp.inf))
    kk = jnp.where(strict, jnp.einsum('bhncd,bhnsd->bhncs', k, k) * ratio, 0.0)
    a_mat = jnp.eye(c, dtype=jnp.float32) + beta[..., None] * kk
    gamma = jnp.exp(gc)
    u_v = lax.linalg.triangular_solve(a_mat, beta[..., None] * v, left_side=True, lower=True, unit_diagonal=True)
    w_k = lax.linalg.triangular_solve(a_mat, (beta * gamma)[..., None] * k, left_side=True, lower=True, unit_diagonal=True)
    qk = jnp.einsum('bhncd,bhnsd->bhncs', q, k) * ratio
    q_g = q * gamma[..., None]
    k_tail = k * jnp.exp(gc[..., -1:] - gc)[..., None]
    chunk_decay = jnp.exp(gc[..., -1])

    def step(state, inp):
        uv_n, w_n, qk_n, qg_n, kt_n, cd_n = inp
        u = uv_n - jnp.einsum('bhcd,bhdv->bhcv', w_n, state)
        o = jnp.einsum('bhcd,bhdv->bhcv', qg_n, state) + jnp.einsum('bhcs,bhsv->bhcv', qk_n, u)
        state = cd_n[..., None, None] * state + jnp.einsum('bhcd,bhcv->bhdv', kt_n, u)
        return state, o

    b, h, _, _, dk = q.shape
    s0 = jnp.zeros((b, h, dk, v.shape[-1]), jnp.float32)
    xs = tuple(jnp.moveaxis(t, 2, 0) for t in (u_v, w_k, qk, q_g, k_tail, chunk_decay))
    _, o = lax.scan(step, s0, xs)
    return jnp.moveaxis(o, 0, 2)

def _gated_linear_chunked(q, k, v, log_f):
    c = q.shape[3]
    gc = jnp.cumsum(log_f, axis=3)
    causal = jnp.tril(jnp.ones((c, c), dtype=bool))[:, :, None]

    def step(state, inp):
        q_n, k_n, v_n, g_n = inp
        diff = g_n[:, :, :, None, :] - g_n[:, :, None, :, :]
        decay = jnp.exp(jnp.where(causal, diff, -jnp.inf))
        scores = jnp.einsum('bhcd,bhsd,bhcsd->bhcs', q_n, k_n, decay)
        o = jnp.einsum('bhcs,bhsv->bhcv', scores, v_n) + jnp.einsum('bhcd,bhdv->bhcv', q_n * jnp.exp(g_n), state)
        k_tail = k_n * jnp.exp(g_n[:, :, -1:] - g_n)
        state = jnp.exp(g_n[:, :, -1])[..., None] * state + jnp.einsum('bhcd,bhcv->bhdv', k_tail, v_n)
        return state, o

    b, h, _, _, dk = q.shape
    s0 = jnp.zeros((b, h, dk, v.shape[-1]), jnp.float32)
    xs = tuple(jnp.moveaxis(t, 2, 0) for t in (q, k, v, gc))
    _, o = lax.scan(step, s0, xs)
    return jnp.moveaxis(o, 0, 2)

def _hybrid_mixer(h, positions, w_in, gdn_conv_w, gdn_a_log, gdn_dt_bias, gdn_norm_w,
                  gla_gk_up, gla_gk_bias, gla_norm_w, hgrn_lb, hgrn_norm_w, w_out):
    b, t, _ = h.shape
    f32 = jnp.float32
    z = jnp.matmul(h, w_in).astype(f32)
    split_points = [int(p) for p in np.cumsum(IN_SPLITS)[:-1]]
    (rq, rk, rv, rg, bq, bk, bv, ba, bb, bg,
     cq, ck, cv, c_lr, cg, dq, df, di, dg) = jnp.split(z, split_points, axis=-1)

    def heads(a):
        return a.reshape(b, t, N_HEADS, -1)

    q_a = _rope(heads(rq), positions)
    k_a = _rope(heads(rk), positions) * HEAD_DIM ** -0.5
    log_gamma = jnp.log(1.0 - jnp.exp2(-5.0 - jnp.arange(N_HEADS, dtype=f32)))
    o_a = _from_chunks(_retention_chunked(_to_chunks(q_a), _to_chunks(k_a), _to_chunks(heads(rv)), log_gamma))
    o_a = _norm_f32(o_a) * jax.nn.silu(heads(rg))

    qkv = jax.nn.silu(_causal_dwconv(jnp.concatenate([bq, bk, bv], axis=-1), gdn_conv_w.astype(f32)))
    q_b, k_b, v_b = jnp.split(qkv, 3, axis=-1)
    q_b = _l2norm(heads(q_b)) * HEAD_DIM ** -0.5
    k_b = _l2norm(heads(k_b))
    beta = jax.nn.sigmoid(bb)
    g_b = -jnp.exp(gdn_a_log.astype(f32)) * jax.nn.softplus(ba + gdn_dt_bias.astype(f32))
    o_b = _from_chunks(_gated_delta_chunked(_to_chunks(q_b), _to_chunks(k_b), _to_chunks(heads(v_b)),
                                            _to_chunks(beta), _to_chunks(g_b)))
    o_b = _norm_f32(o_b) * gdn_norm_w.astype(f32) * jax.nn.silu(heads(bg))

    q_c = heads(cq) * GLA_KEY_DIM ** -0.5
    log_f_c = jax.nn.log_sigmoid(jnp.matmul(c_lr, gla_gk_up.astype(f32)) + gla_gk_bias.astype(f32)) / GLA_GATE_NORM
    o_c = _from_chunks(_gated_linear_chunked(_to_chunks(q_c), _to_chunks(heads(ck)), _to_chunks(heads(cv)),
                                             _to_chunks(heads(log_f_c))))
    o_c = _norm_f32(o_c) * gla_norm_w.astype(f32) * jax.nn.silu(heads(cg))

    lb = hgrn_lb.reshape(N_HEADS, HEAD_DIM)
    f_pre = heads(df)
    log_f_d = jnp.logaddexp(jnp.log(lb), jnp.log1p(-lb) + jax.nn.log_sigmoid(f_pre))
    k_d = (1.0 - lb) * jax.nn.sigmoid(-f_pre)
    o_d = _from_chunks(_gated_linear_chunked(_to_chunks(heads(dq)), _to_chunks(k_d), _to_chunks(heads(di)),
                                             _to_chunks(log_f_d)))
    o_d = _norm_f32(o_d) * hgrn_norm_w.astype(f32) * jax.nn.silu(heads(dg))

    o = jnp.concatenate([o_a.reshape(b, t, GROUP_WIDTH), o_b.reshape(b, t, GROUP_WIDTH),
                         o_c.reshape(b, t, GROUP_WIDTH), o_d.reshape(b, t, GROUP_WIDTH)], axis=-1)
    return jnp.matmul(o.astype(h.dtype), w_out)

def _memory_cross_attn(h, mem_n, wq, wk, wv, wo):
    b, t, _ = h.shape
    m = mem_n.shape[1]
    q = jnp.matmul(h, wq).reshape(b, t, XATTN_HEADS, XATTN_HEAD_DIM)
    k = jnp.matmul(mem_n, wk).reshape(b, m, XATTN_HEADS, XATTN_HEAD_DIM)
    v = jnp.matmul(mem_n, wv).reshape(b, m, XATTN_HEADS, XATTN_HEAD_DIM)
    s = jnp.einsum('bthd,bmhd->bhtm', q, k).astype(jnp.float32) * XATTN_HEAD_DIM ** -0.5
    p = jax.nn.softmax(s, axis=-1).astype(v.dtype)
    o = jnp.einsum('bhtm,bmhd->bthd', p, v).reshape(b, t, D_MODEL)
    return jnp.matmul(o, wo)

def _conv_ffn(h, w_up, conv_w, w_down):
    u = _causal_dwconv(jnp.matmul(h, w_up), conv_w)
    gate, val = jnp.split(u, 2, axis=-1)
    return jnp.matmul(jax.nn.silu(gate) * val, w_down)

def first_inputs(seed: int = 0) -> dict:
    key = jax.random.key(seed)
    ks = jax.random.split(key, 26)
    nrm = jax.random.normal

    def gain(k, shape):
        return 1.0 + 0.02 * nrm(k, shape, jnp.float32)

    dt = jnp.exp(jax.random.uniform(ks[6], (DEPTH, N_HEADS), jnp.float32, np.log(1e-3), np.log(1e-1)))
    pos_offset = jax.random.randint(ks[2], (BATCH, 1), 0, 4096, dtype=jnp.int32)
    return {
        'x': nrm(ks[0], (BATCH, SEQ, D_MODEL), jnp.float32),
        'mem': nrm(ks[1], (BATCH, MEM_LEN, D_MODEL), jnp.float32),
        'positions': pos_offset + jnp.arange(SEQ, dtype=jnp.int32)[None, :],
        'mix_norm_w': gain(ks[3], (DEPTH, D_MODEL)),
        'w_in': nrm(ks[4], (DEPTH, D_MODEL, IN_WIDTH), jnp.float32) * D_MODEL ** -0.5,
        'gdn_conv_w': nrm(ks[5], (DEPTH, GDN_CONV, 3 * GROUP_WIDTH), jnp.float32) * GDN_CONV ** -0.5,
        'gdn_a_log': jnp.log(jax.random.uniform(ks[7], (DEPTH, N_HEADS), jnp.float32, 1.0, 16.0)),
        'gdn_dt_bias': dt + jnp.log(-jnp.expm1(-dt)),
        'gdn_norm_w': gain(ks[8], (DEPTH, HEAD_DIM)),
        'gla_gk_up': nrm(ks[9], (DEPTH, GLA_LOWRANK, N_HEADS * GLA_KEY_DIM), jnp.float32) * GLA_LOWRANK ** -0.5,
        'gla_gk_bias': 0.02 * nrm(ks[10], (DEPTH, N_HEADS * GLA_KEY_DIM), jnp.float32),
        'gla_norm_w': gain(ks[11], (DEPTH, HEAD_DIM)),
        'hgrn_lb_logits': 0.1 * nrm(ks[12], (DEPTH, GROUP_WIDTH), jnp.float32),
        'hgrn_norm_w': gain(ks[13], (DEPTH, HEAD_DIM)),
        'w_out': nrm(ks[14], (DEPTH, D_MODEL, D_MODEL), jnp.float32) * D_MODEL ** -0.5,
        'xattn_norm_w': gain(ks[15], (DEPTH, D_MODEL)),
        'mem_norm_w': gain(ks[16], (D_MODEL,)),
        'xattn_wq': nrm(ks[17], (DEPTH, D_MODEL, D_MODEL), jnp.float32) * D_MODEL ** -0.5,
        'xattn_wk': nrm(ks[18], (DEPTH, D_MODEL, D_MODEL), jnp.float32) * D_MODEL ** -0.5,
        'xattn_wv': nrm(ks[19], (DEPTH, D_MODEL, D_MODEL), jnp.float32) * D_MODEL ** -0.5,
        'xattn_wo': nrm(ks[20], (DEPTH, D_MODEL, D_MODEL), jnp.float32) * D_MODEL ** -0.5,
        'ffn_norm_w': gain(ks[21], (DEPTH, D_MODEL)),
        'ffn_up': nrm(ks[22], (DEPTH, D_MODEL, 2 * D_FF), jnp.float32) * D_MODEL ** -0.5,
        'ffn_conv_w': nrm(ks[23], (DEPTH, FFN_CONV, 2 * D_FF), jnp.float32) * FFN_CONV ** -0.5,
        'ffn_down': nrm(ks[24], (DEPTH, D_FF, D_MODEL), jnp.float32) * D_FF ** -0.5,
        'final_norm_w': gain(ks[25], (D_MODEL,)),
    }

def first_block(x, mem, positions, mix_norm_w, w_in, gdn_conv_w, gdn_a_log, gdn_dt_bias, gdn_norm_w,
              gla_gk_up, gla_gk_bias, gla_norm_w, hgrn_lb_logits, hgrn_norm_w, w_out,
              xattn_norm_w, mem_norm_w, xattn_wq, xattn_wk, xattn_wv, xattn_wo,
              ffn_norm_w, ffn_up, ffn_conv_w, ffn_down, final_norm_w):
    lb_all = jnp.cumsum(jax.nn.softmax(hgrn_lb_logits.astype(jnp.float32), axis=0), axis=0)
    lb_all = lb_all - lb_all[0]
    mem_n = _rmsnorm(mem, mem_norm_w)
    h = x
    for l in range(DEPTH):
        h = h + _hybrid_mixer(_rmsnorm(h, mix_norm_w[l]), positions, w_in[l], gdn_conv_w[l], gdn_a_log[l],
                              gdn_dt_bias[l], gdn_norm_w[l], gla_gk_up[l], gla_gk_bias[l], gla_norm_w[l],
                              lb_all[l], hgrn_norm_w[l], w_out[l])
        h = h + _memory_cross_attn(_rmsnorm(h, xattn_norm_w[l]), mem_n, xattn_wq[l], xattn_wk[l],
                                   xattn_wv[l], xattn_wo[l])
        h = h + _conv_ffn(_rmsnorm(h, ffn_norm_w[l]), ffn_up[l], ffn_conv_w[l], ffn_down[l])
    return _rmsnorm(h, final_norm_w)


DEPTH_2 = 2

HEAD_DIM_2 = 64
HEADS_MLA = 4
HEADS_DIL = 8
HEADS_DSA = 4
D_MIX = (HEADS_MLA + HEADS_DIL + HEADS_DSA) * HEAD_DIM_2
Q_LORA = 256
KV_LORA = 128
MLA_NOPE = 64
MLA_ROPE = 32
MLA_V = HEAD_DIM_2
DIL_PAIRS = ((128, 1), (512, 4), (2048, 16))
IDX_HEADS = 8
IDX_DIM = 32
DSA_TOPK = 256
CONV_WIDTH = 3
ROPE_THETA = 500000.0
ROT_FRAC = 4
BLOCK = 128
NORM_EPS = 1e-6
DIL_PAD = 16 * BLOCK
IN_SPLITS_2 = (Q_LORA, KV_LORA, MLA_ROPE,
             3 * HEADS_DIL * HEAD_DIM_2,
             3 * HEADS_DSA * HEAD_DIM_2,
             IDX_HEADS * IDX_DIM, IDX_DIM, IDX_HEADS)
N_IN = sum(IN_SPLITS_2)


def rms_norm(x, g):
    xf = x.astype(jnp.float32)
    y = xf * lax.rsqrt(jnp.mean(xf * xf, axis=-1, keepdims=True) + NORM_EPS)
    return (y * g.astype(jnp.float32)).astype(x.dtype)

def rope_tables(seq, dim):
    inv = jnp.power(jnp.float32(ROPE_THETA), -jnp.arange(0, dim, 2, dtype=jnp.float32) / dim)
    ang = jnp.arange(seq, dtype=jnp.float32)[:, None] * inv[None, :]
    return jnp.cos(ang), jnp.sin(ang)

def apply_rope(x, cos, sin):
    h = x.shape[-1] // 2
    xf = x.astype(jnp.float32)
    x1, x2 = xf[..., :h], xf[..., h:]
    c, s = cos[None, :, None, :], sin[None, :, None, :]
    return jnp.concatenate([x1 * c - x2 * s, x2 * c + x1 * s], axis=-1).astype(x.dtype)

def partial_rope(x, cos, sin):
    r = 2 * cos.shape[-1]
    return jnp.concatenate([apply_rope(x[..., :r], cos, sin), x[..., r:]], axis=-1)

def mla_attention(c_q, c_kv, k_pe_raw, g_q, w_uq, g_kv, w_ukv, cos_a, sin_a):
    B, S, _ = c_q.shape
    q = (rms_norm(c_q, g_q) @ w_uq).reshape(B, S, HEADS_MLA, MLA_NOPE + MLA_ROPE)
    q_nope = q[..., :MLA_NOPE]
    q_pe = apply_rope(q[..., MLA_NOPE:], cos_a, sin_a)
    kv = (rms_norm(c_kv, g_kv) @ w_ukv).reshape(B, S, HEADS_MLA, MLA_NOPE + MLA_V)
    k_nope, v = kv[..., :MLA_NOPE], kv[..., MLA_NOPE:]
    k_pe = apply_rope(k_pe_raw[:, :, None, :], cos_a, sin_a)[:, :, 0]
    scale = (MLA_NOPE + MLA_ROPE) ** -0.5
    nb = S // BLOCK
    qn_b = q_nope.reshape(B, nb, BLOCK, HEADS_MLA, MLA_NOPE).transpose(1, 0, 2, 3, 4)
    qp_b = q_pe.reshape(B, nb, BLOCK, HEADS_MLA, MLA_ROPE).transpose(1, 0, 2, 3, 4)
    kpos = jnp.arange(S)

    def block(args):
        qn, qp, i = args
        s = (jnp.einsum('bqhe,bshe->bhqs', qn, k_nope).astype(jnp.float32)
             + jnp.einsum('bqhr,bsr->bhqs', qp, k_pe).astype(jnp.float32)) * scale
        qpos = i * BLOCK + jnp.arange(BLOCK)
        s = jnp.where((kpos[None, :] <= qpos[:, None])[None, None], s, -jnp.inf)
        p = jax.nn.softmax(s, axis=-1).astype(v.dtype)
        return jnp.einsum('bhqs,bshe->bqhe', p, v)

    o = lax.map(block, (qn_b, qp_b, jnp.arange(nb)))
    return o.transpose(1, 0, 2, 3, 4).reshape(B, S, HEADS_MLA, MLA_V)

def dilated_window(q, k, v, dilation, n_win):
    B, Sp, H, Dh = q.shape
    n = Sp // dilation
    nb = n // BLOCK

    def stride_split(t):
        return t.reshape(B, n, dilation, H, Dh).transpose(0, 2, 1, 3, 4)

    qs, ks, vs = stride_split(q), stride_split(k), stride_split(v)
    qb = qs.reshape(B, dilation, nb, BLOCK, H, Dh)

    def band(t):
        tp = jnp.pad(t, ((0, 0), (0, 0), (BLOCK, 0), (0, 0), (0, 0)))
        prev = tp[:, :, :n].reshape(B, dilation, nb, BLOCK, H, Dh)
        return jnp.concatenate([prev, t.reshape(B, dilation, nb, BLOCK, H, Dh)], axis=3)

    kb, vb = band(ks), band(vs)
    s = jnp.einsum('bdnqhe,bdnkhe->bdnhqk', qb, kb).astype(jnp.float32) * (Dh ** -0.5)
    qi = jnp.arange(BLOCK)[None, :, None]
    kj = jnp.arange(2 * BLOCK)[None, None, :]
    blk = jnp.arange(nb)[:, None, None]
    dist = BLOCK + qi - kj
    valid = (dist >= 0) & (dist <= n_win) & ((blk > 0) | (kj >= BLOCK))
    s = jnp.where(valid[None, None, :, None], s, -jnp.inf)
    m = jnp.max(s, axis=-1, keepdims=True)
    p = jnp.exp(s - m)
    l = jnp.sum(p, axis=-1, keepdims=True)
    o = jnp.einsum('bdnhqk,bdnkhe->bdnqhe', p / l, vb.astype(jnp.float32))
    o = o.reshape(B, dilation, n, H, Dh).transpose(0, 2, 1, 3, 4).reshape(B, Sp, H, Dh)

    def stat_back(t):
        t = t[..., 0].transpose(0, 1, 2, 4, 3).reshape(B, dilation, n, H)
        return t.transpose(0, 2, 1, 3).reshape(B, Sp, H)

    return o, stat_back(m), stat_back(l)

def dilated_attention(q, k, v):
    B, S, H, Dh = q.shape
    Sp = -(-S // DIL_PAD) * DIL_PAD
    pad = ((0, 0), (0, Sp - S), (0, 0), (0, 0))
    qp, kp, vp = jnp.pad(q, pad), jnp.pad(k, pad), jnp.pad(v, pad)
    os_, ms, ls = [], [], []
    for window, dil in DIL_PAIRS:
        o, m, l = dilated_window(qp, kp, vp, dil, window // dil)
        os_.append(o); ms.append(m); ls.append(l)
    m_all = jnp.stack(ms)
    a = jnp.stack(ls) * jnp.exp(m_all - jnp.max(m_all, axis=0))
    o = jnp.einsum('pbsh,pbshe->bshe', a, jnp.stack(os_)) / jnp.sum(a, axis=0)[..., None]
    return o[:, :S].astype(q.dtype)

def dsa_attention(q, k, v, q_idx, k_idx, w_idx):
    B, S, H, Dh = q.shape
    k_sel = min(DSA_TOPK, S // 4)
    nb = S // BLOCK
    idx_scale = (IDX_HEADS * IDX_DIM) ** -0.5
    kpos = jnp.arange(S)

    def to_blocks(t):
        return t.reshape((B, nb, BLOCK) + t.shape[2:]).swapaxes(0, 1)

    def block(args):
        qb, qib, wib, i = args
        qpos = i * BLOCK + jnp.arange(BLOCK)
        causal = kpos[None, :] <= qpos[:, None]
        dots = jnp.einsum('bqhd,bsd->bqhs', qib, k_idx).astype(jnp.float32)
        score = jnp.einsum('bqhs,bqh->bqs', jax.nn.relu(dots), wib.astype(jnp.float32) * idx_scale)
        score = jnp.where(causal[None], score, -jnp.inf)
        _, sel = lax.top_k(score, k_sel)
        flat = sel.reshape(B, BLOCK * k_sel)
        kg = jax.vmap(lambda a, j: a[j])(k, flat).reshape(B, BLOCK, k_sel, H, Dh)
        vg = jax.vmap(lambda a, j: a[j])(v, flat).reshape(B, BLOCK, k_sel, H, Dh)
        s = jnp.einsum('bqhe,bqkhe->bhqk', qb, kg).astype(jnp.float32) * (Dh ** -0.5)
        ok = sel <= qpos[None, :, None]
        s = jnp.where(ok[:, None], s, -jnp.inf)
        p = jax.nn.softmax(s, axis=-1).astype(v.dtype)
        return jnp.einsum('bhqk,bqkhe->bqhe', p, vg)

    o = lax.map(block, (to_blocks(q), to_blocks(q_idx), to_blocks(w_idx), jnp.arange(nb)))
    return o.swapaxes(0, 1).reshape(B, S, H, Dh)

def causal_dwconv(u, w, b):
    K = w.shape[0]
    S = u.shape[1]
    up = jnp.pad(u, ((0, 0), (K - 1, 0), (0, 0)))
    y = up[:, 0:S] * w[0]
    for j in range(1, K):
        y = y + up[:, j:j + S] * w[j]
    return y + b

def second_inputs(seed: int = 0) -> dict:
    key = jax.random.key(seed)
    ks = jax.random.split(key, 16)
    f32 = jnp.float32

    def nrm(k, shape, scale):
        return jax.random.normal(k, shape, f32) * scale

    def gain(k, shape):
        return 1.0 + 0.02 * jax.random.normal(k, shape, f32)

    L = DEPTH_2
    return {
        "x": nrm(ks[0], (BATCH, SEQ, D_MODEL), 1.0),
        "g_attn": gain(ks[1], (L, D_MODEL)),
        "w_in": nrm(ks[2], (L, D_MODEL, N_IN), D_MODEL ** -0.5),
        "g_q_lat": gain(ks[3], (L, Q_LORA)),
        "w_uq": nrm(ks[4], (L, Q_LORA, HEADS_MLA * (MLA_NOPE + MLA_ROPE)), Q_LORA ** -0.5),
        "g_kv_lat": gain(ks[5], (L, KV_LORA)),
        "w_ukv": nrm(ks[6], (L, KV_LORA, HEADS_MLA * (MLA_NOPE + MLA_V)), KV_LORA ** -0.5),
        "w_o": nrm(ks[7], (L, D_MIX, D_MODEL), D_MIX ** -0.5),
        "g_ffn": gain(ks[8], (L, D_MODEL)),
        "w_up": nrm(ks[9], (L, D_MODEL, 2 * D_FF), D_MODEL ** -0.5),
        "conv_w": nrm(ks[10], (L, CONV_WIDTH, 2 * D_FF), CONV_WIDTH ** -0.5),
        "conv_b": nrm(ks[11], (L, 2 * D_FF), 0.01),
        "w_down": nrm(ks[12], (L, D_FF, D_MODEL), D_FF ** -0.5),
        "g_final": gain(ks[13], (D_MODEL,)),
    }

def second_block(x, g_attn, w_in, g_q_lat, w_uq, g_kv_lat, w_ukv, w_o,
              g_ffn, w_up, conv_w, conv_b, w_down, g_final):
    B, S, _ = x.shape
    cos_a, sin_a = rope_tables(S, MLA_ROPE)
    cos_h, sin_h = rope_tables(S, HEAD_DIM_2 // ROT_FRAC)
    cos_i, sin_i = rope_tables(S, IDX_DIM // ROT_FRAC)
    offsets = np.cumsum(IN_SPLITS_2)[:-1].tolist()
    for l in range(DEPTH_2):
        h = rms_norm(x, g_attn[l])
        z = h @ w_in[l]
        c_q, c_kv, k_pe, z_dil, z_dsa, z_qi, z_ki, z_wi = jnp.split(z, offsets, axis=-1)

        o_a = mla_attention(c_q, c_kv, k_pe, g_q_lat[l], w_uq[l], g_kv_lat[l], w_ukv[l], cos_a, sin_a)

        qkv_b = z_dil.reshape(B, S, 3, HEADS_DIL, HEAD_DIM_2)
        o_b = dilated_attention(partial_rope(qkv_b[:, :, 0], cos_h, sin_h),
                                partial_rope(qkv_b[:, :, 1], cos_h, sin_h),
                                qkv_b[:, :, 2])

        qkv_c = z_dsa.reshape(B, S, 3, HEADS_DSA, HEAD_DIM_2)
        q_idx = partial_rope(z_qi.reshape(B, S, IDX_HEADS, IDX_DIM), cos_i, sin_i)
        k_idx = partial_rope(z_ki[:, :, None, :], cos_i, sin_i)[:, :, 0]
        o_c = dsa_attention(partial_rope(qkv_c[:, :, 0], cos_h, sin_h),
                            partial_rope(qkv_c[:, :, 1], cos_h, sin_h),
                            qkv_c[:, :, 2], q_idx, k_idx, z_wi)

        mix = jnp.concatenate([o_a.reshape(B, S, -1), o_b.reshape(B, S, -1),
                               o_c.reshape(B, S, -1)], axis=-1)
        x = x + mix @ w_o[l]

        h = rms_norm(x, g_ffn[l])
        u = causal_dwconv(h @ w_up[l], conv_w[l], conv_b[l])
        gate, up = u[..., :D_FF], u[..., D_FF:]
        x = x + (jax.nn.silu(gate) * up) @ w_down[l]
    return rms_norm(x, g_final)


def setup_inputs(seed=0):
    out = dict(first_inputs(seed))
    for name, value in second_inputs(seed + 1).items():
        if name != "x":
            out[name + "_2"] = value
    return out


def reference(
    x, mem, positions, mix_norm_w, w_in, gdn_conv_w, gdn_a_log, gdn_dt_bias, gdn_norm_w,
    gla_gk_up, gla_gk_bias, gla_norm_w, hgrn_lb_logits, hgrn_norm_w, w_out, xattn_norm_w,
    mem_norm_w, xattn_wq, xattn_wk, xattn_wv, xattn_wo, ffn_norm_w, ffn_up, ffn_conv_w,
    ffn_down, final_norm_w, g_attn_2, w_in_2, g_q_lat_2, w_uq_2, g_kv_lat_2, w_ukv_2, w_o_2,
    g_ffn_2, w_up_2, conv_w_2, conv_b_2, w_down_2, g_final_2,
):
    x = first_block(
        x, mem, positions, mix_norm_w, w_in, gdn_conv_w, gdn_a_log, gdn_dt_bias, gdn_norm_w,
        gla_gk_up, gla_gk_bias, gla_norm_w, hgrn_lb_logits, hgrn_norm_w, w_out, xattn_norm_w,
        mem_norm_w, xattn_wq, xattn_wk, xattn_wv, xattn_wo, ffn_norm_w, ffn_up, ffn_conv_w,
        ffn_down, final_norm_w,
    )
    return second_block(
        x, g_attn_2, w_in_2, g_q_lat_2, w_uq_2, g_kv_lat_2, w_ukv_2, w_o_2, g_ffn_2, w_up_2,
        conv_w_2, conv_b_2, w_down_2, g_final_2,
    )


_drawn_inputs = setup_inputs


def setup_inputs(seed=0):
    import zlib

    import numpy as np

    out = dict(_drawn_inputs(seed))
    spreads = {}
    factors = {'gdn_norm_w': 4.524,
     'gla_gk_bias': 5.542,
     'gla_norm_w': 3.732,
     'hgrn_norm_w': 3.496,
     'xattn_norm_w': 6.906,
     'mem_norm_w': 5.336,
     'g_q_lat_2': 8.0,
     'g_kv_lat_2': 8.0,
     'conv_b_2': 4.273,
     'g_final_2': 2.781}
    for name, (base, spread) in spreads.items():
        noise = np.random.default_rng([zlib.crc32(name.encode()), seed]).standard_normal(out[name].shape)
        drawn = base * np.exp(spread * noise) if base else spread * noise
        out[name] = __import__('jax').numpy.asarray(drawn.astype(out[name].dtype))
    for name, factor in factors.items():
        out[name] = (out[name] * factor).astype(out[name].dtype)
    return out
```

```python
from contextlib import ExitStack

import numpy as np
import concourse.bass as bass
from concourse import mybir

ALU = mybir.AluOpType
ACT = mybir.ActivationFunctionType
F32 = mybir.dt.float32
F32R = mybir.dt.float32r
I32 = mybir.dt.int32
AX_X = mybir.AxisListType.X

P = 128
T = 256
TT = T // P
D = 1024
KT = D // P
CH = 64
NCH = T // CH
FF = 2816
NFT = FF // P
NFC = NFT + 2
EPS = 1e-6
NEG = -1e30
SLOT = 3104
LAYERS = 2
TOPK = 64

ZB, ZCQ, ZCK, ZDQ, ZDF, ZRQ, ZRK, ZV, ZG, ZLR, ZBA = 0, 768, 896, 1024, 1280, 1536, 1792, 2048, 2816, 3840, 3856
ZW = 3880
IN_COLS, IN_CHUNKS = 388, 10
YCQ, YKV, YPE, YDQ, YDK, YSQ, YSK, YQI, YKI, YDV, YSV, YWI = 0, 256, 384, 416, 928, 1440, 1696, 1952, 2208, 2240, 2752, 3008
YW = 3024
IN2_COLS, IN2_CHUNKS = 378, 8
SQ_CHUNKS = 4

C_IN = 0
C_K = C_IN + IN_CHUNKS
C_V = C_K + SQ_CHUNKS
C_OUT = C_V + SQ_CHUNKS
C_Q = C_OUT + SQ_CHUNKS
C_O = C_Q + SQ_CHUNKS
C_FFN = C_O + SQ_CHUNKS
C_LAYER = C_FFN + NFC
LAYER_CHUNKS = IN2_CHUNKS + SQ_CHUNKS + NFC
END = C_LAYER + LAYERS * LAYER_CHUNKS


def section_sizes():
    out = [(C_IN, IN_CHUNKS, 8 * IN_COLS, "win"), (C_K, 4, 2048, "wk"), (C_V, 4, 2048, "wv"),
           (C_OUT, 4, 2048, "wout"), (C_Q, 4, 2048, "wq"), (C_O, 4, 2048, "wo")]
    out += ffn_sections(C_FFN, "ffn0")
    for l in range(LAYERS):
        b = C_LAYER + l * LAYER_CHUNKS
        out += [(b, IN2_CHUNKS, 8 * IN2_COLS, f"win2_{l}"), (b + IN2_CHUNKS, 4, 2048, f"wo2_{l}")]
        out += ffn_sections(b + IN2_CHUNKS + 4, f"ffn{l + 1}")
    return out


def ffn_sections(b, name):
    return [(b, 1, 2048, name + "a"), (b + 1, NFT - 1, 3072, name + "b"), (b + NFT, 2, 512, name + "c")]


def chunk_size(c):
    for b, n, size, _ in section_sizes():
        if b <= c < b + n:
            return size
    return None


def cut(size):
    return 2048 if size == 3072 else size // 2


def place(h):
    return 2 * (h % 2) + h // 2


def shape_constants():
    f = np.float32
    i = np.arange(P)
    same = (i[:, None] // CH) == (i[None, :] // CH)
    out = {"ident": np.eye(P, dtype=f)}
    sums = np.zeros((P, 8, P), f)
    levels = np.zeros((P, 7, P), f)
    for n, m in enumerate((32, 16, 8, 4, 2, 1)):
        blk, half = i // (2 * m), (i // m) % 2
        edge = blk * 2 * m + m - 1
        t1, t = i[:, None], i[None, :]
        second = (half[None, :] == 1) & (t1 > edge[None, :]) & (t1 <= t)
        first = (half[None, :] == 0) & (t1 > t) & (t1 <= edge[None, :])
        sums[:, n] = second | first
        levels[:, n] = (blk[:, None] == blk[None, :]) & (half[:, None] == 0) & (half[None, :] == 1)
    levels[:, 6] = np.eye(P)
    sums[:, 6] = same & (i[:, None] <= i[None, :])
    sums[:, 7] = same & (i[:, None] > i[None, :])
    out["sums"], out["levels"] = sums, levels
    out["incl"] = (same & (i[:, None] <= i[None, :])).astype(f)
    out["strict"] = (same & (i[:, None] < i[None, :])).astype(f)
    out["chunk_of"] = (i[:, None] // CH == np.arange(2)[None, :]).astype(f)
    lg = np.log(f(1) - np.exp2(f(-5) - np.arange(4, dtype=f))).astype(f)
    ks = f(64 ** -0.5)
    rel = (i[None, :] - i[:, None]).astype(f)
    dec = np.zeros((P, 4, P), f)
    for h in range(4):
        dec[:, place(h)] = np.where(same & (rel >= 0), np.exp(lg[h] * np.maximum(rel, 0)), 0) * ks
    out["ret_decay"] = dec
    pos = (i % CH).astype(f)
    out["ret_ktail"] = (np.exp(lg[None, :] * (f(CH) - 1 - pos[:, None])) * ks).astype(f)
    qd = np.zeros((P, 2, P), f)
    cd = np.zeros((P, 2), f)
    for p in range(2):
        h = 2 * p + i // 64
        qd[:, p] = np.exp(lg[h][:, None] * (pos[None, :] + 1))
        cd[:, p] = np.exp(lg[h] * f(CH))
    out["ret_qdecay"], out["ret_cdecay"] = qd, cd
    own = np.zeros((P, 768), f)
    for a, n in ((0, 2), (128, 2), (256, 4), (512, 2), (640, 2)):
        own[:, a:a + 64 * n] = (i[:, None] // (P // n)) == (np.arange(64 * n)[None, :] // 64)
    out["own"] = own
    q = (i[:, None] + P * np.arange(TT)[None, :])[:, :, None]
    s = np.arange(T)[None, None, :]
    out["causal"] = np.where(s <= q, 0, NEG).astype(f)
    d = q - s
    cnt = ((d >= 0) & (d <= 128)).astype(int) + ((d >= 0) & (d % 4 == 0)) + ((d >= 0) & (d % 16 == 0))
    out["dilated"] = np.where(cnt > 0, np.log(np.maximum(cnt, 1)) * 8.0, NEG).astype(f)
    out["none"] = np.zeros((P, T), f)
    out["neg_half"] = np.full((P, 16), -0.5, f)
    out["freq"] = np.broadcast_to((f(10000.0) ** (-np.arange(0, 64, 2, dtype=f) / f(64))).astype(f), (P, 32))
    for name, dim in (("a", 32), ("h", 16), ("i", 8)):
        inv = np.power(f(500000.0), -np.arange(0, dim, 2, dtype=f) / f(dim)).astype(f)
        ang = (np.arange(T, dtype=f)[:, None] * inv[None, :]).reshape(TT, P, dim // 2).transpose(1, 0, 2)
        out["cos_" + name], out["sin_" + name] = np.cos(ang).astype(f), np.sin(ang).astype(f)
    return out


def table_of(parts):
    at, out = 0, {}
    for name, shape in parts.items():
        n = int(np.prod(shape))
        out[name] = (at, shape)
        at += n
    return out, at


CONSTS = {"ident": (P,), "sums": (8, P), "levels": (7, P), "incl": (P,), "strict": (P,), "chunk_of": (2,),
          "ret_decay": (4, P), "ret_ktail": (4,), "ret_qdecay": (2, P), "ret_cdecay": (2,), "own": (768,),
          "causal": (TT, T), "dilated": (TT, T), "none": (T,), "neg_half": (16,), "freq": (32,),
          "cos_a": (TT, 16), "sin_a": (TT, 16), "cos_h": (TT, 8), "sin_h": (TT, 8), "cos_i": (TT, 4), "sin_i": (TT, 4)}
PARAMS = {"gains": (8, KT), "g_lat": (LAYERS, 3), "gdn_conv": (6, 4), "ffn_conv": (3, NFT, 2, 3),
          "ffn_bias": (3, NFT, 2)}
ROWS = {"a_log": (4,), "dt_bias": (4,), "gk_bias": (P,), "head_gains": (3, 64)}


def hybrid_two_block_kernel(nc, x_d, mem_d, pos_d, consts_d, params_d, rows_d, gfinal_d, gkup_d, lat_d,
                            win_d, wk_d, wv_d, wout_d, wq_d, wo_d, ffn_a_d, ffn_b_d, ffn_c_d, win2_d, wo2_d, out_d):
    ctx = ExitStack()
    with ctx:
        def sb(name, shape, dt=F32):
            return ctx.enter_context(nc.sbuf_tensor(name, shape, dt))

        def sem(name):
            return ctx.enter_context(nc.semaphore(name))

        ps = ctx.enter_context(nc.psum_tensor("ps", [P, 8, 512], F32))
        raw = sb("raw", [P, 2, SLOT])
        w_hi = sb("w_hi", [P, 2, SLOT], F32R)
        w_lo = sb("w_lo", [P, 2, SLOT], F32R)
        z = sb("z", [P, TT, ZW])
        res = sb("res", [P, TT, D])
        hT_hi = sb("hT_hi", [P, KT, T], F32R)
        hT_lo = sb("hT_lo", [P, KT, T], F32R)
        xn = sb("xn", [P, TT, D])
        ctab, cn = table_of(CONSTS)
        ptab, pn = table_of(PARAMS)
        rtab, rn = table_of(ROWS)
        consts = sb("consts", [P, cn])
        params = sb("params", [P, pn])
        rows = sb("rows", [P, rn])
        lat_w = sb("lat_w", [P, 1280])
        gkup = sb("gkup", [16, P])
        stat = sb("stat", [P, 64])
        hstat = sb("hstat", [P, 96])
        lstat = sb("lstat", [P, 12])
        ast = sb("ast", [P, 3, 3, 2])
        wis = sb("wis", [P, TT, 8])
        best = hstat[:, 0:8]
        posf = sb("posf", [P, TT])
        pos_i = sb("pos_i", [P, TT], I32)
        a_hi = sb("a_hi", [P, 2, T], F32R)
        a_lo = sb("a_lo", [P, 2, T], F32R)
        ARENA = 9728
        arena = sb("arena", [P, ARENA])

        def shaped(ap, shape):
            if len(shape) == 2:
                return ap.rearrange("p (a b) -> p a b", b=shape[1])
            if len(shape) == 3:
                return ap.rearrange("p (a b c) -> p a b c", b=shape[1], c=shape[2])
            if len(shape) == 4:
                return ap.rearrange("p (a b c d) -> p a b c d", b=shape[1], c=shape[2], d=shape[3])
            return ap

        def views(buf, tab):
            return {n: shaped(buf[:, at:at + int(np.prod(shape))], shape) for n, (at, shape) in tab.items()}

        def area(at, *shape):
            n = int(np.prod(shape))
            assert at + n <= ARENA, (at, n)
            return shaped(arena[:, at:at + n], shape)

        def rows_flat(buf, at, *shape):
            n = int(np.prod(shape))
            return shaped(buf[:].rearrange("p a b -> p (a b)")[:, at:at + n], shape)

        K, G, R = views(consts, ctab), views(params, ptab), views(rows, rtab)

        cqkT, dqT, kdT = area(0, 2, T), area(512, 2, T), area(1024, 2, T)
        lf = area(1536, TT, 384)
        g_b, beta, ea = shaped(hstat[:, 56:64], (TT, 4)), shaped(hstat[:, 64:72], (TT, 4)), hstat[:, 72:76]
        lrT = area(2336, T)
        zTb, yB = area(2592, 6, T + 3), area(4146, 6, T)
        xl, ropes = rows_flat(xn, 0, TT, 392), rows_flat(xn, 1024, 4, 256)
        trig, ll = area(6912, 4, TT, 32), area(8704, TT, 392)
        qgT = area(5632, 5, T)
        pT7, fades = area(6912, 2, 7, P), area(8704, 8, P)
        qX, kX, ktT = area(2592, 6, P), area(3360, 6, P), area(4128, P)
        qTA, kTA = area(4256, 2, T), area(4768, 2, T)
        pTA = area(6912, 2, 4, P)
        states, kv_own = area(6912, 3, 768), area(2592, 768)
        cdecay = area(5280, 5, NCH)
        qTB, kTB, kbT, qgB = area(0, 2, T), area(512, 2, T), area(1024, 2, T), area(1536, 2, T)
        kb, kbg, qg, kt = area(2048, TT, 256), area(2560, TT, 256), area(3072, TT, 256), area(3584, TT, 256)
        pB = area(4096, TT, 4, P)
        ratio_s, ratio_i = area(5120, 4, P), area(5632, 4, P)
        nT, nmT = area(6144, 4, P), area(6656, 4, P)
        xB, xBT, yBB = area(7168, 4, P), area(7680, 4, P), area(8192, 4, P)
        uv, wT = area(8704, TT, 256), area(9216, 2, T)
        u_nat, stateB, kuB = area(2048, TT, 256), area(5120, 256), area(5376, 256)
        g_exp = area(5632, TT, 256)
        natB_flat, decB_flat = hstat[:, 32:48], hstat[:, 48:56]
        natB, decB = shaped(natB_flat, (TT, 2, 4)), shaped(decB_flat, (2, NCH))
        squares = area(7168, TT, 512)
        kT_mem, v_mem, qT_x = area(0, KT, T), area(2048, TT, D), area(4096, KT, T)
        tT = area(0, 24, T)
        latT = area(6144, 3, T)
        p_sb, pT = area(6912, 3, 2, T), area(8448, 2, 2, T)
        dsa_mask, score = area(6144, TT, T), (area(6656, T), area(9472, T))
        relus, work = rows_flat(xn, 0, 8, T), rows_flat(xn, 0, T)
        conv_g, conv_v, gated, act32 = area(0, 2, T), area(512, 2, T), area(1024, 2, T), area(1536, 2, T)

        landed = [sem("landed_0"), sem("landed_1")]
        hi_done, lo_done, used = sem("hi_done"), sem("lo_done"), sem("used")
        ld_x, ld_c, ld_mem, ld_lat, ld_fin, stored = (sem(n) for n in ("ld_x", "ld_c", "ld_mem", "ld_lat", "ld_fin", "stored"))
        n_ss, n_ms, n_rs, n_xn = sem("n_ss"), sem("n_ms"), sem("n_rs"), sem("n_xn")
        t_ps, t_32, t_hi, t_lo = sem("t_ps"), sem("t_32"), sem("t_hi"), sem("t_lo")
        z_out, sq_out, res_out = sem("z_out"), sem("sq_out"), sem("res_out")
        ff_up, ff_tap, ff_c1, ff_conv, ff_silu, ff_act, ff_hi, ff_lo = (
            sem(n) for n in ("ff_up", "ff_tap", "ff_c1", "ff_conv", "ff_silu", "ff_act", "ff_hi", "ff_lo"))
        at_s, at_max, at_exp, at_p, at_pt, at_ptc, at_o, at_oh, at_ol = (
            sem(n) for n in ("at_s", "at_max", "at_exp", "at_p", "at_pt", "at_ptc", "at_o", "at_oh", "at_ol"))
        v_step, a_step, g_step = sem("v_step"), sem("a_step"), sem("g_step")
        m = {n: sem("m_" + n) for n in (
            "pe_ztp", "act_zB", "dve_zcd", "dve_conv", "act_conv", "pe_back", "act_back", "pe_gl", "dve_ll",
            "act_ll", "dve_kd", "act_kd", "dve_ang", "act_ang", "pe_kdT", "dve_kdT", "pe_fade", "act_fade", "dve_qk",
            "pe_kt", "act_kt", "pe_sc", "dve_pT", "pe_o", "act_o", "dve_rope", "pe_qkA", "dve_qkA", "dve_ktA",
            "pe_scA", "dve_pA", "pe_kv", "dve_state", "pe_inter", "dve_inter",
            "dve_b", "act_sqB", "pool_rsB", "dve_natB", "pe_gB", "act_gB", "pe_tB", "dve_tB", "pe_rB", "act_rB", "pe_kkB", "dve_pB",
            "pe_xB", "dve_xB", "act_yB", "pe_uvB", "act_uvB", "pe_wB", "dve_uB", "pe_oB", "act_oB", "pe_sB", "dve_sB",
            "dve_onorm", "dve_out", "act_osq", "pool_ors", "dve_gate", "act_gate", "pool_init", "dve_on")}
        l_ = {n: sem("l_" + n) for n in (
            "act_ss", "dve_ms", "pool_rs", "dve_n", "pe_lat", "dve_lat", "pe_up", "act_up", "dve_rope", "pe_tT", "act_tT",
            "dve_tT", "pe_dots", "act_relu", "dve_sum")}

        class Steps:

            def __init__(self, eng, step):
                self.eng, self.step, self.n, self.last = eng, step, {}, None

            def __call__(self, ins, signal=None):
                s = self.step if signal is None else signal
                ins.then_inc(s, 1)
                self.n[id(s)] = self.n.get(id(s), 0) + 1
                self.last = (s, self.n[id(s)])

            def fence(self):
                self.eng.wait_ge(*self.last)

        def bc(ap, *shape):
            return ap.broadcast_to([P, *shape])

        def pairs(eng, first, end, body):
            n = (end - first) // 2
            if n == 1:
                body(first)
                body(first + 1)
            elif n > 1:
                with eng.Fori(0, n) as j:
                    for s in range(2):
                        body(2 * j + (first + s), (first + s) % 2)

        block = ctx.enter_context(nc.Block())

        @block.sync
        def _(sp):
            sp.dma_start(res[:], x_d).then_inc(ld_x, 16)
            sp.dma_start(consts[:], consts_d).then_inc(ld_c, 16)
            sp.dma_start(params[:], params_d).then_inc(ld_c, 16)
            sp.dma_start(rows[:], rows_d.partition_broadcast(P)).then_inc(ld_c, 16)
            sp.dma_start(gkup[:], gkup_d).then_inc(ld_c, 16)
            sp.dma_start(pos_i[:], pos_d).then_inc(ld_c, 16)

            def stream(c0, n, size, src, at=0):
                def one(c, slot, i):
                    if not isinstance(c, int) or c >= 2:
                        sp.wait_ge(lo_done, 2 * (c - 1))
                    sp.dma_start(raw[:, slot, 0:size], src[i]).then_inc(landed[slot], 16)

                head = 2 if c0 == 0 else 0
                for i in range(head):
                    one(c0 + i, (c0 + i) % 2, at + i)
                loops = (n - head) // 2
                if loops > 1:
                    with sp.Fori(0, loops) as j:
                        for s in range(2):
                            one(2 * j + (c0 + head + s), (c0 + s) % 2, 2 * j + (at + head + s))
                    head += 2 * loops
                for i in range(head, n):
                    one(c0 + i, (c0 + i) % 2, at + i)

            stream(C_IN, IN_CHUNKS, 8 * IN_COLS, win_d)
            stream(C_K, 4, 2048, wk_d)
            stream(C_V, 4, 2048, wv_d)
            stream(C_OUT, 4, 2048, wout_d)
            stream(C_Q, 4, 2048, wq_d)
            stream(C_O, 4, 2048, wo_d)

            def ffn(c0, n):
                stream(c0, 1, 2048, ffn_a_d, n)
                stream(c0 + 1, NFT - 1, 3072, ffn_b_d, n * (NFT - 1))
                stream(c0 + NFT, 2, 512, ffn_c_d, 2 * n)

            ffn(C_FFN, 0)
            for l in range(LAYERS):
                b = C_LAYER + l * LAYER_CHUNKS
                stream(b, IN2_CHUNKS, 8 * IN2_COLS, win2_d, l * IN2_CHUNKS)
                stream(b + IN2_CHUNKS, 4, 2048, wo2_d, 4 * l)
                ffn(b + IN2_CHUNKS + 4, l + 1)

        SS, MS, RS = 0, 20, 40

        def sources(k):
            return v_mem if k == 1 else res[:]

        def residual_ready(eng, k):
            if k == 0:
                eng.wait_ge(ld_x, 16)
            elif k == 1:
                eng.wait_ge(ld_mem, 16)
            else:
                eng.wait_ge(res_out, 4 * (k - 1))

        TSPLIT = {0: 0, 1: 1, 2: 3, 3: 4, 5: 5, 6: 6, 7: 7, 8: 8}
        t32 = rows_flat(z, 0, 2, 4, P)

        def pairs_of(kind):
            def unit(h, t):
                tok = slice(t * P, t * P + P)
                if kind == "cross":
                    return dict(
                        q=[qT_x[:, 2 * h + d, tok] for d in range(2)], k=[kT_mem[:, 2 * h + d] for d in range(2)],
                        v=[[v_mem[:, b, (2 * h + d) * P:(2 * h + d + 1) * P] for b in range(2)] for d in range(2)],
                        o=[ps[:, h, d * T + t * P:d * T + t * P + P] for d in range(2)],
                        mask=K["none"], scale=-(256 ** -0.5))
                if h < 4:
                    qt, kt_, dim, row, mask, scale = h, 4 + h, 96, 0, K["causal"], -(96 ** -0.5)
                    v0 = 128 + 64 * h
                elif h < 12:
                    g = h - 4
                    qt, kt_, dim, row, mask, scale = 8 + g // 2, 12 + g // 2, 64, 64 * (g % 2), K["dilated"], -0.125
                    v0 = YDV + 64 * g
                else:
                    g = h - 12
                    qt, kt_, dim, row, mask, scale = 16 + g // 2, 18 + g // 2, 64, 64 * (g % 2), dsa_mask, -0.125
                    v0 = YSV + 64 * g
                n = P * (t + 1)
                c = (h // 2) % 2 * T + t * P
                return dict(
                    q=[tT[row:row + dim, qt, tok]], k=[tT[row:row + dim, kt_, 0:n]],
                    v=[[z[:, b, v0:v0 + 64] for b in range(t + 1)]],
                    o=[ps[64 * (h % 2):64 * (h % 2) + 64, h // 4, c:c + P]],
                    mask=mask[:, t, 0:n], scale=scale)

            if kind == "cross":
                heads_of = [(h, h + 1) for h in range(0, 4, 2)]
            else:
                heads_of = [(h + i, h + i + 2) for h in range(0, 16, 4) for i in range(2)]
            return [dict(heads=[unit(h, t) for h in hs], blocks=2 if kind == "cross" else t + 1)
                    for hs in heads_of for t in range(TT)]

        CROSS = pairs_of("cross")
        LAYER = pairs_of("layer")

        def first_pair(l):
            return len(CROSS) + l * len(LAYER)

        def pair_scores(j):
            return ps[:, 4 + j % 2, :].rearrange("p (u n) -> p u n", n=T), ps[:, 6 + j % 2, :].rearrange("p (u n) -> p u n", n=T)

        @block.tensor
        def _(pe):
            ident = K["ident"]

            def mm3(out, a_hi_, a_lo_, b_hi, b_lo, start, stop):
                pe.matmul(out, a_hi_, b_hi, start=start, stop=False)
                pe.matmul(out, a_hi_, b_lo, start=False, stop=False)
                return pe.matmul(out, a_lo_, b_hi, start=False, stop=stop)

            def chunk(c, part):
                pe.wait_ge(lo_done, c * 2 + (part + 1))

            def w(slot, n, cols):
                return (w_hi[:, slot, 0:n].rearrange("p (k c) -> p k c", c=cols),
                        w_lo[:, slot, 0:n].rearrange("p (k c) -> p k c", c=cols))

            def tsplit(k, src, ready, free=None):
                for t in range(TT):
                    ready(t)
                    for half in range(2):
                        q = 2 * t + half
                        if q == 0 and free:
                            free()
                        for j in range(4):
                            ins = pe.transpose(ps[:, 4 + q, j * P:(j + 1) * P],
                                               src[:, t, (4 * half + j) * P:(4 * half + j + 1) * P], ident)
                        ins.then_inc(t_ps, 1)

            def norm(k, free=None):
                tsplit(TSPLIT[k], v_mem if k == 1 else xn[:], lambda t: pe.wait_ge(n_xn, 2 * (k if k < 4 else k - 1) + t + 1), free)

            def columns(c0, n, cols, before):
                def one(i, slot=None):
                    slot = i % 2 if slot is None else slot
                    chunk(i + c0, 0)
                    if not isinstance(i, int) or i >= 2:
                        pe.wait_ge(z_out, i + (before - 1))
                    hi, lo = w(slot, 8 * cols, cols)
                    for t in range(TT):
                        for k in range(KT):
                            if t == 0 and k == KT // 2:
                                chunk(i + c0, 1)
                            ins = mm3(ps[:, 2 * slot + t, 0:cols], hT_hi[:, k, t * P:(t + 1) * P],
                                      hT_lo[:, k, t * P:(t + 1) * P], hi[:, k], lo[:, k], k == 0, k == KT - 1)
                            if t == TT - 1 and k in (KT // 2 - 1, KT - 1):
                                ins.then_inc(used, 1)
                one(0)
                one(1)
                pairs(pe, 2, n, one)

            def square_rows(c0):
                for i in range(4):
                    hi, lo = w(i % 2, 2048, D)
                    for kk in range(2):
                        chunk(c0 + i, kk)
                        k = 2 * i + kk
                        for t in range(TT):
                            for half in range(2):
                                ins = mm3(ps[:, 2 * t + half, :], hT_hi[:, k, t * P:(t + 1) * P],
                                          hT_lo[:, k, t * P:(t + 1) * P], hi[:, kk, half * 512:half * 512 + 512],
                                          lo[:, kk, half * 512:half * 512 + 512], k == 0, k == KT - 1)
                        ins.then_inc(used, 1)

            def square_columns(c0):
                for i in range(4):
                    chunk(c0 + i, 0)
                    hi, lo = w(i % 2, 2048, 256)
                    for j in range(2):
                        for k in range(KT):
                            if j == 0 and k == KT // 2:
                                chunk(c0 + i, 1)
                            a, b = hi[:, k, j * P:(j + 1) * P], lo[:, k, j * P:(j + 1) * P]
                            ins = mm3(ps[:, i, j * T:(j + 1) * T], a, b, hT_hi[:, k], hT_lo[:, k], k == 0, k == KT - 1)
                            if j == 1 and k in (KT // 2 - 1, KT - 1):
                                ins.then_inc(used, 1)

            def ffn(c0, n):
                base = n * NFT

                def up(i, slot):
                    hi, lo = w(slot, 2048, 256)
                    if not isinstance(i, int) or i >= 2:
                        pe.wait_ge(ff_conv, i + (base - 1))
                    for j in range(2):
                        for k in range(KT):
                            a, b = hi[:, k, j * P:(j + 1) * P], lo[:, k, j * P:(j + 1) * P]
                            ins = mm3(ps[:, 4 + slot, j * T:(j + 1) * T], a, b, hT_hi[:, k], hT_lo[:, k],
                                      k == 0, k == KT - 1)
                    ins.then_inc(ff_up, 1)

                def down(i, slot, off, halves, start, stop):
                    pe.wait_ge(ff_lo, i + (base + 1))
                    a = 1 - slot if off else 1
                    for t in range(TT):
                        for half in halves:
                            o = off + (half * 512 if len(halves) == 2 else 0)
                            ins = mm3(ps[:, 2 * t + half, :], a_hi[:, a, t * P:(t + 1) * P],
                                      a_lo[:, a, t * P:(t + 1) * P], w_hi[:, slot, o:o + 512],
                                      w_lo[:, slot, o:o + 512], start, stop)
                    return ins

                chunk(c0, 1)
                up(0, 0)
                chunk(c0 + 1, 0)
                up(1, 1)
                chunk(c0 + 1, 1)
                down(0, 1, 2048, (0, 1), True, False).then_inc(used, 4)

                def one(i, slot=None):
                    slot = i % 2 if slot is None else slot
                    chunk(i + c0, 0)
                    up(i, slot)
                    chunk(i + c0, 1)
                    down(i - 1, slot, 2048, (0, 1), False, False).then_inc(used, 2)
                pairs(pe, 2, NFT, one)
                for half in range(2):
                    chunk(c0 + NFT + half, 1)
                    down(NFT - 1, half, 0, (half,), False, True).then_inc(used, 2)

            def attention(j0, us):
                def scores(j, u):
                    if j >= 2:
                        pe.wait_ge(at_max, j - 1)
                    for i, head in enumerate(u["heads"]):
                        for d, (q, k) in enumerate(zip(head["q"], head["k"])):
                            ins = pe.matmul(pair_scores(j)[0][:, i, 0:P * u["blocks"]], q, k, start=d == 0,
                                            stop=d == len(head["q"]) - 1)
                    ins.then_inc(at_s, 1)

                def turn(j, u):
                    pe.wait_ge(at_p, j + 1)
                    if j >= 2:
                        pe.wait_ge(at_ptc, j - 1)
                    for i in range(2):
                        for b in range(u["blocks"]):
                            ins = pe.transpose(pair_scores(j)[1][:, i, b * P:(b + 1) * P],
                                               p_sb[:, j % 3, i, b * P:(b + 1) * P], ident)
                    ins.then_inc(at_pt, 1)

                def values(j, u):
                    pe.wait_ge(at_ptc, j + 1)
                    for i, head in enumerate(u["heads"]):
                        for v, o in zip(head["v"], head["o"]):
                            for b in range(u["blocks"]):
                                ins = pe.matmul(o, v[b], pT[:, j % 2, i, b * P:(b + 1) * P], start=b == 0,
                                                stop=b == u["blocks"] - 1)
                    ins.then_inc(at_o, 1)

                for i in range(len(us) + 3):
                    if i < len(us):
                        scores(j0 + i, us[i])
                    if 2 <= i <= len(us) + 1:
                        turn(j0 + i - 2, us[i - 2])
                    if i >= 3:
                        values(j0 + i - 3, us[i - 3])

            def values_cd(hn):
                t, q = hn // 8, hn % 8
                v = ZV + 256 + q * 64
                if q == 0:
                    pe.wait_ge(m["act_o"], t + 1)
                pe.wait_ge(m["dve_pT"], hn + 1)
                for lev in range(7):
                    ins = pe.matmul(ps[:, 7, q * 64:q * 64 + 64], pT7[:, hn % 2, lev], z[:, t, v:v + 64],
                                    start=lev == 0, stop=lev == 6)
                ins.then_inc(m["pe_o"], 1)

            pe.wait_ge(ld_c, 80)
            norm(0)
            pe.wait_ge(t_lo, 4)
            columns(C_IN, IN_CHUNKS, IN_COLS, 0)
            pe.wait_ge(z_out, IN_CHUNKS)

            for t in range(TT):
                for b, tiles in enumerate((range(0, 4), range(4, 8), range(8, 10))):
                    for j, c in enumerate(tiles):
                        ins = pe.transpose(ps[:, 3 * t + b, j * P:(j + 1) * P], z[:, t, c * P:(c + 1) * P], ident)
                    ins.then_inc(m["pe_ztp"], 1)
            for t in range(TT):
                ins = pe.transpose(ps[0:16, 6, t * P:(t + 1) * P], z[:, t, ZLR:ZLR + 16], ident)
            ins.then_inc(m["pe_ztp"], 1)
            pe.wait_ge(m["dve_zcd"], 1)
            for t in range(TT):
                ins = pe.matmul(ps[:, 7, t * P:(t + 1) * P], lrT[0:16, t * P:(t + 1) * P], gkup[:, :], start=True, stop=True)
            ins.then_inc(m["pe_gl"], 1)
            pe.wait_ge(m["act_conv"], 1)
            pe.wait_ge(m["dve_zcd"], 3)
            for t in range(TT):
                for b, tiles in enumerate((range(0, 4), range(4, 6))):
                    for j, c in enumerate(tiles):
                        ins = pe.transpose(ps[:, 2 * t + b, j * P:(j + 1) * P], yB[:, c, t * P:(t + 1) * P], ident)
                    ins.then_inc(m["pe_back"], 1)
            pe.wait_ge(m["act_kd"], 1)
            for t in range(TT):
                for j in range(2):
                    ins = pe.transpose(ps[:, 4, (2 * j + t) * P:(2 * j + t + 1) * P],
                                       z[:, t, ZDF + j * P:ZDF + (j + 1) * P], ident)
            ins.then_inc(m["pe_kdT"], 1)
            pe.wait_ge(m["dve_rope"], 1)
            for side in range(2):
                for j in range(2):
                    for t in range(TT):
                        c = ZRQ + side * 256 + j * P
                        ins = pe.transpose(ps[:, 5 + side, (2 * j + t) * P:(2 * j + t + 1) * P], z[:, t, c:c + P], ident)
                ins.then_inc(m["pe_qkA"], 1)
            pe.wait_ge(m["act_back"], 4)
            pe.wait_ge(m["dve_qkA"], 2)
            for t in range(TT):
                tok = slice(t * P, t * P + P)
                for h in range(4):
                    r = slice(64 * (h % 2), 64 * (h % 2) + 64)
                    c = (2 * t + h // 2) * P
                    ins = pe.matmul(ps[:, h % 2, c:c + P], kTA[r, h // 2, tok], qTA[r, h // 2, tok], start=True, stop=True)
            ins.then_inc(m["pe_scA"], 1)
            for t in range(TT):
                pe.wait_ge(m["dve_pA"], t + 1)
                for h in range(4):
                    ins = pe.matmul(ps[:, 7, t * 256 + h * 64:t * 256 + h * 64 + 64], pTA[:, t, place(h)],
                                    z[:, t, ZV + h * 64:ZV + h * 64 + 64], start=True, stop=True)
                ins.then_inc(m["pe_o"], 1)
            unit, hn = 0, 0
            for t in range(TT):
                tok = slice(t * P, t * P + P)
                for g in range(3):
                    pe.wait_ge(m["dve_pA"], 2)
                    if unit >= 1:
                        pe.wait_ge(m["act_fade"], unit)
                    for j in range(2):
                        ins = pe.matmul(ps[:, j, :], lf[:, t, g * P:(g + 1) * P],
                                        K["sums"][:, 4 * j:4 * j + 4].rearrange("p a b -> p (a b)"), start=True, stop=True)
                    ins.then_inc(m["pe_fade"], 1)
                    pe.wait_ge(m["dve_qk"], unit + 1)
                    if unit >= 1:
                        pe.wait_ge(m["act_kt"], unit)
                    pe.transpose(ps[:, 6, 0:P], ktT, ident).then_inc(m["pe_kt"], 1)
                    heads, dim = (4, 32) if g == 0 else (2, 64)
                    for h in range(heads):
                        r = slice(dim * h, dim * h + dim)
                        b = 2 + 2 * (hn % 2)
                        if hn >= 2:
                            pe.wait_ge(m["dve_pT"], hn - 1)
                        qd_, kd_ = (cqkT[:, 0], cqkT[:, 1]) if g == 0 else (dqT[:, g - 1], kdT[:, g - 1])
                        for lev in range(7):
                            lhs = kX[r, lev] if lev < 6 else kd_[r, tok]
                            rhs = qX[r, lev] if lev < 6 else qd_[r, tok]
                            ins = pe.matmul(ps[:, b + lev // 4, (lev % 4) * P:(lev % 4 + 1) * P], lhs, rhs,
                                            start=True, stop=True)
                        ins.then_inc(m["pe_sc"], 1)
                        if hn % 8:
                            values_cd(hn - 1)
                        hn += 1
                    unit += 1
                values_cd(hn - 1)
            for n in range(NCH - 1):
                t, r = n // 2, slice(64 * (n % 2), 64 * (n % 2) + 64)
                pe.wait_ge(m["act_kt"], 6)
                pe.wait_ge(m["dve_ktA"], 1)
                if n >= 1:
                    pe.wait_ge(m["dve_state"], n)
                for k0, a, wd in ((ZRK, 0, 128), (ZRK + 128, 128, 128), (ZCQ, 256, 256), (ZDF, 512, 128), (ZDF + 128, 640, 128)):
                    ins = pe.matmul(ps[:, a // 512, a % 512:a % 512 + wd], z[r, t, k0:k0 + P],
                                    z[r, t, ZV + a:ZV + a + wd], start=True, stop=True)
                ins.then_inc(m["pe_kv"], 1)
            for n in range(1, NCH):
                t, r = n // 2, slice(64 * (n % 2), 64 * (n % 2) + 64)
                pe.wait_ge(m["dve_state"], n)
                b = 2 if t == 0 else 4
                for g, (a, wd) in enumerate(((0, 128), (128, 128), (256, 256), (512, 128), (640, 128))):
                    ins = pe.matmul(ps[r, b + a // 512, a % 512:a % 512 + wd], qgT[:, g, n * CH:(n + 1) * CH],
                                    states[:, n - 1, a:a + wd], start=True, stop=True)
                ins.then_inc(m["pe_inter"], 1)

            pe.wait_ge(m["dve_inter"], 2)
            pe.wait_ge(m["dve_b"], 1)
            for t in range(TT):
                pe.matmul(ps[:, 6, t * 8:t * 8 + 4], K["sums"][:, 6], g_b[:, t], start=True, stop=True)
                pe.matmul(ps[:, 6, t * 8 + 4:t * 8 + 8], K["sums"][:, 7], g_b[:, t], start=True, stop=True)
                for p in range(2):
                    ins = pe.matmul(ps[:, 6, 16 + p * 4 + t * 2:16 + p * 4 + t * 2 + 2], g_exp[:, t, p * P:(p + 1) * P],
                                    K["chunk_of"], start=True, stop=True)
            ins.then_inc(m["pe_gB"], 1)
            pe.wait_ge(m["dve_natB"], 1)
            for side, src in enumerate((z[:, :, 0:256], z[:, :, 256:512], kb, qg)):
                for p in range(2):
                    for t in range(TT):
                        ins = pe.transpose(ps[:, side, (2 * p + t) * P:(2 * p + t + 1) * P], src[:, t, p * P:(p + 1) * P], ident)
                ins.then_inc(m["pe_tB"], 1)
            pe.wait_ge(m["dve_tB"], 4)
            for t in range(TT):
                tok = slice(t * P, t * P + P)
                pe.wait_ge(m["dve_xB"], t * 8 + 1)
                for h in range(4):
                    ins = pe.matmul(ps[:, 4, h * P:(h + 1) * P], xB[:, h], K["incl"], start=True, stop=True)
                ins.then_inc(m["pe_rB"], 1)
                for i, side in enumerate((kbT, qTB)):
                    for h in range(4):
                        r = slice(64 * (h % 2), 64 * (h % 2) + 64)
                        c = (2 * i + h // 2) * P
                        ins = pe.matmul(ps[:, h % 2, c:c + P], kTB[r, h // 2, tok], side[r, h // 2, tok], start=True, stop=True)
                ins.then_inc(m["pe_kkB"], 1)
                pe.wait_ge(m["dve_xB"], t * 8 + 2)
                for h in range(4):
                    ins = pe.transpose(ps[:, 2, h * P:(h + 1) * P], xBT[:, h], ident)
                ins.then_inc(m["pe_xB"], 1)
                for lev in range(5):
                    pe.wait_ge(m["dve_xB"], t * 8 + 3 + lev)
                    for h in range(4):
                        ins = pe.matmul(ps[:, 3, h * P:(h + 1) * P], nmT[:, h], xB[:, h], start=True, stop=True)
                    ins.then_inc(m["pe_xB"], 1)
                    pe.wait_ge(m["act_yB"], t * 5 + lev + 1)
                    if lev < 4:
                        for h in range(4):
                            pe.matmul(ps[:, 0, h * P:(h + 1) * P], xBT[:, h], yBB[:, h], start=True, stop=True)
                    for h in range(4):
                        ins = pe.matmul(ps[:, 1, h * P:(h + 1) * P], yBB[:, h], xBT[:, h], start=True, stop=True)
                    ins.then_inc(m["pe_xB"], 1)
                pe.wait_ge(m["dve_xB"], t * 8 + 8)
                if t == 1:
                    pe.wait_ge(m["act_uvB"], 1)
                for h in range(4):
                    r = slice(64 * (h % 2), 64 * (h % 2) + 64)
                    pe.matmul(ps[:, 5, h * 64:h * 64 + 64], xBT[:, place(h)], z[:, t, 512 + h * 64:512 + h * 64 + 64], start=True, stop=True)
                    ins = pe.matmul(ps[r, 6, (h // 2) * P:(h // 2) * P + P], kbg[:, t, h * 64:h * 64 + 64], xBT[:, place(h)],
                                    start=True, stop=True)
                ins.then_inc(m["pe_uvB"], 1)
            pe.wait_ge(m["act_uvB"], 2)
            for n in range(NCH):
                t, r = n // 2, slice(64 * (n % 2), 64 * (n % 2) + 64)
                tk = slice(n * CH, (n + 1) * CH)
                pe.wait_ge(m["dve_sB"], n + 1)
                for p in range(2):
                    ins = pe.matmul(ps[r, 0, p * P:(p + 1) * P], wT[:, p, tk], stateB[:, p * P:(p + 1) * P], start=True, stop=True)
                ins.then_inc(m["pe_wB"], 1)
                pe.wait_ge(m["dve_uB"], n + 1)
                for h in range(4):
                    v = slice(h * 64, h * 64 + 64)
                    pe.matmul(ps[r, 2 + t, v], qgB[:, h // 2, tk], stateB[:, v], start=True, stop=False)
                    ins = pe.matmul(ps[r, 2 + t, v], pB[r, t, place(h), r], u_nat[r, t, v], start=False, stop=True)
                ins.then_inc(m["pe_oB"], 1)
                if n < NCH - 1:
                    for p in range(2):
                        ins = pe.matmul(ps[:, 1, p * P:(p + 1) * P], kt[r, t, p * P:(p + 1) * P], u_nat[r, t, p * P:(p + 1) * P],
                                        start=True, stop=True)
                    ins.then_inc(m["pe_sB"], 1)

            norm(1)
            pe.wait_ge(t_lo, 8)
            pe.wait_ge(m["act_oB"], 2)
            square_columns(C_K)
            pe.wait_ge(sq_out, 4)
            square_rows(C_V)
            tsplit(2, xn[:], lambda t: pe.wait_ge(m["dve_on"], t + 1))
            pe.wait_ge(t_lo, 12)
            pe.wait_ge(sq_out, 8)
            square_rows(C_OUT)
            norm(2)
            pe.wait_ge(t_lo, 16)
            pe.wait_ge(res_out, 4)
            square_columns(C_Q)
            pe.wait_ge(sq_out, 12)
            attention(0, CROSS)
            pe.wait_ge(at_ol, 4)
            square_rows(C_O)
            norm(3)
            pe.wait_ge(t_lo, 20)
            pe.wait_ge(res_out, 8)
            ffn(C_FFN, 0)
            for l in range(LAYERS):
                b = C_LAYER + l * LAYER_CHUNKS
                norm(5 + 2 * l)
                pe.wait_ge(t_lo, 4 * (6 + 2 * l))
                pe.wait_ge(res_out, 4 * (4 + 2 * l))
                columns(b, IN2_CHUNKS, IN2_COLS, IN_CHUNKS + l * IN2_CHUNKS)
                pe.wait_ge(l_["dve_n"], l + 1)
                for t in range(TT):
                    for j in range(3):
                        ins = pe.transpose(ps[:, 4 + t, j * P:(j + 1) * P], z[:, t, j * P:(j + 1) * P], ident)
                    ins.then_inc(l_["pe_lat"], 1)
                pe.wait_ge(ld_lat, 16 * (l + 1))
                for t in range(TT):
                    tok = slice(t * P, t * P + P)
                    pe.wait_ge(l_["dve_lat"], 2 * (l + 1))
                    for j in range(2):
                        ins = pe.matmul(ps[:, 4 + t, 0:384], latT[:, j, tok], lat_w[:, j * 384:(j + 1) * 384],
                                        start=j == 0, stop=j == 1)
                    ins.then_inc(l_["pe_up"], 1)
                    pe.matmul(ps[:, 6 + t, :], latT[:, 2, tok], lat_w[:, 768:1280], start=True, stop=True).then_inc(l_["pe_up"], 1)
                pe.wait_ge(l_["dve_rope"], l + 1)
                pe.wait_ge(z_out, IN_CHUNKS + (l + 1) * IN2_CHUNKS)
                for n in range(12):
                    t, g = n // 6, n % 6
                    if n >= 8:
                        q = n - 8
                        pe.wait_ge(l_["act_tT"] if q % 2 == 0 else l_["dve_tT"], 6 * l + q // 2 + 1)
                    for j in range(4):
                        tile = 4 * g + j
                        if tile < 8:
                            src = z[:, t, 3024 + tile * 96:3024 + (tile + 1) * 96]
                        elif tile < 20:
                            src = z[:, t, YDQ + (tile - 8) * P:YDQ + (tile - 7) * P]
                        elif tile < 22:
                            src = z[:, t, YQI + (tile - 20) * P:YQI + (tile - 19) * P]
                        elif tile == 22:
                            src = z[:, t, 0:P]
                        else:
                            continue
                        ins = pe.transpose(ps[0:src.shape[-1], n % 8, j * P:(j + 1) * P], src, ident)
                    ins.then_inc(l_["pe_tT"], 1)
                pe.wait_ge(l_["act_tT"], 6 * (l + 1))
                pe.wait_ge(l_["dve_tT"], 6 * (l + 1))
                for t in range(TT):
                    if t == 1:
                        pe.wait_ge(l_["act_relu"], 2 * l + 1)
                    for h in range(8):
                        r = slice(32 * (h % 4), 32 * (h % 4) + 32)
                        ins = pe.matmul(ps[:, h % 4, (h // 4) * T:(h // 4) * T + P * (t + 1)], tT[r, 20 + h // 4, t * P:(t + 1) * P],
                                        tT[r, 22, 0:P * (t + 1)], start=True, stop=True)
                    ins.then_inc(l_["pe_dots"], 1)
                pe.wait_ge(l_["act_relu"], 2 * l + 2)
                attention(first_pair(l), LAYER)
                pe.wait_ge(at_ol, 4 * (l + 2))
                square_rows(b + IN2_CHUNKS)
                norm(6 + 2 * l)
                pe.wait_ge(t_lo, 4 * (7 + 2 * l))
                pe.wait_ge(res_out, 4 * (5 + 2 * l))
                ffn(b + IN2_CHUNKS + 4, l + 1)

        def section(eng, c0, n, first, last, split, epilogue):
            def one(i, slot=None):
                slot = i % 2 if slot is None else slot
                if isinstance(i, int):
                    size = chunk_size(c0 + i + 2)
                    if size:
                        split(c0 + i + 2, slot, size)
                else:
                    split(i + (c0 + 2), slot, chunk_size(c0 + first + 2))
                epilogue(i, slot)
            for i in range(first):
                one(i)
            pairs(eng, first, last, one)
            for i in range(last, n):
                one(i)

        @block.scalar
        def _(act):
            s = Steps(act, a_step)

            def split(c, slot, size):
                for part in range(2):
                    split_part(c, slot, size, part)

            def split_part(c, slot, size, part, up=None):
                if part == 0:
                    act.wait_ge(landed[slot], c * 8 + (16 - 8 * slot))
                if up is not None:
                    act.wait_ge(ff_up, up)
                elif not isinstance(c, int):
                    act.wait_ge(used, c * 2 - (3 - part))
                elif c >= 2:
                    fits = part == 0 and cut(size) <= cut(chunk_size(c - 2))
                    act.wait_ge(used, c * 2 - (3 if fits else 2))
                a, b = (0, cut(size)) if part == 0 else (cut(size), size)
                act.activation(w_hi[:, slot, a:b], raw[:, slot, a:b], ACT.Copy).then_inc(hi_done, 1)

            def norm(k):
                residual_ready(act, k)
                for t in range(TT):
                    s(act.activation(rows_flat(z, 1024, D), sources(k)[:, t], ACT.Square,
                                     accum_out=stat[:, SS + 2 * k + t:SS + 2 * k + t + 1]), n_ss)
                    if t == 0:
                        s.fence()

            def tsplit(k):
                for q in range(4):
                    t, half = q // 2, q % 2
                    act.wait_ge(t_32, 4 * k + q + 1)
                    s(act.activation(hT_hi[:, 4 * half:4 * half + 4, t * P:(t + 1) * P], t32[:, q % 2], ACT.Copy), t_hi)

            def columns(c0, n, cols):
                def out(i, slot):
                    act.wait_ge(used, i * 2 + 2 * (c0 + 1))
                    for t in range(TT):
                        ins = act.activation(z[:, t, bass.ds(i * cols, cols)], ps[:, 2 * slot + t, 0:cols], ACT.Copy)
                    ins.then_inc(z_out, 1)
                section(act, c0, n, 0, n - 2, split, out)

            def residual(c0):
                section(act, c0, 4, 0, 0, split, lambda i, slot: None)

            def square_columns(c0, dst):
                def out(i, slot):
                    act.wait_ge(used, 2 * (c0 + i + 1))
                    s(act.activation(dst[:, 2 * i:2 * i + 2], ps[:, i].rearrange("p (a b) -> p a b", b=T), ACT.Copy), sq_out)
                section(act, c0, 4, 0, 0, split, out)

            def square_rows(c0, dst):
                residual(c0)
                act.wait_ge(used, 2 * (c0 + 4))
                for q in range(4):
                    s(act.activation(dst[:, q // 2, q % 2 * 512:q % 2 * 512 + 512], ps[:, q], ACT.Copy), sq_out)

            def ffn(c0, n):
                base = n * NFT

                def one(i, slot=None):
                    slot = i % 2 if slot is None else slot
                    tile = not isinstance(i, int) or i < NFT
                    size = chunk_size(c0 + i + 2) if isinstance(i, int) else 3072
                    if tile:
                        act.wait_ge(ff_up, i + (base + 1))
                        if not isinstance(i, int) or i >= 2:
                            act.wait_ge(ff_act, i + (base - 1))
                        for g, dst in enumerate((conv_g, conv_v)):
                            wc = ptab["ffn_conv"][0] + n * NFT * 6 + 3 * g + 2
                            bc_ = ptab["ffn_bias"][0] + n * NFT * 2 + g
                            ins = act.activation(dst[:, slot], ps[:, 4 + slot, g * T:(g + 1) * T], ACT.Identity,
                                                 bias=params[:, bass.ds(i * 2 + bc_, 1)], scale=params[:, bass.ds(i * 6 + wc, 1)])
                        ins.then_inc(ff_tap, 1)
                    if size:
                        split_part(c0 + i + 2 if isinstance(i, int) else i + (c0 + 2), slot, size, 0,
                                   i + (base + 1) if size == 3072 and tile else None)
                    if tile:
                        act.wait_ge(ff_conv, i + (base + 1))
                        act.activation(gated[:, slot], conv_g[:, slot], ACT.Silu).then_inc(ff_silu, 1)
                    if size:
                        split_part(c0 + i + 2 if isinstance(i, int) else i + (c0 + 2), slot, size, 1,
                                   base + 1 if isinstance(i, int) and i == 0 else None)
                    if tile:
                        act.wait_ge(ff_act, i + (base + 1))
                        if not isinstance(i, int) or i >= 1:
                            act.wait_ge(used, i * 2 + 2 * c0)
                        act.activation(a_hi[:, slot], act32[:, slot], ACT.Copy).then_inc(ff_hi, 1)
                one(0)
                one(1)
                pairs(act, 2, 20, one)
                for i in range(20, NFC):
                    one(i)

            def attention(j0, us):
                for i in range(len(us) + 2):
                    if i < len(us):
                        j, n = j0 + i, P * us[i]["blocks"]
                        act.wait_ge(at_max, j + 1)
                        for h in range(2):
                            ins = act.activation(p_sb[:, j % 3, h, 0:n], p_sb[:, j % 3, h, 0:n], ACT.Exp, scale=-1.0,
                                                 bias=ast[:, j % 3, 0, h:h + 1], accum_out=ast[:, j % 3, 1, h:h + 1])
                        s(ins, at_exp)
                    if i >= 2:
                        j, n = j0 + i - 2, P * us[i - 2]["blocks"]
                        act.wait_ge(at_pt, j + 1)
                        if j >= 2:
                            act.wait_ge(at_o, j - 1)
                        s(act.activation(pT[:, j % 2, :, 0:n], pair_scores(j)[1][:, :, 0:n], ACT.Copy), at_ptc)
                act.wait_ge(at_o, j0 + len(us))
                for q in range(4):
                    s(act.activation(hT_hi[:, 2 * q:2 * q + 2], ps[:, q].rearrange("p (a b) -> p a b", b=T), ACT.Copy), at_oh)

            split(0, 0, chunk_size(0))
            split(1, 1, chunk_size(1))
            norm(0)
            tsplit(0)
            columns(C_IN, IN_CHUNKS, IN_COLS)

            act.wait_ge(m["pool_init"], 1)
            for t in range(TT):
                for b, (lo, hi) in enumerate(((0, 4), (4, 6))):
                    act.wait_ge(m["pe_ztp"], 3 * t + b + 1)
                    s(act.activation(zTb[:, lo:hi, 3 + t * P:3 + (t + 1) * P],
                                     ps[:, 3 * t + b, 0:(hi - lo) * P].rearrange("p (a b) -> p a b", b=P), ACT.Copy), m["act_zB"])
            for t in range(TT):
                s(act.activation(z[:, t, ZG:ZG + D], z[:, t, ZG:ZG + D], ACT.Silu), m["act_gate"])
            act.wait_ge(m["dve_ang"], 1)
            for i in range(2):
                ins = act.activation(trig[:, 1 + i], trig[:, 1 + i], ACT.Sin)
            s(ins, m["act_ang"])
            act.wait_ge(m["dve_conv"], 1)
            s(act.activation(yB[:, :, :], yB[:, :, :], ACT.Silu), m["act_conv"])
            for t in range(TT):
                for b, (lo, hi) in enumerate(((0, 4), (4, 6))):
                    act.wait_ge(m["pe_back"], 2 * t + b + 1)
                    s(act.activation(z[:, t, lo * P:hi * P], ps[:, 2 * t + b, 0:(hi - lo) * P], ACT.Copy), m["act_back"])
            act.wait_ge(m["dve_ll"], 1)
            s(act.activation(ll, ll, ACT.Exp, scale=-1.0))
            s.fence()
            s(act.activation(ll, ll, ACT.Ln, bias=1.0))
            s(act.activation(ea, R["a_log"], ACT.Exp), m["act_ll"])
            act.wait_ge(m["dve_kd"], 1)
            s(act.activation(beta, beta, ACT.Exp))
            s(act.activation(z[:, :, ZDF:ZDF + 256], z[:, :, ZDF:ZDF + 256], ACT.Exp, scale=-1.0), m["act_kd"])
            act.wait_ge(m["pe_o"], 2)
            act.wait_ge(m["dve_rope"], 1)
            s(act.activation(xn[:, :, 0:256], ps[:, 7, :].rearrange("p (a b) -> p a b", b=256), ACT.Copy), m["act_o"])
            unit, hn = 0, 0
            for t in range(TT):
                for g in range(3):
                    act.wait_ge(m["pe_fade"], unit + 1)
                    if unit >= 1:
                        act.wait_ge(m["dve_qk"], unit)
                    s(act.activation(fades, ps[:, 0:2].rearrange("p a (b c) -> p (a b) c", c=P), ACT.Exp), m["act_fade"])
                    act.wait_ge(m["pe_kt"], unit + 1)
                    c = ZCQ if g == 0 else ZDF + (g - 1) * P
                    s(act.activation(z[:, t, c:c + P], ps[:, 6, 0:P], ACT.Copy), m["act_kt"])
                    unit += 1
                act.wait_ge(m["pe_o"], 2 + 8 * (t + 1))
                s(act.activation(xn[:, t, 512:1024], ps[:, 7, :], ACT.Copy), m["act_o"])
            act.wait_ge(m["dve_inter"], 2)
            s(act.activation(squares, z[:, :, 0:512], ACT.Square), m["act_sqB"])
            act.wait_ge(m["pe_gB"], 1)
            act.activation(natB_flat, ps[:, 6, 0:16], ACT.Exp)
            s(act.activation(decB_flat, ps[:, 6, 16:24], ACT.Exp), m["act_gB"])
            for t in range(TT):
                act.wait_ge(m["pe_rB"], t + 1)
                if t == 1:
                    act.wait_ge(m["dve_xB"], 9)
                s(act.activation(ratio_i, ps[:, 4, :].rearrange("p (a b) -> p a b", b=P), ACT.Exp), m["act_rB"])
                for lev in range(5):
                    act.wait_ge(m["pe_xB"], t * 11 + 2 + 2 * lev)
                    s(act.activation(yBB, ps[:, 3, :].rearrange("p (a b) -> p a b", b=P), ACT.Copy), m["act_yB"])
                act.wait_ge(m["pe_uvB"], t + 1)
                act.activation(uv[:, t], ps[:, 5, 0:256], ACT.Copy)
                s(act.activation(wT[:, :, t * P:(t + 1) * P], ps[:, 6, 0:256].rearrange("p (a b) -> p a b", b=P), ACT.Copy), m["act_uvB"])
            for t in range(TT):
                act.wait_ge(m["pe_oB"], 2 * t + 2)
                s(act.activation(xn[:, t, 256:512], ps[:, 2 + t, 0:256], ACT.Copy), m["act_oB"])
            act.wait_ge(m["dve_sB"], NCH + 1)
            s.fence()
            s(act.activation(area(4096, TT, D), xn[:, :, :], ACT.Square), m["act_osq"])

            norm(1)
            tsplit(1)
            square_columns(C_K, kT_mem)
            act.wait_ge(t_lo, 8)
            square_rows(C_V, v_mem)
            tsplit(2)
            residual(C_OUT)
            norm(2)
            tsplit(3)
            square_columns(C_Q, qT_x)
            attention(0, CROSS)
            residual(C_O)
            norm(3)
            tsplit(4)
            ffn(C_FFN, 0)
            norm(4)
            for l in range(LAYERS):
                b = C_LAYER + l * LAYER_CHUNKS
                norm(5 + 2 * l)
                tsplit(5 + 2 * l)
                columns(b, IN2_CHUNKS, IN2_COLS)
                s.last = (z_out, IN_CHUNKS + (l + 1) * IN2_CHUNKS)
                s.fence()
                for t in range(TT):
                    for i, (c, n) in enumerate(((YCQ, 256), (YKV, 128))):
                        s(act.activation(area(0, 8, T)[:, 2 * t + i, 0:n], z[:, t, c:c + n], ACT.Square,
                                         accum_out=lstat[:, 2 * t + i:2 * t + i + 1]), l_["act_ss"])
                for t in range(TT):
                    act.wait_ge(l_["pe_up"], 4 * l + 2 * t + 2)
                    act.activation(z[:, t, 3024:3408], ps[:, 4 + t, 0:384], ACT.Copy)
                    kv = ps[:, 6 + t, :].rearrange("p (h c) -> p h c", c=P)
                    act.activation(z[:, t, 3408:3792].rearrange("p (h c) -> p h c", c=96)[:, :, 0:64], kv[:, :, 0:64], ACT.Copy)
                    s(act.activation(z[:, t, 128:384].rearrange("p (h c) -> p h c", c=64), kv[:, :, 64:128], ACT.Copy), l_["act_up"])
                for n in range(0, 12, 2):
                    t, g = n // 6, n % 6
                    act.wait_ge(l_["pe_tT"], 12 * l + n + 1)
                    r = 96 if g < 2 else P
                    s(act.activation(tT[0:r, 4 * g:4 * g + 4, t * P:(t + 1) * P],
                                     ps[0:r, n % 8, :].rearrange("p (a b) -> p a b", b=P), ACT.Copy), l_["act_tT"])
                for t in range(TT):
                    act.wait_ge(l_["pe_dots"], 2 * l + t + 1)
                    if t == 1:
                        act.wait_ge(l_["dve_sum"], 2 * l + 1)
                    n = P * (t + 1)
                    s(act.activation(relus[:, :, 0:n], ps[:, 0:4].rearrange("p a (b c) -> p (a b) c", c=T)[:, :, 0:n], ACT.Relu), l_["act_relu"])
                attention(first_pair(l), LAYER)
                residual(b + IN2_CHUNKS)
                norm(6 + 2 * l)
                tsplit(6 + 2 * l)
                ffn(b + IN2_CHUNKS + 4, l + 1)
            norm(9)

        @block.gpsimd
        def _(pool):
            s = Steps(pool, g_step)
            ring = zTb[:, :, 0:3]

            def power(out, in_, n, signal):
                s(pool.tensor_tensor(out, in_, K["neg_half"][:, 0:n], ALU.pow), signal)

            def norm(k):
                pool.wait_ge(n_ms, k + 1)
                power(stat[:, RS + 2 * k:RS + 2 * k + 2], stat[:, MS + 2 * k:MS + 2 * k + 2], 2, n_rs)

            s(pool.memset(ring, 0.0), m["pool_init"])
            pool.wait_ge(ld_c, 80)
            norm(0)
            pool.wait_ge(m["dve_b"], 1)
            power(hstat[:, 16:32], hstat[:, 0:16], 16, m["pool_rsB"])
            pool.wait_ge(m["dve_onorm"], 1)
            for t in range(TT):
                power(hstat[:, 32 + 16 * t:48 + 16 * t], hstat[:, 64 + 16 * t:80 + 16 * t], 16, m["pool_ors"])
            pool.wait_ge(m["act_oB"], 2)
            pool.wait_ge(m["dve_sB"], NCH + 1)
            pool.dma_start(v_mem, mem_d).then_inc(ld_mem, 16)
            norm(1)
            norm(2)
            pool.wait_ge(at_ol, 4)
            pool.dma_start(area(2048, D), gfinal_d[0].partition_broadcast(P)).then_inc(ld_fin, 16)
            norm(3)
            norm(4)
            for l in range(LAYERS):
                if l:
                    pool.wait_ge(l_["pe_up"], 4 * l)
                pool.dma_start(lat_w[:], lat_d[l]).then_inc(ld_lat, 16)
                norm(5 + 2 * l)
                pool.wait_ge(l_["dve_ms"], l + 1)
                power(lstat[:, 8:12], lstat[:, 4:8], 4, l_["pool_rs"])
                norm(6 + 2 * l)
            pool.wait_ge(res_out, 28)
            pool.dma_start(area(2048, D), gfinal_d[1].partition_broadcast(P)).then_inc(ld_fin, 16)
            norm(9)
            for t in range(TT):
                pool.wait_ge(m["dve_out"], 2 * t + 2)
                pool.dma_start(out_d[:, t], xn[:, t]).then_inc(stored, 16)
            pool.wait_ge(stored, 32)

        @block.vector
        def _(dve):
            s = Steps(dve, v_step)

            def split(c, slot, size):
                for part in range(2):
                    split_part(c, slot, size, part)

            def split_part(c, slot, size, part):
                dve.wait_ge(hi_done, c * 2 + (part + 1))
                a, b = (0, cut(size)) if part == 0 else (cut(size), size)
                dve.tensor_tensor(w_lo[:, slot, a:b], raw[:, slot, a:b], w_hi[:, slot, a:b].bitcast(F32),
                                  ALU.subtract).then_inc(lo_done, 1)

            def norm(k, dst=None, gain=None, signal=None):
                dve.wait_ge(n_ss, 2 * k + 2)
                s(dve.tensor_scalar(stat[:, MS + 2 * k:MS + 2 * k + 2], stat[:, SS + 2 * k:SS + 2 * k + 2], 1.0 / D, EPS,
                                    ALU.mult, ALU.add), n_ms)
                dve.wait_ge(n_rs, k + 1)
                if gain is not None:
                    dve.wait_ge(ld_fin, 16 if k == 4 else 32)
                    for q in range(4):
                        t, c = q // 2, slice(q % 2 * 512, q % 2 * 512 + 512)
                        s(dve.scalar_tensor_tensor(out=dst[:, t, c], in0=res[:, t, c], scalar=stat[:, RS + 2 * k + t:RS + 2 * k + t + 1],
                                                   in1=gain[:, c], op0=ALU.mult, op1=ALU.mult), signal)
                    return
                dst = v_mem if k == 1 else xn[:]
                for t in range(TT):
                    s(dve.tensor_scalar(dst[:, t], sources(k)[:, t], stat[:, RS + 2 * k + t:RS + 2 * k + t + 1], None,
                                        ALU.mult), n_xn)

            def tsplit(k, gain):
                for q in range(4):
                    t, half = q // 2, q % 2
                    dve.wait_ge(t_ps, 4 * k + q + 1)
                    if q >= 2:
                        s.fence()
                    src = ps[:, 4 + q, :].rearrange("p (a b) -> p a b", b=P)
                    if gain is None:
                        s(dve.tensor_copy(t32[:, q % 2], src), t_32)
                    else:
                        g = G["gains"][:, gain, 4 * half:4 * half + 4].unsqueeze(2)
                        s(dve.tensor_tensor(t32[:, q % 2], src, bc(g, 4, P), ALU.mult), t_32)
                    dve.wait_ge(t_hi, 4 * k + q + 1)
                    dst = (slice(None), slice(4 * half, 4 * half + 4), slice(t * P, (t + 1) * P))
                    s(dve.tensor_tensor(hT_lo[dst], t32[:, q % 2], hT_hi[dst].bitcast(F32), ALU.subtract), t_lo)

            def splits_only(c0, n, loop_to=0):
                section(dve, c0, n, 0, loop_to, split, lambda i, slot: None)

            def residual(c0):
                splits_only(c0, 4)
                add_residual(c0 + 4)

            def add_residual(c):
                dve.wait_ge(used, 2 * c)
                for q in range(4):
                    part = res[:, q // 2, q % 2 * 512:q % 2 * 512 + 512]
                    s(dve.tensor_tensor(part, ps[:, q], part, ALU.add), res_out)

            def ffn(c0, n):
                base = n * NFT

                def one(i, slot=None):
                    slot = i % 2 if slot is None else slot
                    tile = not isinstance(i, int) or i < NFT
                    size, c = (chunk_size(c0 + i + 2), c0 + i + 2) if isinstance(i, int) else (3072, i + (c0 + 2))
                    if tile:
                        u = [ps[:, 4 + slot, g * T:(g + 1) * T] for g in range(2)]
                        y = [conv_g[:, slot], conv_v[:, slot]]
                        wc = ptab["ffn_conv"][0] + n * NFT * 6
                        dve.wait_ge(ff_tap, i + (base + 1))
                        for g in range(2):
                            ins = dve.scalar_tensor_tensor(out=y[g][:, 1:T], in0=u[g][:, 0:T - 1],
                                                           scalar=params[:, bass.ds(i * 6 + (wc + 3 * g + 1), 1)],
                                                           in1=y[g][:, 1:T], op0=ALU.mult, op1=ALU.add)
                        ins.then_inc(ff_c1, 1)
                        dve.wait_ge(ff_c1, i + (base + 1))
                        for g in range(2):
                            ins = dve.scalar_tensor_tensor(out=y[g][:, 2:T], in0=u[g][:, 0:T - 2],
                                                           scalar=params[:, bass.ds(i * 6 + (wc + 3 * g), 1)],
                                                           in1=y[g][:, 2:T], op0=ALU.mult, op1=ALU.add)
                        ins.then_inc(ff_conv, 1)
                    if size:
                        split_part(c, slot, size, 0)
                    if tile:
                        dve.wait_ge(ff_silu, i + (base + 1))
                        if not isinstance(i, int) or i >= 2:
                            dve.wait_ge(ff_lo, i + (base - 1))
                        dve.wait_ge(ff_conv, i + (base + 1))
                        dve.tensor_tensor(act32[:, slot], gated[:, slot], y[1], ALU.mult).then_inc(ff_act, 1)
                    if size:
                        split_part(c, slot, size, 1)
                    if tile:
                        dve.wait_ge(ff_hi, i + (base + 1))
                        dve.tensor_tensor(a_lo[:, slot], act32[:, slot], a_hi[:, slot].bitcast(F32), ALU.subtract).then_inc(ff_lo, 1)
                one(0)
                one(1)
                pairs(dve, 2, 20, one)
                for i in range(20, NFC):
                    one(i)
                add_residual(c0 + NFC)

            def attention(j0, us, between=None):
                for i in range(len(us) + 1):
                    if i < len(us):
                        j, u = j0 + i, us[i]
                        n = P * u["blocks"]
                        dve.wait_ge(at_s, j + 1)
                        if j >= 3:
                            dve.wait_ge(at_pt, j - 2)
                        for h, head in enumerate(u["heads"]):
                            ins = dve.tensor_tensor_reduce(p_sb[:, j % 3, h, 0:n], pair_scores(j)[0][:, h, 0:n], head["mask"],
                                                           head["scale"], 3.0e38, ALU.add, ALU.min, ast[:, j % 3, 0, h:h + 1])
                        s(ins, at_max)
                    if i >= 1:
                        j, u = j0 + i - 1, us[i - 1]
                        n = P * u["blocks"]
                        dve.wait_ge(at_exp, j + 1)
                        s(dve.reciprocal(ast[:, j % 3, 2], ast[:, j % 3, 1]))
                        s.fence()
                        s(dve.tensor_tensor(p_sb[:, j % 3, :, 0:n], p_sb[:, j % 3, :, 0:n],
                                            bc(ast[:, j % 3, 2].unsqueeze(2), 2, n), ALU.mult), at_p)
                    if between:
                        between(i)

            def oT_low(a):
                for q in range(4):
                    dve.wait_ge(at_oh, a + q + 1)
                    s(dve.tensor_tensor(hT_lo[:, 2 * q:2 * q + 2], ps[:, q].rearrange("p (a b) -> p a b", b=T),
                                        hT_hi[:, 2 * q:2 * q + 2].bitcast(F32), ALU.subtract), at_ol)

            def rotate(x1, x2, cos, sin, tmp, signal=None):
                s(dve.tensor_tensor(tmp[0], x1, cos, ALU.mult))
                s(dve.tensor_tensor(tmp[1], x2, sin, ALU.mult))
                s(dve.tensor_tensor(tmp[2], x2, cos, ALU.mult))
                s(dve.tensor_tensor(tmp[3], x1, sin, ALU.mult))
                s.fence()
                s(dve.tensor_tensor(x1, tmp[0], tmp[1], ALU.subtract))
                s(dve.tensor_tensor(x2, tmp[2], tmp[3], ALU.add), signal)

            def even_odd(first):
                return ps[:, 0:2, first * P:(first + 2) * P].rearrange("p a (b c) -> p a b c", c=P)

            split(0, 0, chunk_size(0))
            split(1, 1, chunk_size(1))
            dve.wait_ge(ld_c, 80)
            norm(0)
            tsplit(0, 0)
            splits_only(C_IN, IN_CHUNKS, IN_CHUNKS - 2)

            s(dve.tensor_copy(posf[:, 0:TT], pos_i[:]))
            s.fence()
            for t in range(TT):
                ins = dve.tensor_scalar(trig[:, 0, t], K["freq"], posf[:, t:t + 1], None, ALU.mult)
            s(ins)
            s.fence()
            turn, a, b, c = 2 * np.pi, 6.28125, 0.0019350051879882812, 3.0199159e-07
            s(dve.tensor_scalar(trig[:, 3], trig[:, 0], 1 / turn, 12582912.0, ALU.mult, ALU.add))
            s.fence()
            s(dve.tensor_scalar(trig[:, 3], trig[:, 3], 12582912.0, None, ALU.subtract))
            for part in (a, b, c):
                s.fence()
                s(dve.scalar_tensor_tensor(out=trig[:, 0], in0=trig[:, 3], scalar=-part, in1=trig[:, 0], op0=ALU.mult, op1=ALU.add))
            s.fence()
            s(dve.tensor_scalar(trig[:, 2], trig[:, 0], float(np.float32(3.1415925)), -float(np.float32(3.1415925)), ALU.min, ALU.max))
            s(dve.scalar_tensor_tensor(out=trig[:, 1], in0=trig[:, 0], scalar=-1.0, in1=trig[:, 0], op0=ALU.mult, op1=ALU.min))
            s.fence()
            s(dve.tensor_scalar(trig[:, 1], trig[:, 1], float(np.pi / 2), None, ALU.add), m["dve_ang"])

            dve.wait_ge(m["pe_ztp"], 7)
            s(dve.tensor_copy(lrT[0:16, :], ps[0:16, 6, 0:T]), m["dve_zcd"])
            for t in range(TT):
                tok = slice(t * P, (t + 1) * P)
                dve.wait_ge(m["act_zB"], 2 * t + 2)
                s(dve.tensor_scalar(cqkT[:, 0, tok], ps[:, 3 * t + 1, 256:384], 32 ** -0.5, None, ALU.mult))
                s(dve.tensor_copy(cqkT[:, 1, tok], ps[:, 3 * t + 1, 384:512]))
                s(dve.tensor_copy(dqT[:, :, tok], ps[:, 3 * t + 2, 0:256].rearrange("p (a b) -> p a b", b=P)), m["dve_zcd"])
            dve.wait_ge(m["act_zB"], 4)
            for j in range(4):
                for ct in range(6):
                    wgt = G["gdn_conv"][:, ct, j:j + 1]
                    if j == 0:
                        ins = dve.tensor_scalar(yB[:, ct], zTb[:, ct, 0:T], wgt, None, ALU.mult)
                    else:
                        ins = dve.scalar_tensor_tensor(out=yB[:, ct], in0=zTb[:, ct, j:j + T], scalar=wgt, in1=yB[:, ct],
                                                       op0=ALU.mult, op1=ALU.add)
                s(ins, m["dve_conv"] if j == 3 else None)
                if j < 3:
                    s.fence()
            s(dve.tensor_copy(xl[:, :, 128:384], z[:, :, ZDF:ZDF + 256]))
            s(dve.tensor_tensor(xl[:, :, 384:388], z[:, :, ZBA:ZBA + 4], bc(R["dt_bias"].unsqueeze(1), TT, 4), ALU.add))
            s(dve.tensor_copy(xl[:, :, 388:392], z[:, :, ZBA + 4:ZBA + 8]))
            dve.wait_ge(m["pe_gl"], 1)
            s(dve.tensor_tensor(xl[:, :, 0:128], ps[:, 7, 0:256].rearrange("p (a b) -> p a b", b=P),
                                bc(R["gk_bias"].unsqueeze(1), TT, P), ALU.add))
            s.fence()
            s(dve.scalar_tensor_tensor(out=ll, in0=xl, scalar=-1.0, in1=xl, op0=ALU.mult, op1=ALU.max), m["dve_ll"])
            dve.wait_ge(m["act_ang"], 1)
            for t in range(TT):
                qk = z[:, t, ZRQ:ZRQ + 512].rearrange("p (h c) -> p h c", c=64)
                cos, sin = (bc(trig[:, 1 + i, t].unsqueeze(1), 8, 32) for i in range(2))
                if t:
                    s.fence()
                rotate(qk[:, :, 0:32], qk[:, :, 32:64], cos, sin,
                       [ropes[:, i].rearrange("p (h c) -> p h c", c=32) for i in range(4)], m["dve_rope"] if t else None)
            dve.wait_ge(m["act_ll"], 1)
            s(dve.scalar_tensor_tensor(out=lf, in0=xl[:, :, 0:384], scalar=0.0, in1=ll[:, :, 0:384], op0=ALU.min, op1=ALU.subtract))
            s(dve.scalar_tensor_tensor(out=z[:, :, ZDF:ZDF + 256], in0=xl[:, :, 128:384], scalar=0.0, in1=ll[:, :, 128:384],
                                       op0=ALU.max, op1=ALU.add))
            s(dve.scalar_tensor_tensor(out=g_b, in0=xl[:, :, 384:388], scalar=0.0, in1=ll[:, :, 384:388], op0=ALU.max, op1=ALU.add))
            s(dve.scalar_tensor_tensor(out=beta, in0=xl[:, :, 388:392], scalar=0.0, in1=ll[:, :, 388:392], op0=ALU.min,
                                       op1=ALU.subtract), m["dve_kd"])
            s.fence()
            s(dve.tensor_scalar(lf[:, :, 0:128], lf[:, :, 0:128], 1.0 / 16, None, ALU.mult))
            s(dve.scalar_tensor_tensor(out=g_b, in0=g_b, scalar=-1.0, in1=bc(ea.unsqueeze(1), TT, 4), op0=ALU.mult, op1=ALU.mult))
            dve.wait_ge(m["pe_kdT"], 1)
            s(dve.tensor_copy(kdT, ps[:, 4, :].rearrange("p (a b) -> p a b", b=T)), m["dve_kdT"])
            for side, dst in enumerate((qTA, kTA)):
                dve.wait_ge(m["pe_qkA"], side + 1)
                s(dve.tensor_copy(dst, ps[:, 5 + side, :].rearrange("p (a b) -> p a b", b=T)), m["dve_qkA"])
            s.fence()
            for t in range(TT):
                s(dve.tensor_tensor(qgT[:, 0:2, t * P:(t + 1) * P], qTA[:, :, t * P:(t + 1) * P], K["ret_qdecay"], ALU.mult))
            for t in range(TT):
                keys = z[:, t, ZRK:ZRK + 256].rearrange("p (h c) -> p h c", c=64)
                s(dve.tensor_tensor(keys, keys, bc(K["ret_ktail"].unsqueeze(2), 4, 64), ALU.mult), m["dve_ktA"] if t else None)
            for t in range(TT):
                dve.wait_ge(m["pe_scA"], 1)
                s(dve.tensor_tensor(pTA[:, t].rearrange("p (a b) c -> p a b c", b=2), even_odd(2 * t),
                                    K["ret_decay"].rearrange("p (a b) c -> p a b c", b=2), ALU.mult), m["dve_pA"])
            for t in range(TT):
                dve.wait_ge(m["act_gate"], t + 1)
                gate = z[:, t, ZG + 256:ZG + D].rearrange("p (a h c) -> p a h c", a=3, c=64)
                s(dve.tensor_tensor(gate, gate, bc(R["head_gains"].unsqueeze(2), 3, 4, 64), ALU.mult), m["dve_gate"])
            unit, hn = 0, 0
            dve.wait_ge(m["pe_o"], 2)
            for t in range(TT):
                tok = slice(t * P, (t + 1) * P)
                for g in range(3):
                    q_, k_ = (cqkT[:, 0, tok], cqkT[:, 1, tok]) if g == 0 else (dqT[:, g - 1, tok], kdT[:, g - 1, tok])
                    dve.wait_ge(m["act_fade"], unit + 1)
                    s(dve.tensor_tensor(ktT, k_, fades[:, 7], ALU.mult))
                    s(dve.tensor_tensor(qX, fades[:, 0:6], bc(q_.unsqueeze(1), 6, P), ALU.mult))
                    s(dve.tensor_tensor(qgT[:, 2 + g, tok], q_, fades[:, 6], ALU.mult))
                    s(dve.tensor_copy(cdecay[:, 2 + g, 2 * t:2 * t + 2], fades[:, 6, CH - 1:P:CH]))
                    s(dve.tensor_tensor(kX, fades[:, 0:6], bc(k_.unsqueeze(1), 6, P), ALU.mult), m["dve_qk"])
                    for h in range(4 if g == 0 else 2):
                        dve.wait_ge(m["pe_sc"], hn + 1)
                        if hn >= 2:
                            dve.wait_ge(m["pe_o"], 2 + hn - 1)
                        b = 2 + 2 * (hn % 2)
                        s(dve.tensor_tensor(pT7[:, hn % 2], ps[:, b:b + 2].rearrange("p a (b c) -> p (a b) c", c=P)[:, 0:7],
                                            K["levels"], ALU.mult), m["dve_pT"])
                        hn += 1
                    unit += 1
            dve.wait_ge(m["pe_o"], 18)
            both = ps[:, 0:2].rearrange("p a b -> p (a b)")[:, 0:768]
            for n in range(NCH - 1):
                dve.wait_ge(m["pe_kv"], n + 1)
                if n == 0:
                    s(dve.tensor_tensor(states[:, 0], both, K["own"], ALU.mult), m["dve_state"])
                    continue
                s.fence()
                s(dve.tensor_tensor(kv_own, both, K["own"], ALU.mult))
                s.fence()
                for g, (a, wd) in enumerate(((0, 128), (128, 128), (256, 256), (512, 128), (640, 128))):
                    cd = K["ret_cdecay"][:, g:g + 1] if g < 2 else cdecay[:, g, n:n + 1]
                    ins = dve.scalar_tensor_tensor(out=states[:, n, a:a + wd], in0=states[:, n - 1, a:a + wd], scalar=cd,
                                                   in1=kv_own[:, a:a + wd], op0=ALU.mult, op1=ALU.add)
                s(ins, m["dve_state"])
            dve.wait_ge(m["act_o"], 3)
            for t in range(TT):
                dve.wait_ge(m["pe_inter"], 1 if t == 0 else 3)
                r = slice(64, 128) if t == 0 else slice(0, 128)
                src = ps[r, 2 + 2 * t:4 + 2 * t].rearrange("p a b -> p (a b)")
                s(dve.tensor_tensor(xn[r, t, 0:256], xn[r, t, 0:256], src[:, 0:256], ALU.add))
                s(dve.tensor_tensor(xn[r, t, 512:1024], xn[r, t, 512:1024], src[:, 256:768], ALU.add), m["dve_inter"])

            dve.wait_ge(m["act_sqB"], 1)
            hs = hstat[:, 0:16].rearrange("p (a b) -> p a b", b=8)
            s(dve.tensor_reduce(hs, squares.rearrange("p a (h c) -> p a h c", c=64), AX_X, ALU.add))
            s.fence()
            s(dve.tensor_scalar(hs, hs, EPS, None, ALU.add))
            s(dve.tensor_copy(g_exp.rearrange("p a (h c) -> p a h c", c=64), bc(g_b.unsqueeze(3), TT, 4, 64)), m["dve_b"])
            dve.wait_ge(m["pool_rsB"], 1)
            rs = hstat[:, 16:32].rearrange("p (a b) -> p a b", b=8)
            s(dve.tensor_scalar(rs[:, :, 0:4], rs[:, :, 0:4], 0.125, None, ALU.mult))
            s.fence()
            for t in range(TT):
                qk = z[:, t, 0:512].rearrange("p (h c) -> p h c", c=64)
                s(dve.tensor_tensor(qk, qk, bc(rs[:, t].unsqueeze(2), 8, 64), ALU.mult))
            s.fence()
            dve.wait_ge(m["act_gB"], 1)

            def heads(ap):
                return ap.rearrange("p (h c) -> p h c", c=64)
            for t in range(TT):
                b4, gm, tl = (bc(a_.unsqueeze(2), 4, 64) for a_ in (beta[:, t], natB[:, t, 0], natB[:, t, 1]))
                s(dve.tensor_tensor(heads(kb[:, t]), heads(z[:, t, 256:512]), b4, ALU.mult))
                s(dve.tensor_tensor(heads(qg[:, t]), heads(z[:, t, 0:256]), gm, ALU.mult))
                s(dve.tensor_tensor(heads(kt[:, t]), heads(z[:, t, 256:512]), tl, ALU.mult))
                s(dve.tensor_tensor(heads(z[:, t, 512:768]), heads(z[:, t, 512:768]), b4, ALU.mult))
                s.fence()
                s(dve.tensor_tensor(heads(kbg[:, t]), heads(kb[:, t]), gm, ALU.mult), m["dve_natB"] if t else None)
            for side, dst in enumerate((qTB, kTB, kbT, qgB)):
                dve.wait_ge(m["pe_tB"], side + 1)
                s(dve.tensor_copy(dst, ps[:, side, :].rearrange("p (a b) -> p a b", b=T)), m["dve_tB"])

            def four(ap):
                return ap.rearrange("p (a b) c -> p a b c", b=2)

            def bank(b):
                return ps[:, b, :].rearrange("p (a b) -> p a b", b=P)
            for t in range(TT):
                for h in range(4):
                    ins = dve.tensor_scalar(xB[:, place(h)], K["sums"][:, 7], g_b[:, t, h:h + 1], None, ALU.mult)
                s(ins, m["dve_xB"])
                dve.wait_ge(m["act_rB"], t + 1)
                s(dve.tensor_tensor(ratio_s, ratio_i, bc(K["strict"].unsqueeze(1), 4, P), ALU.mult))
                s.fence()
                s(dve.tensor_tensor(ratio_i, ratio_i, bc(K["incl"].unsqueeze(1), 4, P), ALU.mult))
                dve.wait_ge(m["pe_kkB"], t + 1)
                s(dve.tensor_tensor(four(nT), even_odd(0), four(ratio_s), ALU.mult))
                s.fence()
                s(dve.tensor_tensor(four(pB[:, t]), even_odd(2), four(ratio_i), ALU.mult))
                if t:
                    dve.wait_ge(m["pe_uvB"], 1)
                s(dve.tensor_tensor(nmT, nT, bc(K["levels"][:, 5].unsqueeze(1), 4, P), ALU.mult))
                s.fence()
                s(dve.tensor_tensor(xBT, bc(K["ident"].unsqueeze(1), 4, P), nmT, ALU.subtract), m["dve_xB"])
                dve.wait_ge(m["pe_xB"], t * 11 + 1)
                s.fence()
                s(dve.tensor_copy(xB, bank(2)))
                s(dve.tensor_tensor(nmT, nT, bc(K["levels"][:, 4].unsqueeze(1), 4, P), ALU.mult), m["dve_xB"])
                for lev in range(5):
                    dve.wait_ge(m["pe_xB"], t * 11 + 3 + 2 * lev)
                    s.fence()
                    if lev < 4:
                        s(dve.tensor_tensor(xB, xB, bank(0), ALU.subtract))
                        s(dve.tensor_tensor(nmT, nT, bc(K["levels"][:, 3 - lev].unsqueeze(1), 4, P), ALU.mult))
                    s(dve.tensor_tensor(xBT, xBT, bank(1), ALU.subtract), m["dve_xB"])
            dve.wait_ge(m["act_uvB"], 2)
            s.fence()
            s(dve.memset(stateB, 0.0), m["dve_sB"])
            for n in range(NCH):
                t, r = n // 2, slice(64 * (n % 2), 64 * (n % 2) + 64)
                dve.wait_ge(m["pe_wB"], n + 1)
                s(dve.tensor_tensor(u_nat[r, t], uv[r, t], ps[r, 0, 0:256], ALU.subtract), m["dve_uB"])
                if n == NCH - 1:
                    dve.wait_ge(m["pe_oB"], n + 1)
                    s(dve.memset(stateB, 0.0), m["dve_sB"])
                    break
                dve.wait_ge(m["pe_sB"], n + 1)
                s(dve.tensor_tensor(kuB, ps[:, 1, 0:256], K["own"][:, 0:256], ALU.mult))
                s.fence()
                for p in range(2):
                    ins = dve.scalar_tensor_tensor(out=stateB[:, p * P:(p + 1) * P], in0=stateB[:, p * P:(p + 1) * P],
                                                   scalar=decB[:, p, n:n + 1], in1=kuB[:, p * P:(p + 1) * P],
                                                   op0=ALU.mult, op1=ALU.add)
                s(ins, m["dve_sB"])
            dve.wait_ge(m["act_osq"], 1)
            hs = hstat[:, 64:96].rearrange("p (a b) -> p a b", b=16)
            s(dve.tensor_reduce(hs, area(4096, TT, D).rearrange("p a (h c) -> p a h c", c=64), AX_X, ALU.add))
            s.fence()
            s(dve.tensor_scalar(hs, hs, 1.0 / 64, EPS, ALU.mult, ALU.add), m["dve_onorm"])
            for t in range(TT):
                dve.wait_ge(m["pool_ors"], t + 1)
                o = xn[:, t].rearrange("p (h c) -> p h c", c=64)
                s(dve.tensor_tensor(o, o, bc(hstat[:, 32 + 16 * t:48 + 16 * t].unsqueeze(2), 16, 64), ALU.mult))
                s.fence()
                s(dve.tensor_tensor(xn[:, t], xn[:, t], z[:, t, ZG:ZG + D], ALU.mult), m["dve_on"])

            norm(1)
            tsplit(1, 1)
            splits_only(C_K, 4)
            splits_only(C_V, 4)
            dve.wait_ge(used, 2 * (C_V + 4))
            tsplit(2, None)
            residual(C_OUT)
            norm(2)
            tsplit(3, 2)
            splits_only(C_Q, 4)
            attention(0, CROSS)
            oT_low(0)
            residual(C_O)
            norm(3)
            tsplit(4, 3)
            ffn(C_FFN, 0)
            norm(4, res, area(2048, D), res_out)
            for l in range(LAYERS):
                b = C_LAYER + l * LAYER_CHUNKS
                norm(5 + 2 * l)
                tsplit(5 + 2 * l, 4 + 2 * l)
                splits_only(b, IN2_CHUNKS, IN2_CHUNKS - 2)
                dve.wait_ge(l_["act_ss"], 4 * (l + 1))
                st = lstat[:, 0:8].rearrange("p (k a b) -> p k a b", k=2, b=2)
                s(dve.tensor_scalar(st[:, 1, :, 0], st[:, 0, :, 0], 1.0 / 256, EPS, ALU.mult, ALU.add))
                s(dve.tensor_scalar(st[:, 1, :, 1], st[:, 0, :, 1], 1.0 / 128, EPS, ALU.mult, ALU.add), l_["dve_ms"])
                dve.wait_ge(l_["pool_rs"], l + 1)
                for t in range(TT):
                    for i, (c, n) in enumerate(((YCQ, 256), (YKV, 128))):
                        ins = dve.tensor_scalar(z[:, t, c:c + n], z[:, t, c:c + n], lstat[:, 8 + 2 * t + i:9 + 2 * t + i], None, ALU.mult)
                s(ins, l_["dve_n"])
                for t in range(TT):
                    dve.wait_ge(l_["pe_lat"], 2 * l + t + 1)
                    s(dve.tensor_tensor(latT[:, :, t * P:(t + 1) * P], ps[:, 4 + t, 0:384].rearrange("p (a b) -> p a b", b=P),
                                        bc(G["g_lat"][:, l].unsqueeze(2), 3, P), ALU.mult), l_["dve_lat"])
                def quad(n, *shape):
                    return [shaped(xn[:].rearrange("p a b -> p (a b)")[:, i * 384:i * 384 + n], shape) for i in range(4)]
                hd = z[:, :, YDQ:YDQ + 1536].rearrange("p a (h c) -> p a h c", c=64)
                rotate(hd[:, :, :, 0:8], hd[:, :, :, 8:16], *(bc(K[n].unsqueeze(2), TT, 24, 8) for n in ("cos_h", "sin_h")),
                       quad(384, TT, 24, 8))
                ix = z[:, :, YQI:YQI + 288].rearrange("p a (h c) -> p a h c", c=32)
                s.fence()
                rotate(ix[:, :, :, 0:4], ix[:, :, :, 4:8], *(bc(K[n].unsqueeze(2), TT, 9, 4) for n in ("cos_i", "sin_i")),
                       quad(72, TT, 9, 4))
                s.fence()
                kp = z[:, :, YPE:YPE + 32]
                rotate(kp[:, :, 0:16], kp[:, :, 16:32], K["cos_a"], K["sin_a"], quad(32, TT, 16))
                dve.wait_ge(l_["act_up"], 2 * (l + 1))
                s.fence()
                mq = z[:, :, 3024:3408].rearrange("p a (h c) -> p a h c", c=96)
                rotate(mq[:, :, :, 64:80], mq[:, :, :, 80:96], *(bc(K[n].unsqueeze(2), TT, 4, 16) for n in ("cos_a", "sin_a")),
                       quad(128, TT, 4, 16))
                s.fence()
                s(dve.tensor_copy(z[:, :, 3408:3792].rearrange("p a (h c) -> p a h c", c=96)[:, :, :, 64:96],
                                  bc(kp.unsqueeze(2), TT, 4, 32)))
                s(dve.tensor_copy(z[:, :, 0:128].rearrange("p a (h c) -> p a h c", c=32),
                                  bc(z[:, :, YKI:YKI + 32].unsqueeze(2), TT, 4, 32)))
                s(dve.tensor_scalar(wis[:], z[:, :, YWI:YWI + 8], 256 ** -0.5, None, ALU.mult), l_["dve_rope"])
                for n in range(1, 12, 2):
                    t, g = n // 6, n % 6
                    dve.wait_ge(l_["pe_tT"], 12 * l + n + 1)
                    r, k = 96 if g < 2 else P, 3 if g == 5 else 4
                    s(dve.tensor_copy(tT[0:r, 4 * g:4 * g + k, t * P:(t + 1) * P],
                                      ps[0:r, n % 8, 0:k * P].rearrange("p (a b) -> p a b", b=P)), l_["dve_tT"])
                for t in range(TT):
                    n = P * (t + 1)
                    dve.wait_ge(l_["act_relu"], 2 * l + t + 1)
                    for h in range(8):
                        if h:
                            s.fence()
                        s(dve.scalar_tensor_tensor(out=score[t][:, 0:n], in0=relus[:, 2 * (h % 4) + h // 4, 0:n], scalar=wis[:, t, h:h + 1],
                                                   in1=K["causal"][:, t, 0:n] if h == 0 else score[t][:, 0:n],
                                                   op0=ALU.mult, op1=ALU.add), l_["dve_sum"] if h == 7 else None)
                s.fence()
                rounds = TOPK // 8

                def best_keys(step):
                    t, i = divmod(step, rounds + 1)
                    n = P * (t + 1)
                    src = score[t][:, 0:n] if i == 0 else work[:, 0:n]
                    s.fence()
                    if i < rounds:
                        s(dve.max(best, src))
                        s.fence()
                        s(dve.match_replace(work[:, 0:n], best, src, -3.0e38))
                        return
                    s(dve.tensor_tensor(work[:, 0:n], src, score[t][:, 0:n], ALU.is_equal))
                    s.fence()
                    s(dve.scalar_tensor_tensor(out=dsa_mask[:, t, 0:n], in0=work[:, 0:n], scalar=NEG, in1=K["causal"][:, t, 0:n],
                                               op0=ALU.mult, op1=ALU.add))
                    s.fence()

                def between(i):
                    before, steps = len(LAYER) * 3 // 4, 2 * (rounds + 1)
                    if i < before:
                        for step in range(i * steps // before, (i + 1) * steps // before):
                            best_keys(step)
                attention(first_pair(l), LAYER, between)
                oT_low(4 * (l + 1))
                residual(b + IN2_CHUNKS)
                norm(6 + 2 * l)
                tsplit(6 + 2 * l, 5 + 2 * l)
                ffn(b + IN2_CHUNKS + 4, l + 1)
            norm(9, xn, area(2048, D), m["dve_out"])


def pack_columns(w, cols):
    n = w.shape[1] // cols
    return np.ascontiguousarray(w.reshape(KT, P, n, cols).transpose(2, 1, 0, 3)).reshape(n, P, KT * cols)


def pack_rows(w):
    return np.ascontiguousarray(w.reshape(4, 2, P, D).transpose(0, 2, 1, 3)).reshape(4, P, 2 * D)


def pack_ffn(up, down):
    u = up.reshape(KT, P, 2, NFT, P).transpose(3, 1, 0, 2, 4).reshape(NFT, P, KT * 2 * P)
    d = down.reshape(NFT, P, D)
    mid = np.concatenate([u[1:], d[:-1]], axis=2)
    last = d[-1].reshape(P, 2, D // 2).transpose(1, 0, 2)
    return u[:1], mid, last


def kernel(**inputs):
    import concourse.bacc as bacc
    from concourse.bass_utils import run_bass_kernel_spmd

    a = {k: np.asarray(v) for k, v in inputs.items()}

    def by_partition(rows_):
        v = rows_.reshape(*rows_.shape[:-1], -1, P)
        return np.moveaxis(v, -1, 0).reshape(P, -1)

    arrays = {
        "x": np.ascontiguousarray(a["x"].reshape(TT, P, D).transpose(1, 0, 2)),
        "mem": np.ascontiguousarray(a["mem"].reshape(TT, P, D).transpose(1, 0, 2)),
        "pos": np.ascontiguousarray(a["positions"].reshape(TT, P).T),
    }
    made = shape_constants()
    arrays["consts"] = np.concatenate([made[n].reshape(P, -1) for n in CONSTS], axis=1)
    gains = np.stack([a["mix_norm_w"][0], a["mem_norm_w"], a["xattn_norm_w"][0], a["ffn_norm_w"][0],
                      a["g_attn_2"][0], a["g_ffn_2"][0], a["g_attn_2"][1], a["g_ffn_2"][1]])
    lat = np.concatenate([a["g_q_lat_2"], a["g_kv_lat_2"]], axis=1)
    convs = np.concatenate([a["ffn_conv_w"], a["conv_w_2"]], axis=0)
    convs = convs.reshape(3, 3, 2, NFT, P).transpose(4, 0, 3, 2, 1).reshape(P, -1)
    bias = np.concatenate([np.zeros((1, 2 * FF), np.float32), a["conv_b_2"]], axis=0)
    bias = bias.reshape(3, 2, NFT, P).transpose(3, 0, 2, 1).reshape(P, -1)
    gdn = a["gdn_conv_w"][0].reshape(4, 6, P).transpose(2, 1, 0).reshape(P, -1)
    arrays["params"] = np.concatenate([by_partition(gains), by_partition(lat), gdn, convs, bias], axis=1)
    arrays["rows"] = np.concatenate([a["gdn_a_log"][0], a["gdn_dt_bias"][0], a["gla_gk_bias"][0], a["gdn_norm_w"][0],
                                     a["gla_norm_w"][0], a["hgrn_norm_w"][0]])
    arrays["gfinal"] = np.stack([a["final_norm_w"], a["g_final_2"]])
    arrays["gkup"] = a["gla_gk_up"][0]
    uq = a["w_uq_2"].reshape(LAYERS, 2, P, 384).transpose(0, 2, 1, 3).reshape(LAYERS, P, 768)
    arrays["lat"] = np.concatenate([uq, a["w_ukv_2"]], axis=2)

    w = a["w_in"][0]
    at = np.cumsum([0, 256, 256, 256, 256, 256, 256, 256, 4, 4, 256, 128, 128, 256, 16, 256, 256, 256, 256, 256])
    names = "rq rk rv rg bq bk bv ba bb bg cq ck cv lr cg dq df di dg".split()
    col = {n: w[:, at[i]:at[i + 1]] for i, n in enumerate(names)}
    order = "bq bk bv cq ck dq df rq rk rv cv di rg bg cg dg lr ba bb".split()
    w = np.concatenate([col[n] for n in order] + [np.zeros((D, ZW - 3864), np.float32)], axis=1)
    arrays["win"] = pack_columns(w, IN_COLS)
    arrays["wk"] = pack_columns(a["xattn_wk"][0], 256)
    arrays["wv"] = pack_rows(a["xattn_wv"][0])
    arrays["wout"] = pack_rows(a["w_out"][0])
    arrays["wq"] = pack_columns(a["xattn_wq"][0], 256)
    arrays["wo"] = pack_rows(a["xattn_wo"][0])
    ffns = [pack_ffn(a["ffn_up"][0], a["ffn_down"][0])]
    ffns += [pack_ffn(a["w_up_2"][l], a["w_down_2"][l]) for l in range(LAYERS)]
    for i, n in enumerate("abc"):
        arrays["ffn_" + n] = np.concatenate([f[i] for f in ffns], axis=0)
    win2 = []
    for l in range(LAYERS):
        w = a["w_in_2"][l]
        dil, dsa, rest = w[:, 416:1952], w[:, 1952:2720], w[:, 2720:]
        w = np.concatenate([w[:, :416], dil[:, :1024], dsa[:, :512], rest[:, :288], dil[:, 1024:], dsa[:, 512:],
                            rest[:, 288:296], np.zeros((D, YW - 3016), np.float32)], axis=1)
        win2.append(pack_columns(w, IN2_COLS))
    arrays["win2"] = np.concatenate(win2)
    arrays["wo2"] = np.concatenate([pack_rows(a["w_o_2"][l]) for l in range(LAYERS)])

    nc = bacc.Bacc("TRN2", target_bir_lowering=False, num_devices=1)
    arrays = {f"in_{k}": np.ascontiguousarray(v) for k, v in arrays.items()}
    aps = {k[3:] + "_d": nc.dram_tensor(k, v.shape, mybir.dt.from_np(v.dtype), kind="ExternalInput").ap()
           for k, v in arrays.items()}
    out = nc.dram_tensor("out", (P, TT, D), F32, kind="ExternalOutput").ap()
    hybrid_two_block_kernel(nc, out_d=out, **aps)
    r = run_bass_kernel_spmd(nc, [arrays], core_ids=[0])
    return np.asarray(r.results[0]["out"]).transpose(1, 0, 2).reshape(1, T, D)
```

```python
from contextlib import ExitStack

import numpy as np
import concourse.bass as bass
from concourse import mybir

ALU = mybir.AluOpType
ACT = mybir.ActivationFunctionType
F32 = mybir.dt.float32
F32R = mybir.dt.float32r
I32 = mybir.dt.int32
AX_X = mybir.AxisListType.X

P = 128
T = 256
TT = T // P
D = 1024
KT = D // P
CH = 64
NCH = T // CH
FF = 2816
NFT = FF // P
NFC = NFT + 2
EPS = 1e-6
NEG = -1e30
SLOT = 3104
LAYERS = 2
TOPK = 64

ZB, ZCQ, ZCK, ZDQ, ZDF, ZRQ, ZRK, ZV, ZG, ZLR, ZBA = 0, 768, 896, 1024, 1280, 1536, 1792, 2048, 2816, 3840, 3856
ZW = 3880
IN_COLS, IN_CHUNKS = 388, 10
YCQ, YKV, YPE, YDQ, YDK, YSQ, YSK, YQI, YKI, YDV, YSV, YWI = 0, 256, 384, 416, 928, 1440, 1696, 1952, 2208, 2240, 2752, 3008
YW = 3024
IN2_COLS, IN2_CHUNKS = 378, 8
SQ_CHUNKS = 4

C_IN = 0
C_K = C_IN + IN_CHUNKS
C_V = C_K + SQ_CHUNKS
C_OUT = C_V + SQ_CHUNKS
C_Q = C_OUT + SQ_CHUNKS
C_O = C_Q + SQ_CHUNKS
C_FFN = C_O + SQ_CHUNKS
C_LAYER = C_FFN + NFC
LAYER_CHUNKS = IN2_CHUNKS + SQ_CHUNKS + NFC
END = C_LAYER + LAYERS * LAYER_CHUNKS


def section_sizes():
    out = [(C_IN, IN_CHUNKS, 8 * IN_COLS, "win"), (C_K, 4, 2048, "wk"), (C_V, 4, 2048, "wv"),
           (C_OUT, 4, 2048, "wout"), (C_Q, 4, 2048, "wq"), (C_O, 4, 2048, "wo")]
    out += ffn_sections(C_FFN, "ffn0")
    for l in range(LAYERS):
        b = C_LAYER + l * LAYER_CHUNKS
        out += [(b, IN2_CHUNKS, 8 * IN2_COLS, f"win2_{l}"), (b + IN2_CHUNKS, 4, 2048, f"wo2_{l}")]
        out += ffn_sections(b + IN2_CHUNKS + 4, f"ffn{l + 1}")
    return out


def ffn_sections(b, name):
    return [(b, 1, 2048, name + "a"), (b + 1, NFT - 1, 3072, name + "b"), (b + NFT, 2, 512, name + "c")]


def chunk_size(c):
    for b, n, size, _ in section_sizes():
        if b <= c < b + n:
            return size
    return None


def cut(size):
    return 2048 if size == 3072 else size // 2


def place(h):
    return 2 * (h % 2) + h // 2


def shape_constants():
    f = np.float32
    i = np.arange(P)
    same = (i[:, None] // CH) == (i[None, :] // CH)
    out = {"ident": np.eye(P, dtype=f)}
    sums = np.zeros((P, 8, P), f)
    levels = np.zeros((P, 7, P), f)
    for n, m in enumerate((32, 16, 8, 4, 2, 1)):
        blk, half = i // (2 * m), (i // m) % 2
        edge = blk * 2 * m + m - 1
        t1, t = i[:, None], i[None, :]
        second = (half[None, :] == 1) & (t1 > edge[None, :]) & (t1 <= t)
        first = (half[None, :] == 0) & (t1 > t) & (t1 <= edge[None, :])
        sums[:, n] = second | first
        levels[:, n] = (blk[:, None] == blk[None, :]) & (half[:, None] == 0) & (half[None, :] == 1)
    levels[:, 6] = np.eye(P)
    sums[:, 6] = same & (i[:, None] <= i[None, :])
    sums[:, 7] = same & (i[:, None] > i[None, :])
    out["sums"], out["levels"] = sums, levels
    out["incl"] = (same & (i[:, None] <= i[None, :])).astype(f)
    out["strict"] = (same & (i[:, None] < i[None, :])).astype(f)
    out["chunk_of"] = (i[:, None] // CH == np.arange(2)[None, :]).astype(f)
    lg = np.log(f(1) - np.exp2(f(-5) - np.arange(4, dtype=f))).astype(f)
    ks = f(64 ** -0.5)
    rel = (i[None, :] - i[:, None]).astype(f)
    dec = np.zeros((P, 4, P), f)
    for h in range(4):
        dec[:, place(h)] = np.where(same & (rel >= 0), np.exp(lg[h] * np.maximum(rel, 0)), 0) * ks
    out["ret_decay"] = dec
    pos = (i % CH).astype(f)
    out["ret_ktail"] = (np.exp(lg[None, :] * (f(CH) - 1 - pos[:, None])) * ks).astype(f)
    qd = np.zeros((P, 2, P), f)
    cd = np.zeros((P, 2), f)
    for p in range(2):
        h = 2 * p + i // 64
        qd[:, p] = np.exp(lg[h][:, None] * (pos[None, :] + 1))
        cd[:, p] = np.exp(lg[h] * f(CH))
    out["ret_qdecay"], out["ret_cdecay"] = qd, cd
    own = np.zeros((P, 768), f)
    for a, n in ((0, 2), (128, 2), (256, 4), (512, 2), (640, 2)):
        own[:, a:a + 64 * n] = (i[:, None] // (P // n)) == (np.arange(64 * n)[None, :] // 64)
    out["own"] = own
    q = (i[:, None] + P * np.arange(TT)[None, :])[:, :, None]
    s = np.arange(T)[None, None, :]
    out["causal"] = np.where(s <= q, 0, NEG).astype(f)
    d = q - s
    cnt = ((d >= 0) & (d <= 128)).astype(int) + ((d >= 0) & (d % 4 == 0)) + ((d >= 0) & (d % 16 == 0))
    out["dilated"] = np.where(cnt > 0, np.log(np.maximum(cnt, 1)) * 8.0, NEG).astype(f)
    out["none"] = np.zeros((P, T), f)
    out["neg_half"] = np.full((P, 16), -0.5, f)
    out["freq"] = np.broadcast_to((f(10000.0) ** (-np.arange(0, 64, 2, dtype=f) / f(64))).astype(f), (P, 32))
    for name, dim in (("a", 32), ("h", 16), ("i", 8)):
        inv = np.power(f(500000.0), -np.arange(0, dim, 2, dtype=f) / f(dim)).astype(f)
        ang = (np.arange(T, dtype=f)[:, None] * inv[None, :]).reshape(TT, P, dim // 2).transpose(1, 0, 2)
        out["cos_" + name], out["sin_" + name] = np.cos(ang).astype(f), np.sin(ang).astype(f)
    return out


def table_of(parts):
    at, out = 0, {}
    for name, shape in parts.items():
        n = int(np.prod(shape))
        out[name] = (at, shape)
        at += n
    return out, at


CONSTS = {"ident": (P,), "neg_half": (16,), "sums": (8, P), "levels": (7, P), "incl": (P,), "strict": (P,), "chunk_of": (2,),
          "ret_decay": (4, P), "ret_ktail": (4,), "ret_qdecay": (2, P), "ret_cdecay": (2,), "own": (768,),
          "causal": (TT, T), "dilated": (TT, T), "none": (T,), "freq": (32,),
          "cos_a": (TT, 16), "sin_a": (TT, 16), "cos_h": (TT, 8), "sin_h": (TT, 8), "cos_i": (TT, 4), "sin_i": (TT, 4)}
CONSTS_FIRST = P + 16
PARAMS = {"gains": (8, KT), "g_lat": (LAYERS, 3), "gdn_conv": (6, 4), "ffn_conv": (3, NFT, 2, 3),
          "ffn_bias": (3, NFT, 2)}
ROWS = {"a_log": (4,), "dt_bias": (4,), "gk_bias": (P,), "head_gains": (3, 64)}


def hybrid_two_block_kernel(nc, x_d, mem_d, pos_d, consts_d, params_d, rows_d, gfinal_d, gkup_d, lat_d,
                            win_d, wk_d, wv_d, wout_d, wq_d, wo_d, ffn_a_d, ffn_b_d, ffn_c_d, win2_d, wo2_d, out_d):
    ctx = ExitStack()
    with ctx:
        def sb(name, shape, dt=F32):
            return ctx.enter_context(nc.sbuf_tensor(name, shape, dt))

        def sem(name):
            return ctx.enter_context(nc.semaphore(name))

        ps = ctx.enter_context(nc.psum_tensor("ps", [P, 8, 512], F32))
        raw = sb("raw", [P, 2, SLOT])
        w_hi = sb("w_hi", [P, 2, SLOT], F32R)
        w_lo = sb("w_lo", [P, 2, SLOT], F32R)
        z = sb("z", [P, TT, ZW])
        res = sb("res", [P, TT, D])
        hT_hi = sb("hT_hi", [P, KT, T], F32R)
        hT_lo = sb("hT_lo", [P, KT, T], F32R)
        xn = sb("xn", [P, TT, D])
        ctab, cn = table_of(CONSTS)
        ptab, pn = table_of(PARAMS)
        rtab, rn = table_of(ROWS)
        consts = sb("consts", [P, cn])
        params = sb("params", [P, pn])
        rows = sb("rows", [P, rn])
        lat_w = sb("lat_w", [P, 1280])
        gkup = sb("gkup", [16, P])
        stat = sb("stat", [P, 64])
        hstat = sb("hstat", [P, 96])
        lstat = sb("lstat", [P, 12])
        ast = sb("ast", [P, 3, 3, 2])
        wis = sb("wis", [P, TT, 8])
        best = hstat[:, 0:8]
        posf = sb("posf", [P, TT])
        pos_i = sb("pos_i", [P, TT], I32)
        a_hi = sb("a_hi", [P, 2, T], F32R)
        a_lo = sb("a_lo", [P, 2, T], F32R)
        ARENA = 9728
        arena = sb("arena", [P, ARENA])

        def shaped(ap, shape):
            if len(shape) == 2:
                return ap.rearrange("p (a b) -> p a b", b=shape[1])
            if len(shape) == 3:
                return ap.rearrange("p (a b c) -> p a b c", b=shape[1], c=shape[2])
            if len(shape) == 4:
                return ap.rearrange("p (a b c d) -> p a b c d", b=shape[1], c=shape[2], d=shape[3])
            return ap

        def views(buf, tab):
            return {n: shaped(buf[:, at:at + int(np.prod(shape))], shape) for n, (at, shape) in tab.items()}

        def area(at, *shape):
            n = int(np.prod(shape))
            assert at + n <= ARENA, (at, n)
            return shaped(arena[:, at:at + n], shape)

        def rows_flat(buf, at, *shape):
            n = int(np.prod(shape))
            return shaped(buf[:].rearrange("p a b -> p (a b)")[:, at:at + n], shape)

        K, G, R = views(consts, ctab), views(params, ptab), views(rows, rtab)

        cqkT, dqT, kdT = area(0, 2, T), area(512, 2, T), area(1024, 2, T)
        lf = area(1536, TT, 384)
        g_b, beta, ea = shaped(hstat[:, 56:64], (TT, 4)), shaped(hstat[:, 64:72], (TT, 4)), hstat[:, 72:76]
        lrT = area(2336, T)
        zTb, yB = area(2592, 6, T + 3), area(4146, 6, T)
        xl, ropes = rows_flat(xn, 0, TT, 392), rows_flat(xn, 1024, 4, 256)
        trig, ll = area(6912, 4, TT, 32), area(8704, TT, 392)
        qgT = area(5632, 5, T)
        pT7, pT_sum, fades = area(6912, 7, P), area(5024, 2, P), area(8704, 8, P)
        qX, kX, ktT = (area(2592, 6, P), area(4256, 6, P)), (area(3360, 6, P), area(7936, 6, P)), area(4128, P)
        qTA, kTA = area(4256, 2, T), area(4768, 2, T)
        pTA = area(6912, 2, 4, P)
        states, kv_own = area(6912, 3, 768), area(2592, 768)
        cdecay = area(5280, 5, NCH)
        qTB, kTB, kbT, qgB = area(0, 2, T), area(512, 2, T), area(1024, 2, T), area(1536, 2, T)
        kb, kbg, qg, kt = area(2048, TT, 256), area(2560, TT, 256), area(3072, TT, 256), area(3584, TT, 256)
        pB = area(4096, TT, 4, P)
        ratio_s, ratio_i = area(5120, 4, P), area(5632, 4, P)
        nT, nmT = area(6144, 4, P), area(6656, 4, P)
        xB, xBT, yBB = area(7168, 4, P), area(7680, 4, P), area(8192, 4, P)
        uv, wT = area(8704, TT, 256), area(9216, 2, T)
        u_nat, stateB, kuB = area(2048, TT, 256), area(5120, 256), area(5376, 256)
        g_exp = area(5632, TT, 256)
        natB_flat, decB_flat = hstat[:, 32:48], hstat[:, 48:56]
        natB, decB = shaped(natB_flat, (TT, 2, 4)), shaped(decB_flat, (2, NCH))
        squares = area(7168, TT, 512)
        kT_mem, v_mem, qT_x = area(0, KT, T), area(2048, TT, D), area(4096, KT, T)
        tT = area(0, 24, T)
        latT = area(6144, 3, T)
        p_sb, pT = area(6912, 3, 2, T), area(8448, 2, 2, T)
        dsa_mask, score = area(6144, TT, T), (area(6656, T), area(9472, T))
        relus = (shaped(z[:, 0, YDQ:YDQ + 8 * P], (8, P)), rows_flat(xn, 0, 8, T))
        work = z[:, 1, YDQ:YDQ + T]
        mem_rows = z[:, :, ZG - D:ZG]
        conv_g, conv_v, gated, act32 = area(0, 2, T), area(512, 2, T), area(1024, 2, T), area(1536, 2, T)

        landed = [sem("landed_0"), sem("landed_1")]
        hi_done, lo_done, used = sem("hi_done"), sem("lo_done"), sem("used")
        ld_x, ld_c, ld_tab, ld_mem, ld_lat, ld_fin, stored = (sem(n) for n in ("ld_x", "ld_c", "ld_tab", "ld_mem", "ld_lat", "ld_fin", "stored"))
        n_ss, n_sum, n_ms, n_rs, n_xn = sem("n_ss"), sem("n_sum"), sem("n_ms"), sem("n_rs"), sem("n_xn")
        bank_done = sem("bank_done")
        t_ps, t_32, t_hi, t_lo = sem("t_ps"), sem("t_32"), sem("t_hi"), sem("t_lo")
        z_out, sq_out, res_out = sem("z_out"), sem("sq_out"), sem("res_out")
        ff_up, ff_tap, ff_c1, ff_conv, ff_silu, ff_act, ff_hi, ff_lo = (
            sem(n) for n in ("ff_up", "ff_tap", "ff_c1", "ff_conv", "ff_silu", "ff_act", "ff_hi", "ff_lo"))
        at_s, at_max, at_exp, at_p, at_pt, at_ptc, at_o, at_oh, at_ol = (
            sem(n) for n in ("at_s", "at_max", "at_exp", "at_p", "at_pt", "at_ptc", "at_o", "at_oh", "at_ol"))
        v_step, a_step, g_step = sem("v_step"), sem("a_step"), sem("g_step")
        m = {n: sem("m_" + n) for n in (
            "pe_ztp", "act_zB", "dve_zcd", "dve_conv", "act_conv", "pe_back", "act_back", "pe_gl", "dve_ll",
            "act_ll", "dve_kd", "act_kd", "dve_ang", "act_ang", "pe_kdT", "dve_kdT", "pe_fade", "act_fade", "dve_qk", "pool_qk",
            "pe_kt", "act_kt", "pe_sc", "dve_pT", "pe_o", "act_o", "dve_rope", "pe_qkA", "dve_qkA", "dve_ktA",
            "pe_scA", "dve_pA", "pe_kv", "dve_state", "pe_inter", "dve_inter",
            "dve_b", "act_sqB", "pool_rsB", "dve_natB", "pe_gB", "act_gB", "pe_tB", "dve_tB", "pe_rB", "act_rB", "pe_kkB",
            "pe_xB", "dve_xB", "pe_yB", "act_yB", "pe_uvB", "act_uvB", "pe_wB", "dve_uB", "pe_oB", "act_oB", "pe_sB", "dve_sB",
            "dve_onorm", "dve_out", "act_osq", "pool_ors", "dve_gate", "act_gate", "pool_init", "dve_on")}
        l_ = {n: sem("l_" + n) for n in (
            "act_ss", "dve_ms", "pool_rs", "dve_n", "pe_lat", "dve_lat", "pe_up", "act_up", "dve_rope", "pe_tT", "act_tT",
            "dve_tT", "pe_dots", "act_relu")}

        class Steps:

            def __init__(self, eng, step):
                self.eng, self.step, self.n, self.last = eng, step, {}, None

            def __call__(self, ins, signal=None):
                s = self.step if signal is None else signal
                ins.then_inc(s, 1)
                self.n[id(s)] = self.n.get(id(s), 0) + 1
                self.last = (s, self.n[id(s)])

            def fence(self):
                self.eng.wait_ge(*self.last)

        def bc(ap, *shape):
            return ap.broadcast_to([P, *shape])

        def pairs(eng, first, end, body):
            n = (end - first) // 2
            if n == 1:
                body(first)
                body(first + 1)
            elif n > 1:
                with eng.Fori(0, n) as j:
                    for s in range(2):
                        body(2 * j + (first + s), (first + s) % 2)

        block = ctx.enter_context(nc.Block())

        @block.sync
        def _(sp):
            sp.dma_start(res[:], x_d).then_inc(ld_x, 16)
            sp.dma_start(consts[:, 0:CONSTS_FIRST], consts_d[:, 0:CONSTS_FIRST]).then_inc(ld_c, 16)
            sp.dma_start(params[:], params_d).then_inc(ld_c, 16)

            def mixers_tables():
                sp.dma_start(consts[:, CONSTS_FIRST:cn], consts_d[:, CONSTS_FIRST:cn]).then_inc(ld_tab, 16)
                sp.dma_start(rows[:], rows_d.partition_broadcast(P)).then_inc(ld_tab, 16)
                sp.dma_start(gkup[:], gkup_d).then_inc(ld_tab, 16)
                sp.dma_start(pos_i[:], pos_d).then_inc(ld_tab, 16)

            def stream(c0, n, size, src, at=0):
                def one(c, slot, i):
                    if not isinstance(c, int) or c >= 2:
                        sp.wait_ge(lo_done, 2 * (c - 1))
                    sp.dma_start(raw[:, slot, 0:size], src[i]).then_inc(landed[slot], 16)

                head = 2 if c0 == 0 else 0
                for i in range(head):
                    one(c0 + i, (c0 + i) % 2, at + i)
                if head:
                    mixers_tables()
                loops = (n - head) // 2
                if loops > 1:
                    with sp.Fori(0, loops) as j:
                        for s in range(2):
                            one(2 * j + (c0 + head + s), (c0 + s) % 2, 2 * j + (at + head + s))
                    head += 2 * loops
                for i in range(head, n):
                    one(c0 + i, (c0 + i) % 2, at + i)

            stream(C_IN, IN_CHUNKS, 8 * IN_COLS, win_d)
            stream(C_K, 4, 2048, wk_d)
            stream(C_V, 4, 2048, wv_d)
            stream(C_OUT, 4, 2048, wout_d)
            stream(C_Q, 4, 2048, wq_d)
            stream(C_O, 4, 2048, wo_d)

            def ffn(c0, n):
                stream(c0, 1, 2048, ffn_a_d, n)
                stream(c0 + 1, NFT - 1, 3072, ffn_b_d, n * (NFT - 1))
                stream(c0 + NFT, 2, 512, ffn_c_d, 2 * n)

            ffn(C_FFN, 0)
            for l in range(LAYERS):
                b = C_LAYER + l * LAYER_CHUNKS
                stream(b, IN2_CHUNKS, 8 * IN2_COLS, win2_d, l * IN2_CHUNKS)
                stream(b + IN2_CHUNKS, 4, 2048, wo2_d, 4 * l)
                ffn(b + IN2_CHUNKS + 4, l + 1)

        SS, MS, RS = 0, 20, 40

        def sources(k):
            return mem_rows if k == 1 else res[:]

        TOKENS_FIRST, HALVES_FIRST = (0, 1, 2, 3), (0, 2, 1, 3)

        def added(k):
            return HALVES_FIRST if k in (4, 7, 9) else TOKENS_FIRST

        def turned(left):
            return TOKENS_FIRST if left in (0, 5, 7) else HALVES_FIRST

        def quarter(buf, q):
            return buf[:, q // 2, q % 2 * 512:q % 2 * 512 + 512]

        def residual_ready(eng, k, i):
            if k == 0:
                eng.wait_ge(ld_x, 16)
            elif k == 1:
                eng.wait_ge(ld_mem, 16)
            else:
                eng.wait_ge(res_out, 4 * (k - 2) + i + 1)

        TSPLIT = {0: 0, 1: 1, 2: 3, 3: 4, 5: 5, 6: 6, 7: 7, 8: 8}
        t32 = rows_flat(z, 0, 2, 4, P)

        def pairs_of(kind):
            def unit(h, t):
                tok = slice(t * P, t * P + P)
                if kind == "cross":
                    return dict(
                        q=[qT_x[:, 2 * h + d, tok] for d in range(2)], k=[kT_mem[:, 2 * h + d] for d in range(2)],
                        v=[[v_mem[:, b, (2 * h + d) * P:(2 * h + d + 1) * P] for b in range(2)] for d in range(2)],
                        o=[ps[:, h, d * T + t * P:d * T + t * P + P] for d in range(2)],
                        mask=K["none"], scale=-(256 ** -0.5))
                if h < 4:
                    qt, kt_, dim, row, mask, scale = h, 4 + h, 96, 0, K["causal"], -(96 ** -0.5)
                    v0 = 128 + 64 * h
                elif h < 12:
                    g = h - 4
                    qt, kt_, dim, row, mask, scale = 8 + g // 2, 12 + g // 2, 64, 64 * (g % 2), K["dilated"], -0.125
                    v0 = YDV + 64 * g
                else:
                    g = h - 12
                    qt, kt_, dim, row, mask, scale = 16 + g // 2, 18 + g // 2, 64, 64 * (g % 2), dsa_mask, -0.125
                    v0 = YSV + 64 * g
                n = P * (t + 1)
                c = (h // 2) % 2 * T + t * P
                return dict(
                    q=[tT[row:row + dim, qt, tok]], k=[tT[row:row + dim, kt_, 0:n]],
                    v=[[z[:, b, v0:v0 + 64] for b in range(t + 1)]],
                    o=[ps[64 * (h % 2):64 * (h % 2) + 64, h // 4, c:c + P]],
                    mask=mask[:, t, 0:n], scale=scale)

            if kind == "cross":
                heads_of = [(h, h + 1) for h in range(0, 4, 2)]
            else:
                heads_of = [(h + i, h + i + 2) for h in range(0, 16, 4) for i in range(2)]
            return [dict(heads=[unit(h, t) for h in hs], blocks=2 if kind == "cross" else t + 1)
                    for hs in heads_of for t in range(TT)]

        CROSS = pairs_of("cross")
        LAYER = pairs_of("layer")

        def first_pair(l):
            return len(CROSS) + l * len(LAYER)

        def pair_scores(j):
            return ps[:, 4 + j % 2, :].rearrange("p (u n) -> p u n", n=T), ps[:, 6 + j % 2, :].rearrange("p (u n) -> p u n", n=T)

        @block.tensor
        def _(pe):
            ident = K["ident"]

            def mm3(out, a_hi_, a_lo_, b_hi, b_lo, start, stop):
                pe.matmul(out, a_hi_, b_hi, start=start, stop=False)
                pe.matmul(out, a_hi_, b_lo, start=False, stop=False)
                return pe.matmul(out, a_lo_, b_hi, start=False, stop=stop)

            def chunk(c, part):
                pe.wait_ge(lo_done, c * 2 + (part + 1))

            def w(slot, n, cols):
                return (w_hi[:, slot, 0:n].rearrange("p (k c) -> p k c", c=cols),
                        w_lo[:, slot, 0:n].rearrange("p (k c) -> p k c", c=cols))

            def tsplit(k, src, ready):
                for i, q in enumerate(turned(k)):
                    ready(i, q)
                    for j in range(4):
                        ins = pe.transpose(ps[:, 4 + q, j * P:(j + 1) * P], quarter(src, q)[:, j * P:(j + 1) * P], ident)
                    ins.then_inc(t_ps, 1)

            def norm(k):
                tsplit(TSPLIT[k], mem_rows if k == 1 else xn[:],
                       lambda i, q: pe.wait_ge(n_xn, 4 * (k if k < 4 else k - 1) + i + 1))

            def left(k, half):
                pe.wait_ge(t_lo, 4 * k + 2 * (half + 1))

            def columns(c0, n, cols, before, k_left, between=None):
                def one(i, slot=None):
                    slot = i % 2 if slot is None else slot
                    chunk(i + c0, 0)
                    if not isinstance(i, int) or i >= 2:
                        pe.wait_ge(z_out, i + (before - 1))
                    hi, lo = w(slot, 8 * cols, cols)
                    for t in range(TT):
                        if isinstance(i, int) and i == 0:
                            left(k_left, t)
                        for k in range(KT):
                            if t == 0 and k == KT // 2:
                                chunk(i + c0, 1)
                            ins = mm3(ps[:, 2 * slot + t, 0:cols], hT_hi[:, k, t * P:(t + 1) * P],
                                      hT_lo[:, k, t * P:(t + 1) * P], hi[:, k], lo[:, k], k == 0, k == KT - 1)
                            if t == TT - 1 and k in (KT // 2 - 1, KT - 1):
                                ins.then_inc(used, 1)
                one(0)
                one(1)
                if between is None:
                    pairs(pe, 2, n, one)
                    return
                for i in range(2, n):
                    one(i)
                    between(i)

            def square_rows(c0, k_left=None):
                for i in range(4):
                    hi, lo = w(i % 2, 2048, D)
                    for kk in range(2):
                        chunk(c0 + i, kk)
                        k = 2 * i + kk
                        if k_left is not None and k % (KT // 2) == 0:
                            left(k_left, k // (KT // 2))
                        for t in range(TT):
                            for half in range(2):
                                ins = mm3(ps[:, 2 * t + half, :], hT_hi[:, k, t * P:(t + 1) * P],
                                          hT_lo[:, k, t * P:(t + 1) * P], hi[:, kk, half * 512:half * 512 + 512],
                                          lo[:, kk, half * 512:half * 512 + 512], k == 0, k == KT - 1)
                                if k == KT - 1 and (t, half) != (1, 1):
                                    ins.then_inc(bank_done, 1)
                        ins.then_inc(used, 1)

            def column_chunk(c0, i, k_left, bank0=0):
                chunk(c0 + i, 0)
                hi, lo = w(i % 2, 2048, 256)
                for j in range(2):
                    for k in range(KT):
                        if j == 0 and k == KT // 2:
                            chunk(c0 + i, 1)
                        if i == 0 and j == 0 and k % (KT // 2) == 0:
                            left(k_left, k // (KT // 2))
                        a, b = hi[:, k, j * P:(j + 1) * P], lo[:, k, j * P:(j + 1) * P]
                        ins = mm3(ps[:, bank0 + i, j * T:(j + 1) * T], a, b, hT_hi[:, k], hT_lo[:, k], k == 0, k == KT - 1)
                        if j == 1 and k in (KT // 2 - 1, KT - 1):
                            ins.then_inc(used, 1)

            def ffn(c0, n, k_left):
                base = n * NFT

                def up(i, slot):
                    hi, lo = w(slot, 2048, 256)
                    if not isinstance(i, int) or i >= 2:
                        pe.wait_ge(ff_conv, i + (base - 1))
                    for j in range(2):
                        for k in range(KT):
                            if isinstance(i, int) and i == 0 and j == 0 and k % (KT // 2) == 0:
                                left(k_left, k // (KT // 2))
                            a, b = hi[:, k, j * P:(j + 1) * P], lo[:, k, j * P:(j + 1) * P]
                            ins = mm3(ps[:, 4 + slot, j * T:(j + 1) * T], a, b, hT_hi[:, k], hT_lo[:, k],
                                      k == 0, k == KT - 1)
                    ins.then_inc(ff_up, 1)

                def down(i, slot, start):
                    pe.wait_ge(ff_lo, i + (base + 1))
                    a = 1 - slot
                    for t in range(TT):
                        for half in range(2):
                            o = 2048 + half * 512
                            ins = mm3(ps[:, 2 * t + half, :], a_hi[:, a, t * P:(t + 1) * P],
                                      a_lo[:, a, t * P:(t + 1) * P], w_hi[:, slot, o:o + 512],
                                      w_lo[:, slot, o:o + 512], start, False)
                    return ins

                def down_last(half):
                    pe.wait_ge(ff_lo, NFT + base)
                    for t in range(TT):
                        ins = mm3(ps[:, 2 * t + half, :], a_hi[:, 1, t * P:(t + 1) * P], a_lo[:, 1, t * P:(t + 1) * P],
                                  w_hi[:, half, 0:512], w_lo[:, half, 0:512], False, True)
                        if t == 0:
                            ins.then_inc(bank_done, 1)
                    ins.then_inc(used, 2)

                chunk(c0, 1)
                up(0, 0)
                chunk(c0 + 1, 0)
                up(1, 1)
                chunk(c0 + 1, 1)
                down(0, 1, True).then_inc(used, 4)

                def one(i, slot=None):
                    slot = i % 2 if slot is None else slot
                    chunk(i + c0, 0)
                    up(i, slot)
                    chunk(i + c0, 1)
                    down(i - 1, slot, False).then_inc(used, 2)
                pairs(pe, 2, NFT, one)
                for half in range(2):
                    chunk(c0 + NFT + half, 1)
                    down_last(half)

            def attention(j0, us):
                def scores(j, u):
                    if j >= 2:
                        pe.wait_ge(at_max, j - 1)
                    for i, head in enumerate(u["heads"]):
                        for d, (q, k) in enumerate(zip(head["q"], head["k"])):
                            ins = pe.matmul(pair_scores(j)[0][:, i, 0:P * u["blocks"]], q, k, start=d == 0,
                                            stop=d == len(head["q"]) - 1)
                    ins.then_inc(at_s, 1)

                def turn(j, u):
                    pe.wait_ge(at_p, j + 1)
                    if j >= 2:
                        pe.wait_ge(at_ptc, j - 1)
                    for i in range(2):
                        for b in range(u["blocks"]):
                            ins = pe.transpose(pair_scores(j)[1][:, i, b * P:(b + 1) * P],
                                               p_sb[:, j % 3, i, b * P:(b + 1) * P], ident)
                    ins.then_inc(at_pt, 1)

                def values(j, u):
                    pe.wait_ge(at_ptc, j + 1)
                    for i, head in enumerate(u["heads"]):
                        for v, o in zip(head["v"], head["o"]):
                            for b in range(u["blocks"]):
                                ins = pe.matmul(o, v[b], pT[:, j % 2, i, b * P:(b + 1) * P], start=b == 0,
                                                stop=b == u["blocks"] - 1)
                    ins.then_inc(at_o, 1)

                for i in range(len(us) + 3):
                    if i < len(us):
                        scores(j0 + i, us[i])
                    if 2 <= i <= len(us) + 1:
                        turn(j0 + i - 2, us[i - 2])
                    if i >= 3:
                        values(j0 + i - 3, us[i - 3])

            def values_cd(hn):
                t, q = hn // 8, hn % 8
                v = ZV + 256 + q * 64
                if q == 0:
                    pe.wait_ge(m["act_o"], t + 1)
                pe.wait_ge(m["dve_pT"], hn + 1)
                pe.matmul(ps[:, 7, q * 64:q * 64 + 64], pT_sum[:, hn % 2], z[:, t, v:v + 64], start=True,
                          stop=True).then_inc(m["pe_o"], 1)

            pe.wait_ge(ld_c, 32)
            norm(0)
            columns(C_IN, IN_CHUNKS, IN_COLS, 0, 0)
            pe.wait_ge(z_out, IN_CHUNKS)
            pe.wait_ge(ld_tab, 64)

            for t in range(TT):
                for b, tiles in enumerate((range(0, 4), range(4, 8), range(8, 10))):
                    for j, c in enumerate(tiles):
                        ins = pe.transpose(ps[:, 3 * t + b, j * P:(j + 1) * P], z[:, t, c * P:(c + 1) * P], ident)
                    ins.then_inc(m["pe_ztp"], 1)
            for t in range(TT):
                ins = pe.transpose(ps[0:16, 6, t * P:(t + 1) * P], z[:, t, ZLR:ZLR + 16], ident)
            ins.then_inc(m["pe_ztp"], 1)
            pe.wait_ge(m["dve_zcd"], 1)
            for t in range(TT):
                ins = pe.matmul(ps[:, 7, t * P:(t + 1) * P], lrT[0:16, t * P:(t + 1) * P], gkup[:, :], start=True, stop=True)
            ins.then_inc(m["pe_gl"], 1)
            pe.wait_ge(m["act_conv"], 1)
            pe.wait_ge(m["dve_zcd"], 3)
            for t in range(TT):
                for b, tiles in enumerate((range(0, 4), range(4, 6))):
                    for j, c in enumerate(tiles):
                        ins = pe.transpose(ps[:, 2 * t + b, j * P:(j + 1) * P], yB[:, c, t * P:(t + 1) * P], ident)
                    ins.then_inc(m["pe_back"], 1)
            pe.wait_ge(m["act_kd"], 1)
            for t in range(TT):
                for j in range(2):
                    ins = pe.transpose(ps[:, 4, (2 * j + t) * P:(2 * j + t + 1) * P],
                                       z[:, t, ZDF + j * P:ZDF + (j + 1) * P], ident)
            ins.then_inc(m["pe_kdT"], 1)
            pe.wait_ge(m["dve_rope"], 1)
            for side in range(2):
                for j in range(2):
                    for t in range(TT):
                        c = ZRQ + side * 256 + j * P
                        ins = pe.transpose(ps[:, 5 + side, (2 * j + t) * P:(2 * j + t + 1) * P], z[:, t, c:c + P], ident)
                ins.then_inc(m["pe_qkA"], 1)
            pe.wait_ge(m["act_back"], 4)
            pe.wait_ge(m["dve_qkA"], 2)
            for t in range(TT):
                tok = slice(t * P, t * P + P)
                for h in range(4):
                    r = slice(64 * (h % 2), 64 * (h % 2) + 64)
                    c = (2 * t + h // 2) * P
                    ins = pe.matmul(ps[:, h % 2, c:c + P], kTA[r, h // 2, tok], qTA[r, h // 2, tok], start=True, stop=True)
            ins.then_inc(m["pe_scA"], 1)
            for t in range(TT):
                pe.wait_ge(m["dve_pA"], t + 1)
                for h in range(4):
                    ins = pe.matmul(ps[:, 7, t * 256 + h * 64:t * 256 + h * 64 + 64], pTA[:, t, place(h)],
                                    z[:, t, ZV + h * 64:ZV + h * 64 + 64], start=True, stop=True)
                ins.then_inc(m["pe_o"], 1)
            def fade(unit):
                t, g = unit // 3, unit % 3
                if unit:
                    pe.wait_ge(m["act_fade"], unit)
                for j in range(2):
                    ins = pe.matmul(ps[:, j, :], lf[:, t, g * P:(g + 1) * P],
                                    K["sums"][:, 4 * j:4 * j + 4].rearrange("p a b -> p (a b)"), start=True, stop=True)
                ins.then_inc(m["pe_fade"], 1)

            pe.wait_ge(m["dve_pA"], 2)
            fade(0)
            hn = 0
            for unit in range(3 * TT):
                t, g = unit // 3, unit % 3
                tok = slice(t * P, t * P + P)
                pe.wait_ge(m["dve_qk"], unit + 1)
                pe.wait_ge(m["pool_qk"], unit + 1)
                if unit:
                    pe.wait_ge(m["act_kt"], unit)
                pe.transpose(ps[:, 6, 0:P], ktT, ident).then_inc(m["pe_kt"], 1)
                if unit + 1 < 3 * TT:
                    fade(unit + 1)
                heads, dim = (4, 32) if g == 0 else (2, 64)
                for h in range(heads):
                    r = slice(dim * h, dim * h + dim)
                    b = 2 + 2 * (hn % 2)
                    if hn >= 2:
                        pe.wait_ge(m["dve_pT"], hn - 1)
                    qd_, kd_ = (cqkT[:, 0], cqkT[:, 1]) if g == 0 else (dqT[:, g - 1], kdT[:, g - 1])
                    for lev in range(7):
                        lhs = kX[unit % 2][r, lev] if lev < 6 else kd_[r, tok]
                        rhs = qX[unit % 2][r, lev] if lev < 6 else qd_[r, tok]
                        ins = pe.matmul(ps[:, b + lev // 4, (lev % 4) * P:(lev % 4 + 1) * P], lhs, rhs,
                                        start=True, stop=True)
                    ins.then_inc(m["pe_sc"], 1)
                    if hn:
                        values_cd(hn - 1)
                    hn += 1
            values_cd(hn - 1)
            for n in range(NCH - 1):
                t, r = n // 2, slice(64 * (n % 2), 64 * (n % 2) + 64)
                pe.wait_ge(m["act_kt"], 6)
                pe.wait_ge(m["dve_ktA"], 1)
                if n >= 1:
                    pe.wait_ge(m["dve_state"], n)
                for k0, a, wd in ((ZRK, 0, 128), (ZRK + 128, 128, 128), (ZCQ, 256, 256), (ZDF, 512, 128), (ZDF + 128, 640, 128)):
                    ins = pe.matmul(ps[:, a // 512, a % 512:a % 512 + wd], z[r, t, k0:k0 + P],
                                    z[r, t, ZV + a:ZV + a + wd], start=True, stop=True)
                ins.then_inc(m["pe_kv"], 1)
            for n in range(1, NCH):
                t, r = n // 2, slice(64 * (n % 2), 64 * (n % 2) + 64)
                pe.wait_ge(m["dve_state"], n)
                b = 2 if t == 0 else 4
                for g, (a, wd) in enumerate(((0, 128), (128, 128), (256, 256), (512, 128), (640, 128))):
                    ins = pe.matmul(ps[r, b + a // 512, a % 512:a % 512 + wd], qgT[:, g, n * CH:(n + 1) * CH],
                                    states[:, n - 1, a:a + wd], start=True, stop=True)
                ins.then_inc(m["pe_inter"], 1)

            pe.wait_ge(m["dve_inter"], 2)
            pe.wait_ge(m["dve_b"], 1)
            for t in range(TT):
                pe.matmul(ps[:, 6, t * 8:t * 8 + 4], K["sums"][:, 6], g_b[:, t], start=True, stop=True)
                pe.matmul(ps[:, 6, t * 8 + 4:t * 8 + 8], K["sums"][:, 7], g_b[:, t], start=True, stop=True)
                for p in range(2):
                    ins = pe.matmul(ps[:, 6, 16 + p * 4 + t * 2:16 + p * 4 + t * 2 + 2], g_exp[:, t, p * P:(p + 1) * P],
                                    K["chunk_of"], start=True, stop=True)
            ins.then_inc(m["pe_gB"], 1)
            pe.wait_ge(m["dve_natB"], 1)
            for side, src in enumerate((z[:, :, 0:256], z[:, :, 256:512], kb, qg)):
                for p in range(2):
                    for t in range(TT):
                        ins = pe.transpose(ps[:, side, (2 * p + t) * P:(2 * p + t + 1) * P], src[:, t, p * P:(p + 1) * P], ident)
                ins.then_inc(m["pe_tB"], 1)
            pe.wait_ge(m["dve_tB"], 4)
            for t in range(TT):
                tok = slice(t * P, t * P + P)
                pe.wait_ge(m["dve_xB"], t * 13 + 1)
                for h in range(4):
                    ins = pe.matmul(ps[:, 4, h * P:(h + 1) * P], xB[:, h], K["incl"], start=True, stop=True)
                ins.then_inc(m["pe_rB"], 1)
                for i, side in enumerate((kbT, qTB)):
                    for h in range(4):
                        r = slice(64 * (h % 2), 64 * (h % 2) + 64)
                        c = (2 * i + h // 2) * P
                        ins = pe.matmul(ps[:, h % 2, c:c + P], kTB[r, h // 2, tok], side[r, h // 2, tok], start=True, stop=True)
                ins.then_inc(m["pe_kkB"], 1)
                pe.wait_ge(m["dve_xB"], t * 13 + 2)
                for h in range(4):
                    ins = pe.transpose(ps[:, 2, h * P:(h + 1) * P], xBT[:, h], ident)
                ins.then_inc(m["pe_xB"], 1)
                for lev in range(5):
                    for pair in range(2):
                        pe.wait_ge(m["dve_xB"], t * 13 + (3 if lev == 0 else 2 + 2 * lev + pair))
                        for i in range(2):
                            h = 2 * pair + i
                            ins = pe.matmul(ps[:, 3 + 4 * pair, i * P:(i + 1) * P], nmT[:, h], xB[:, h], start=True, stop=True)
                        ins.then_inc(m["pe_yB"], 1)
                    for pair in range(2):
                        pe.wait_ge(m["act_yB"], t * 10 + 2 * lev + pair + 1)
                        for i in range(2):
                            h = 2 * pair + i
                            if lev < 4:
                                pe.matmul(ps[:, pair, i * P:(i + 1) * P], xBT[:, h], yBB[:, h], start=True, stop=True)
                            ins = pe.matmul(ps[:, pair, (2 + i) * P:(3 + i) * P], yBB[:, h], xBT[:, h], start=True, stop=True)
                        ins.then_inc(m["pe_xB"], 1)
                pe.wait_ge(m["dve_xB"], t * 13 + 13)
                if t == 1:
                    pe.wait_ge(m["act_uvB"], 1)
                for h in range(4):
                    r = slice(64 * (h % 2), 64 * (h % 2) + 64)
                    pe.matmul(ps[:, 5, h * 64:h * 64 + 64], xBT[:, place(h)], z[:, t, 512 + h * 64:512 + h * 64 + 64], start=True, stop=True)
                    ins = pe.matmul(ps[r, 6, (h // 2) * P:(h // 2) * P + P], kbg[:, t, h * 64:h * 64 + 64], xBT[:, place(h)],
                                    start=True, stop=True)
                ins.then_inc(m["pe_uvB"], 1)
            pe.wait_ge(m["act_uvB"], 2)
            norm(1)
            for n in range(NCH):
                t, r = n // 2, slice(64 * (n % 2), 64 * (n % 2) + 64)
                tk = slice(n * CH, (n + 1) * CH)
                pe.wait_ge(m["dve_sB"], n + 1)
                for p in range(2):
                    ins = pe.matmul(ps[r, 0, p * P:(p + 1) * P], wT[:, p, tk], stateB[:, p * P:(p + 1) * P], start=True, stop=True)
                ins.then_inc(m["pe_wB"], 1)
                pe.wait_ge(m["dve_uB"], n + 1)
                for h in range(4):
                    v = slice(h * 64, h * 64 + 64)
                    pe.matmul(ps[r, 2 + t, v], qgB[:, h // 2, tk], stateB[:, v], start=True, stop=False)
                    ins = pe.matmul(ps[r, 2 + t, v], pB[r, t, place(h), r], u_nat[r, t, v], start=False, stop=True)
                ins.then_inc(m["pe_oB"], 1)
                if n < NCH - 1:
                    for p in range(2):
                        ins = pe.matmul(ps[:, 1, p * P:(p + 1) * P], kt[r, t, p * P:(p + 1) * P], u_nat[r, t, p * P:(p + 1) * P],
                                        start=True, stop=True)
                    ins.then_inc(m["pe_sB"], 1)
                column_chunk(C_K, n, 1, 4)

            pe.wait_ge(m["act_oB"], 2)
            pe.wait_ge(m["dve_sB"], NCH + 1)
            square_rows(C_V)
            pe.wait_ge(sq_out, 4)
            tsplit(2, xn[:], lambda i, q: pe.wait_ge(m["dve_on"], q // 2 + 1))
            pe.wait_ge(sq_out, 8)
            square_rows(C_OUT, 2)
            norm(2)
            pe.wait_ge(res_out, 4)
            for i in range(4):
                column_chunk(C_Q, i, 3)
            pe.wait_ge(sq_out, 12)
            attention(0, CROSS)
            pe.wait_ge(at_ol, 4)
            square_rows(C_O)
            norm(3)
            pe.wait_ge(res_out, 8)
            ffn(C_FFN, 0, 4)
            for l in range(LAYERS):
                b = C_LAYER + l * LAYER_CHUNKS
                norm(5 + 2 * l)
                pe.wait_ge(res_out, 4 * (4 + 2 * l))
                def latents(i):
                    if i == 3:
                        pe.wait_ge(l_["dve_n"], l + 1)
                        for t in range(TT):
                            for j in range(3):
                                ins = pe.transpose(ps[:, 4 + t, j * P:(j + 1) * P], z[:, t, j * P:(j + 1) * P], ident)
                            ins.then_inc(l_["pe_lat"], 1)
                    if i == 5:
                        pe.wait_ge(ld_lat, 16 * (l + 1))
                        pe.wait_ge(l_["dve_lat"], 2 * (l + 1))
                        for t in range(TT):
                            tok = slice(t * P, t * P + P)
                            for j in range(2):
                                ins = pe.matmul(ps[:, 4 + t, 0:384], latT[:, j, tok], lat_w[:, j * 384:(j + 1) * 384],
                                                start=j == 0, stop=j == 1)
                            ins.then_inc(l_["pe_up"], 1)
                            pe.matmul(ps[:, 6 + t, :], latT[:, 2, tok], lat_w[:, 768:1280], start=True,
                                      stop=True).then_inc(l_["pe_up"], 1)
                columns(b, IN2_CHUNKS, IN2_COLS, IN_CHUNKS + l * IN2_CHUNKS, 5 + 2 * l, latents)
                pe.wait_ge(l_["dve_rope"], l + 1)
                for n in range(12):
                    t, g = n // 6, n % 6
                    if n == 4:
                        pe.wait_ge(z_out, IN_CHUNKS + (l + 1) * IN2_CHUNKS)
                    if n >= 8:
                        q = n - 8
                        pe.wait_ge(l_["act_tT"] if q % 2 == 0 else l_["dve_tT"], 6 * l + q // 2 + 1)
                    for j in range(4):
                        tile = 4 * g + j
                        if tile < 8:
                            src = z[:, t, 3024 + tile * 96:3024 + (tile + 1) * 96]
                        elif tile < 20:
                            src = z[:, t, YDQ + (tile - 8) * P:YDQ + (tile - 7) * P]
                        elif tile < 22:
                            src = z[:, t, YQI + (tile - 20) * P:YQI + (tile - 19) * P]
                        elif tile == 22:
                            src = z[:, t, 0:P]
                        else:
                            continue
                        ins = pe.transpose(ps[0:src.shape[-1], (n + 4) % 8, j * P:(j + 1) * P], src, ident)
                    ins.then_inc(l_["pe_tT"], 1)
                pe.wait_ge(l_["act_tT"], 6 * (l + 1))
                pe.wait_ge(l_["dve_tT"], 6 * (l + 1))
                for t in range(TT):
                    for h in range(8):
                        r = slice(32 * (h % 4), 32 * (h % 4) + 32)
                        ins = pe.matmul(ps[:, 4 * t + h % 4, (h // 4) * T:(h // 4) * T + P * (t + 1)], tT[r, 20 + h // 4, t * P:(t + 1) * P],
                                        tT[r, 22, 0:P * (t + 1)], start=True, stop=True)
                    ins.then_inc(l_["pe_dots"], 1)
                pe.wait_ge(l_["act_relu"], 2 * l + 2)
                attention(first_pair(l), LAYER)
                pe.wait_ge(at_ol, 4 * (l + 2))
                square_rows(b + IN2_CHUNKS)
                norm(6 + 2 * l)
                pe.wait_ge(res_out, 4 * (5 + 2 * l))
                ffn(b + IN2_CHUNKS + 4, l + 1, 6 + 2 * l)

        def section(eng, c0, n, first, last, split, epilogue, later=1, between=None):
            def one(i, slot=None):
                slot = i % 2 if slot is None else slot
                if isinstance(i, int):
                    if i < n - later:
                        split(c0 + i + 2, slot, chunk_size(c0 + i + 2))
                else:
                    split(i + (c0 + 2), slot, chunk_size(c0 + first + 2))
                epilogue(i, slot)
            for i in range(first):
                one(i)
            pairs(eng, first, last, one)
            for i in range(last, n):
                one(i)
                if between:
                    between(i)

        @block.scalar
        def _(act):
            s = Steps(act, a_step)

            def split(c, slot, size):
                for part in range(2):
                    split_part(c, slot, size, part)

            def split_part(c, slot, size, part, up=None):
                if part == 0:
                    act.wait_ge(landed[slot], c * 8 + (16 - 8 * slot))
                if up is not None:
                    act.wait_ge(ff_up, up)
                elif not isinstance(c, int):
                    act.wait_ge(used, c * 2 - (3 - part))
                elif c >= 2:
                    fits = part == 0 and cut(size) <= cut(chunk_size(c - 2))
                    act.wait_ge(used, c * 2 - (3 if fits else 2))
                a, b = (0, cut(size)) if part == 0 else (cut(size), size)
                act.activation(w_hi[:, slot, a:b], raw[:, slot, a:b], ACT.Copy).then_inc(hi_done, 1)

            def split_now(c):
                split(c, c % 2, chunk_size(c))

            def norm(k):
                for i, q in enumerate(added(k)):
                    residual_ready(act, k, i)
                    if k < 2 and i >= 2:
                        s.fence()
                    s(act.activation(rows_flat(z, 768 + 512 * (i % 2) if k < 2 else 1024 + 512 * i, 512), quarter(sources(k), q), ACT.Square,
                                     accum_out=stat[:, SS + 4 * (k % 2) + q:SS + 4 * (k % 2) + q + 1]), n_ss)

            def tsplit(k, between=None):
                for i, q in enumerate(turned(k)):
                    if between:
                        between(i)
                    t, half = q // 2, q % 2
                    act.wait_ge(t_32, 4 * k + i + 1)
                    s(act.activation(hT_hi[:, 4 * half:4 * half + 4, t * P:(t + 1) * P], t32[:, i % 2], ACT.Copy), t_hi)

            def first_parts(b):
                return lambda i: split_part(b, b % 2, chunk_size(b), i // 2) if i % 2 == 0 else None

            def columns(c0, n, cols, between=None):
                def out(i, slot):
                    act.wait_ge(used, i * 2 + 2 * (c0 + 1))
                    for t in range(TT):
                        ins = act.activation(z[:, t, bass.ds(i * cols, cols)], ps[:, 2 * slot + t, 0:cols], ACT.Copy)
                    ins.then_inc(z_out, 1)
                section(act, c0, n, 0, 0 if between else n - 2, split, out, between=between)

            def residual(c0):
                section(act, c0, 4, 0, 0, split, lambda i, slot: None)

            def square_columns(c0, dst, bank0=0):
                def out(i, slot):
                    act.wait_ge(used, 2 * (c0 + i + 1))
                    s(act.activation(dst[:, 2 * i:2 * i + 2], ps[:, bank0 + i].rearrange("p (a b) -> p a b", b=T), ACT.Copy), sq_out)
                section(act, c0, 4, 0, 0, split, out)

            def square_rows(c0, dst):
                residual(c0)
                act.wait_ge(used, 2 * (c0 + 4))
                for q in range(4):
                    s(act.activation(dst[:, q // 2, q % 2 * 512:q % 2 * 512 + 512], ps[:, q], ACT.Copy), sq_out)

            def ffn(c0, n):
                base = n * NFT

                def one(i, slot=None):
                    slot = i % 2 if slot is None else slot
                    size, c = (chunk_size(c0 + i + 2), c0 + i + 2) if isinstance(i, int) else (3072, i + (c0 + 2))
                    act.wait_ge(ff_up, i + (base + 1))
                    if not isinstance(i, int) or i >= 2:
                        act.wait_ge(ff_act, i + (base - 1))
                    for g, dst in enumerate((conv_g, conv_v)):
                        wc = ptab["ffn_conv"][0] + n * NFT * 6 + 3 * g + 2
                        bc_ = ptab["ffn_bias"][0] + n * NFT * 2 + g
                        ins = act.activation(dst[:, slot], ps[:, 4 + slot, g * T:(g + 1) * T], ACT.Identity,
                                             bias=params[:, bass.ds(i * 2 + bc_, 1)], scale=params[:, bass.ds(i * 6 + wc, 1)])
                    ins.then_inc(ff_tap, 1)
                    split_part(c, slot, size, 0, i + (base + 1) if size == 3072 else None)
                    act.wait_ge(ff_conv, i + (base + 1))
                    act.activation(gated[:, slot], conv_g[:, slot], ACT.Silu).then_inc(ff_silu, 1)
                    split_part(c, slot, size, 1, base + 1 if isinstance(i, int) and i == 0 else None)
                    act.wait_ge(ff_act, i + (base + 1))
                    if not isinstance(i, int) or i >= 1:
                        act.wait_ge(used, i * 2 + 2 * c0)
                    act.activation(a_hi[:, slot], act32[:, slot], ACT.Copy).then_inc(ff_hi, 1)
                one(0)
                one(1)
                pairs(act, 2, 20, one)
                for i in range(20, NFT):
                    one(i)

            def attention(j0, us):
                for i in range(len(us) + 2):
                    if i < len(us):
                        j, n = j0 + i, P * us[i]["blocks"]
                        act.wait_ge(at_max, j + 1)
                        for h in range(2):
                            ins = act.activation(p_sb[:, j % 3, h, 0:n], p_sb[:, j % 3, h, 0:n], ACT.Exp, scale=-1.0,
                                                 bias=ast[:, j % 3, 0, h:h + 1], accum_out=ast[:, j % 3, 1, h:h + 1])
                        s(ins, at_exp)
                    if i >= 2:
                        j, n = j0 + i - 2, P * us[i - 2]["blocks"]
                        act.wait_ge(at_pt, j + 1)
                        if j >= 2:
                            act.wait_ge(at_o, j - 1)
                        s(act.activation(pT[:, j % 2, :, 0:n], pair_scores(j)[1][:, :, 0:n], ACT.Copy), at_ptc)
                act.wait_ge(at_o, j0 + len(us))
                for q in range(4):
                    s(act.activation(hT_hi[:, 2 * q:2 * q + 2], ps[:, q].rearrange("p (a b) -> p a b", b=T), ACT.Copy), at_oh)

            norm(0)
            tsplit(0, first_parts(0))
            split_now(1)
            columns(C_IN, IN_CHUNKS, IN_COLS)

            act.wait_ge(m["pool_init"], 1)
            for t in range(TT):
                for b, (lo, hi) in enumerate(((0, 4), (4, 6))):
                    act.wait_ge(m["pe_ztp"], 3 * t + b + 1)
                    s(act.activation(zTb[:, lo:hi, 3 + t * P:3 + (t + 1) * P],
                                     ps[:, 3 * t + b, 0:(hi - lo) * P].rearrange("p (a b) -> p a b", b=P), ACT.Copy), m["act_zB"])
            for t in range(TT):
                s(act.activation(z[:, t, ZG:ZG + D], z[:, t, ZG:ZG + D], ACT.Silu), m["act_gate"])
            split_now(C_K + 1)
            act.wait_ge(m["dve_ang"], 1)
            for i in range(2):
                ins = act.activation(trig[:, 1 + i], trig[:, 1 + i], ACT.Sin)
            s(ins, m["act_ang"])
            act.wait_ge(m["dve_conv"], 1)
            s(act.activation(yB[:, :, :], yB[:, :, :], ACT.Silu), m["act_conv"])
            for t in range(TT):
                for b, (lo, hi) in enumerate(((0, 4), (4, 6))):
                    act.wait_ge(m["pe_back"], 2 * t + b + 1)
                    s(act.activation(z[:, t, lo * P:hi * P], ps[:, 2 * t + b, 0:(hi - lo) * P], ACT.Copy), m["act_back"])
            act.wait_ge(m["dve_ll"], 1)
            s(act.activation(ll, ll, ACT.Exp, scale=-1.0))
            s.fence()
            s(act.activation(ll, ll, ACT.Ln, bias=1.0))
            s(act.activation(ea, R["a_log"], ACT.Exp), m["act_ll"])
            act.wait_ge(m["dve_kd"], 1)
            s(act.activation(beta, beta, ACT.Exp))
            s(act.activation(z[:, :, ZDF:ZDF + 256], z[:, :, ZDF:ZDF + 256], ACT.Exp, scale=-1.0), m["act_kd"])
            act.wait_ge(m["pe_o"], 2)
            act.wait_ge(m["dve_rope"], 1)
            s(act.activation(xn[:, :, 0:256], ps[:, 7, :].rearrange("p (a b) -> p a b", b=256), ACT.Copy), m["act_o"])
            for unit in range(3 * TT):
                t, g = unit // 3, unit % 3
                act.wait_ge(m["pe_fade"], unit + 1)
                if unit:
                    act.wait_ge(m["dve_qk"], unit)
                    act.wait_ge(m["pool_qk"], unit)
                s(act.activation(fades, ps[:, 0:2].rearrange("p a (b c) -> p (a b) c", c=P), ACT.Exp), m["act_fade"])
                act.wait_ge(m["pe_kt"], unit + 1)
                c = ZCQ if g == 0 else ZDF + (g - 1) * P
                s(act.activation(z[:, t, c:c + P], ps[:, 6, 0:P], ACT.Copy), m["act_kt"])
                if unit in (3, 5):
                    tile = unit // 4
                    act.wait_ge(m["pe_o"], 2 + 8 * (tile + 1))
                    s(act.activation(xn[:, tile, 512:1024], ps[:, 7, :], ACT.Copy), m["act_o"])
            act.wait_ge(m["dve_inter"], 2)
            s(act.activation(squares, z[:, :, 0:512], ACT.Square), m["act_sqB"])
            act.wait_ge(m["pe_gB"], 1)
            act.activation(natB_flat, ps[:, 6, 0:16], ACT.Exp)
            s(act.activation(decB_flat, ps[:, 6, 16:24], ACT.Exp), m["act_gB"])
            norm(1)
            for t in range(TT):
                act.wait_ge(m["pe_rB"], t + 1)
                if t == 1:
                    act.wait_ge(m["dve_xB"], 14)
                s(act.activation(ratio_i, ps[:, 4, :].rearrange("p (a b) -> p a b", b=P), ACT.Exp), m["act_rB"])
                for lev in range(5):
                    for pair in range(2):
                        act.wait_ge(m["pe_yB"], t * 10 + 2 * lev + pair + 1)
                        s(act.activation(yBB[:, 2 * pair:2 * pair + 2],
                                         ps[:, 3 + 4 * pair, 0:2 * P].rearrange("p (a b) -> p a b", b=P), ACT.Copy), m["act_yB"])
                act.wait_ge(m["pe_uvB"], t + 1)
                act.activation(uv[:, t], ps[:, 5, 0:256], ACT.Copy)
                s(act.activation(wT[:, :, t * P:(t + 1) * P], ps[:, 6, 0:256].rearrange("p (a b) -> p a b", b=P), ACT.Copy), m["act_uvB"])
            tsplit(1)
            square_columns(C_K, kT_mem, 4)
            for t in range(TT):
                act.wait_ge(m["pe_oB"], 2 * t + 2)
                s(act.activation(xn[:, t, 256:512], ps[:, 2 + t, 0:256], ACT.Copy), m["act_oB"])
            act.wait_ge(m["dve_sB"], NCH + 1)
            s.fence()
            s(act.activation(area(4096, TT, D), xn[:, :, :], ACT.Square), m["act_osq"])
            split_now(C_V + 1)
            square_rows(C_V, v_mem)
            tsplit(2)
            split_now(C_OUT + 1)
            residual(C_OUT)
            norm(2)
            tsplit(3)
            split_now(C_Q + 1)
            square_columns(C_Q, qT_x)
            attention(0, CROSS)
            split_now(C_O + 1)
            residual(C_O)
            norm(3)
            tsplit(4)
            split_now(C_FFN + 1)
            ffn(C_FFN, 0)
            norm(4)
            for l in range(LAYERS):
                b = C_LAYER + l * LAYER_CHUNKS
                norm(5 + 2 * l)
                tsplit(5 + 2 * l, first_parts(b))
                split_now(b + 1)
                def latents(i):
                    if i == 2:
                        act.wait_ge(z_out, IN_CHUNKS + l * IN2_CHUNKS + 2)
                        for t in range(TT):
                            for j, (c, n) in enumerate(((YCQ, 256), (YKV, 128))):
                                s(act.activation(area(0, 8, T)[:, 2 * t + j, 0:n], z[:, t, c:c + n], ACT.Square,
                                                 accum_out=lstat[:, 2 * t + j:2 * t + j + 1]), l_["act_ss"])
                    if i == 5:
                        for t in range(TT):
                            act.wait_ge(l_["pe_up"], 4 * l + 2 * t + 2)
                            act.activation(z[:, t, 3024:3408], ps[:, 4 + t, 0:384], ACT.Copy)
                            kv = ps[:, 6 + t, :].rearrange("p (h c) -> p h c", c=P)
                            act.activation(z[:, t, 3408:3792].rearrange("p (h c) -> p h c", c=96)[:, :, 0:64], kv[:, :, 0:64], ACT.Copy)
                            s(act.activation(z[:, t, 128:384].rearrange("p (h c) -> p h c", c=64), kv[:, :, 64:128], ACT.Copy), l_["act_up"])
                columns(b, IN2_CHUNKS, IN2_COLS, latents)
                for n in range(0, 12, 2):
                    t, g = n // 6, n % 6
                    act.wait_ge(l_["pe_tT"], 12 * l + n + 1)
                    r = 96 if g < 2 else P
                    s(act.activation(tT[0:r, 4 * g:4 * g + 4, t * P:(t + 1) * P],
                                     ps[0:r, (n + 4) % 8, :].rearrange("p (a b) -> p a b", b=P), ACT.Copy), l_["act_tT"])
                for t in range(TT):
                    act.wait_ge(l_["pe_dots"], 2 * l + t + 1)
                    dots = ps[:, 4 * t:4 * t + 4].rearrange("p a (b c) -> p (a b) c", c=T)
                    s(act.activation(relus[t], dots[:, :, 0:P * (t + 1)], ACT.Relu), l_["act_relu"])
                attention(first_pair(l), LAYER)
                split_now(b + IN2_CHUNKS + 1)
                residual(b + IN2_CHUNKS)
                norm(6 + 2 * l)
                tsplit(6 + 2 * l)
                split_now(b + IN2_CHUNKS + 5)
                ffn(b + IN2_CHUNKS + 4, l + 1)
            norm(9)

        @block.gpsimd
        def _(pool):
            s = Steps(pool, g_step)
            ring = zTb[:, :, 0:3]

            def power(out, in_, n, signal):
                s(pool.tensor_tensor(out, in_, K["neg_half"][:, 0:n], ALU.pow), signal)

            def norm(k):
                pool.wait_ge(n_ms, k + 1)
                power(stat[:, RS + 2 * k:RS + 2 * k + 2], stat[:, MS + 2 * k:MS + 2 * k + 2], 2, n_rs)

            s(pool.memset(ring, 0.0), m["pool_init"])
            pool.wait_ge(ld_c, 32)
            norm(0)
            pool.wait_ge(m["pe_o"], 2)
            pool.wait_ge(m["dve_pA"], 2)
            for unit in range(3 * TT):
                t, g = unit // 3, unit % 3
                tok = slice(t * P, (t + 1) * P)
                q_, k_ = (cqkT[:, 0, tok], cqkT[:, 1, tok]) if g == 0 else (dqT[:, g - 1, tok], kdT[:, g - 1, tok])
                pool.wait_ge(m["act_fade"], unit + 1)
                if unit:
                    pool.wait_ge(m["pe_kt"], unit)
                if unit >= 2:
                    pool.wait_ge(m["pe_sc"], (0, 0, 4, 6, 8, 12)[unit])
                s(pool.tensor_tensor(ktT, k_, fades[:, 7], ALU.mult))
                s(pool.tensor_tensor(qX[unit % 2], fades[:, 0:6], bc(q_.unsqueeze(1), 6, P), ALU.mult))
                s(pool.tensor_tensor(qgT[:, 2 + g, tok], q_, fades[:, 6], ALU.mult))
                s(pool.tensor_copy(cdecay[:, 2 + g, 2 * t:2 * t + 2], fades[:, 6, CH - 1:P:CH]), m["pool_qk"])
            pool.wait_ge(m["dve_inter"], 2)
            pool.dma_start(mem_rows, mem_d).then_inc(ld_mem, 16)
            pool.wait_ge(m["dve_b"], 1)
            power(hstat[:, 16:32], hstat[:, 0:16], 16, m["pool_rsB"])
            norm(1)
            pool.wait_ge(m["dve_onorm"], 1)
            for t in range(TT):
                power(hstat[:, 32 + 16 * t:48 + 16 * t], hstat[:, 64 + 16 * t:80 + 16 * t], 16, m["pool_ors"])
            norm(2)
            pool.wait_ge(at_ol, 4)
            pool.dma_start(area(2048, D), gfinal_d[0].partition_broadcast(P)).then_inc(ld_fin, 16)
            norm(3)
            norm(4)
            for l in range(LAYERS):
                if l:
                    pool.wait_ge(l_["pe_up"], 4 * l)
                pool.dma_start(lat_w[:], lat_d[l]).then_inc(ld_lat, 16)
                norm(5 + 2 * l)
                pool.wait_ge(l_["dve_ms"], l + 1)
                power(lstat[:, 8:12], lstat[:, 4:8], 4, l_["pool_rs"])
                norm(6 + 2 * l)
            pool.wait_ge(res_out, 28)
            pool.dma_start(area(2048, D), gfinal_d[1].partition_broadcast(P)).then_inc(ld_fin, 16)
            norm(9)
            for t in range(TT):
                pool.wait_ge(m["dve_out"], 2 * t + 2)
                pool.dma_start(out_d[:, t], xn[:, t]).then_inc(stored, 16)
            pool.wait_ge(stored, 32)

        @block.vector
        def _(dve):
            s = Steps(dve, v_step)

            def split(c, slot, size):
                for part in range(2):
                    split_part(c, slot, size, part)

            def split_part(c, slot, size, part):
                dve.wait_ge(hi_done, c * 2 + (part + 1))
                a, b = (0, cut(size)) if part == 0 else (cut(size), size)
                dve.tensor_tensor(w_lo[:, slot, a:b], raw[:, slot, a:b], w_hi[:, slot, a:b].bitcast(F32),
                                  ALU.subtract).then_inc(lo_done, 1)

            def split_now(c):
                split(c, c % 2, chunk_size(c))

            def norm(k, dst=None, gain=None, signal=None):
                sums_of_squares, ms = stat[:, SS + 4 * (k % 2):SS + 4 * (k % 2) + 4], stat[:, MS + 2 * k:MS + 2 * k + 2]
                dve.wait_ge(n_ss, 4 * k + 4)
                s(dve.tensor_reduce(ms, shaped(sums_of_squares, (TT, 2)), AX_X, ALU.add), n_sum)
                s.fence()
                s(dve.tensor_scalar(ms, ms, 1.0 / D, EPS, ALU.mult, ALU.add), n_ms)
                dve.wait_ge(n_rs, k + 1)
                if gain is not None:
                    dve.wait_ge(ld_fin, 16 if k == 4 else 32)
                    for q in range(4):
                        t, c = q // 2, slice(q % 2 * 512, q % 2 * 512 + 512)
                        s(dve.scalar_tensor_tensor(out=dst[:, t, c], in0=res[:, t, c], scalar=stat[:, RS + 2 * k + t:RS + 2 * k + t + 1],
                                                   in1=gain[:, c], op0=ALU.mult, op1=ALU.mult), signal)
                    return
                dst = mem_rows if k == 1 else xn[:]
                for q in turned(TSPLIT[k]):
                    t = q // 2
                    s(dve.tensor_scalar(quarter(dst, q), quarter(sources(k), q), stat[:, RS + 2 * k + t:RS + 2 * k + t + 1], None,
                                        ALU.mult), n_xn)

            def tsplit(k, gain, between=None):
                for pair in range(2):
                    two = [(i, turned(k)[i]) for i in (2 * pair, 2 * pair + 1)]
                    if between:
                        between(2 * pair)
                    if pair:
                        dve.wait_ge(t_lo, 4 * k + 2)
                    for i, q in two:
                        half = q % 2
                        dve.wait_ge(t_ps, 4 * k + i + 1)
                        src = ps[:, 4 + q, :].rearrange("p (a b) -> p a b", b=P)
                        if gain is None:
                            s(dve.tensor_copy(t32[:, i % 2], src), t_32)
                        else:
                            g = G["gains"][:, gain, 4 * half:4 * half + 4].unsqueeze(2)
                            s(dve.tensor_tensor(t32[:, i % 2], src, bc(g, 4, P), ALU.mult), t_32)
                    for i, q in two:
                        t, half = q // 2, q % 2
                        dve.wait_ge(t_hi, 4 * k + i + 1)
                        dve.wait_ge(t_32, 4 * k + i + 1)
                        dst = (slice(None), slice(4 * half, 4 * half + 4), slice(t * P, (t + 1) * P))
                        s(dve.tensor_tensor(hT_lo[dst], t32[:, i % 2], hT_hi[dst].bitcast(F32), ALU.subtract), t_lo)

            def first_parts(b):
                return lambda i: split_part(b, b % 2, chunk_size(b), i // 2)

            def splits_only(c0, n, loop_to=0):
                section(dve, c0, n, 0, loop_to, split, lambda i, slot: None)

            def residual(c0, done):
                splits_only(c0, 4)
                add_residual([(bank_done, done + 1), (bank_done, done + 2), (bank_done, done + 3), (used, 2 * (c0 + 4))],
                             TOKENS_FIRST)

            def add_residual(finished, order):
                for (signal, count), q in zip(finished, order):
                    dve.wait_ge(signal, count)
                    s(dve.tensor_tensor(quarter(res, q), ps[:, q], quarter(res, q), ALU.add), res_out)

            def ffn(c0, n, done):
                base = n * NFT

                def one(i, slot=None):
                    slot = i % 2 if slot is None else slot
                    size, c = (chunk_size(c0 + i + 2), c0 + i + 2) if isinstance(i, int) else (3072, i + (c0 + 2))
                    u = [ps[:, 4 + slot, g * T:(g + 1) * T] for g in range(2)]
                    y = [conv_g[:, slot], conv_v[:, slot]]
                    wc = ptab["ffn_conv"][0] + n * NFT * 6
                    dve.wait_ge(ff_tap, i + (base + 1))
                    for g in range(2):
                        ins = dve.scalar_tensor_tensor(out=y[g][:, 1:T], in0=u[g][:, 0:T - 1],
                                                       scalar=params[:, bass.ds(i * 6 + (wc + 3 * g + 1), 1)],
                                                       in1=y[g][:, 1:T], op0=ALU.mult, op1=ALU.add)
                    ins.then_inc(ff_c1, 1)
                    dve.wait_ge(ff_c1, i + (base + 1))
                    for g in range(2):
                        ins = dve.scalar_tensor_tensor(out=y[g][:, 2:T], in0=u[g][:, 0:T - 2],
                                                       scalar=params[:, bass.ds(i * 6 + (wc + 3 * g), 1)],
                                                       in1=y[g][:, 2:T], op0=ALU.mult, op1=ALU.add)
                    ins.then_inc(ff_conv, 1)
                    split_part(c, slot, size, 0)
                    dve.wait_ge(ff_silu, i + (base + 1))
                    if not isinstance(i, int) or i >= 2:
                        dve.wait_ge(ff_lo, i + (base - 1))
                    dve.wait_ge(ff_conv, i + (base + 1))
                    dve.tensor_tensor(act32[:, slot], gated[:, slot], y[1], ALU.mult).then_inc(ff_act, 1)
                    split_part(c, slot, size, 1)
                    dve.wait_ge(ff_hi, i + (base + 1))
                    dve.tensor_tensor(a_lo[:, slot], act32[:, slot], a_hi[:, slot].bitcast(F32), ALU.subtract).then_inc(ff_lo, 1)
                one(0)
                one(1)
                pairs(dve, 2, 20, one)
                for i in range(20, NFT):
                    one(i)
                add_residual([(bank_done, done + 1), (used, 2 * (c0 + NFT + 1)), (bank_done, done + 2), (used, 2 * (c0 + NFC))],
                             HALVES_FIRST)

            def attention(j0, us, between=None):
                for i in range(len(us) + 1):
                    if i < len(us):
                        j, u = j0 + i, us[i]
                        n = P * u["blocks"]
                        dve.wait_ge(at_s, j + 1)
                        if j >= 3:
                            dve.wait_ge(at_pt, j - 2)
                        for h, head in enumerate(u["heads"]):
                            ins = dve.tensor_tensor_reduce(p_sb[:, j % 3, h, 0:n], pair_scores(j)[0][:, h, 0:n], head["mask"],
                                                           head["scale"], 3.0e38, ALU.add, ALU.min, ast[:, j % 3, 0, h:h + 1])
                        s(ins, at_max)
                    if i >= 1:
                        j, u = j0 + i - 1, us[i - 1]
                        n = P * u["blocks"]
                        dve.wait_ge(at_exp, j + 1)
                        s(dve.reciprocal(ast[:, j % 3, 2], ast[:, j % 3, 1]))
                        s.fence()
                        s(dve.tensor_tensor(p_sb[:, j % 3, :, 0:n], p_sb[:, j % 3, :, 0:n],
                                            bc(ast[:, j % 3, 2].unsqueeze(2), 2, n), ALU.mult), at_p)
                    if between:
                        between(i)

            def oT_low(a):
                for q in range(4):
                    dve.wait_ge(at_oh, a + q + 1)
                    s(dve.tensor_tensor(hT_lo[:, 2 * q:2 * q + 2], ps[:, q].rearrange("p (a b) -> p a b", b=T),
                                        hT_hi[:, 2 * q:2 * q + 2].bitcast(F32), ALU.subtract), at_ol)

            def rotate(x1, x2, cos, sin, tmp, signal=None):
                s(dve.tensor_tensor(tmp[0], x1, cos, ALU.mult))
                s(dve.tensor_tensor(tmp[1], x2, sin, ALU.mult))
                s(dve.tensor_tensor(tmp[2], x2, cos, ALU.mult))
                s(dve.tensor_tensor(tmp[3], x1, sin, ALU.mult))
                s.fence()
                s(dve.tensor_tensor(x1, tmp[0], tmp[1], ALU.subtract))
                s(dve.tensor_tensor(x2, tmp[2], tmp[3], ALU.add), signal)

            def even_odd(first):
                return ps[:, 0:2, first * P:(first + 2) * P].rearrange("p a (b c) -> p a b c", c=P)

            dve.wait_ge(ld_c, 32)
            norm(0)
            tsplit(0, 0, first_parts(0))
            split_now(1)
            splits_only(C_IN, IN_CHUNKS, IN_CHUNKS - 2)
            dve.wait_ge(ld_tab, 64)

            s(dve.tensor_copy(posf[:, 0:TT], pos_i[:]))
            s.fence()
            for t in range(TT):
                ins = dve.tensor_scalar(trig[:, 0, t], K["freq"], posf[:, t:t + 1], None, ALU.mult)
            s(ins)
            s.fence()
            turn, a, b, c = 2 * np.pi, 6.28125, 0.0019350051879882812, 3.0199159e-07
            s(dve.tensor_scalar(trig[:, 3], trig[:, 0], 1 / turn, 12582912.0, ALU.mult, ALU.add))
            s.fence()
            s(dve.tensor_scalar(trig[:, 3], trig[:, 3], 12582912.0, None, ALU.subtract))
            for part in (a, b, c):
                s.fence()
                s(dve.scalar_tensor_tensor(out=trig[:, 0], in0=trig[:, 3], scalar=-part, in1=trig[:, 0], op0=ALU.mult, op1=ALU.add))
            s.fence()
            s(dve.tensor_scalar(trig[:, 2], trig[:, 0], float(np.float32(3.1415925)), -float(np.float32(3.1415925)), ALU.min, ALU.max))
            s(dve.scalar_tensor_tensor(out=trig[:, 1], in0=trig[:, 0], scalar=-1.0, in1=trig[:, 0], op0=ALU.mult, op1=ALU.min))
            s.fence()
            s(dve.tensor_scalar(trig[:, 1], trig[:, 1], float(np.pi / 2), None, ALU.add), m["dve_ang"])

            dve.wait_ge(m["pe_ztp"], 7)
            s(dve.tensor_copy(lrT[0:16, :], ps[0:16, 6, 0:T]), m["dve_zcd"])
            for t in range(TT):
                tok = slice(t * P, (t + 1) * P)
                dve.wait_ge(m["act_zB"], 2 * t + 2)
                s(dve.tensor_scalar(cqkT[:, 0, tok], ps[:, 3 * t + 1, 256:384], 32 ** -0.5, None, ALU.mult))
                s(dve.tensor_copy(cqkT[:, 1, tok], ps[:, 3 * t + 1, 384:512]))
                s(dve.tensor_copy(dqT[:, :, tok], ps[:, 3 * t + 2, 0:256].rearrange("p (a b) -> p a b", b=P)), m["dve_zcd"])
            dve.wait_ge(m["act_zB"], 4)
            for j in range(4):
                for ct in range(6):
                    wgt = G["gdn_conv"][:, ct, j:j + 1]
                    if j == 0:
                        ins = dve.tensor_scalar(yB[:, ct], zTb[:, ct, 0:T], wgt, None, ALU.mult)
                    else:
                        ins = dve.scalar_tensor_tensor(out=yB[:, ct], in0=zTb[:, ct, j:j + T], scalar=wgt, in1=yB[:, ct],
                                                       op0=ALU.mult, op1=ALU.add)
                s(ins, m["dve_conv"] if j == 3 else None)
                if j < 3:
                    s.fence()
            split_now(C_K + 1)
            s(dve.tensor_copy(xl[:, :, 128:384], z[:, :, ZDF:ZDF + 256]))
            s(dve.tensor_tensor(xl[:, :, 384:388], z[:, :, ZBA:ZBA + 4], bc(R["dt_bias"].unsqueeze(1), TT, 4), ALU.add))
            s(dve.tensor_copy(xl[:, :, 388:392], z[:, :, ZBA + 4:ZBA + 8]))
            dve.wait_ge(m["pe_gl"], 1)
            s(dve.tensor_tensor(xl[:, :, 0:128], ps[:, 7, 0:256].rearrange("p (a b) -> p a b", b=P),
                                bc(R["gk_bias"].unsqueeze(1), TT, P), ALU.add))
            s.fence()
            s(dve.scalar_tensor_tensor(out=ll, in0=xl, scalar=-1.0, in1=xl, op0=ALU.mult, op1=ALU.max), m["dve_ll"])
            dve.wait_ge(m["act_ang"], 1)
            for t in range(TT):
                qk = z[:, t, ZRQ:ZRQ + 512].rearrange("p (h c) -> p h c", c=64)
                cos, sin = (bc(trig[:, 1 + i, t].unsqueeze(1), 8, 32) for i in range(2))
                if t:
                    s.fence()
                rotate(qk[:, :, 0:32], qk[:, :, 32:64], cos, sin,
                       [ropes[:, i].rearrange("p (h c) -> p h c", c=32) for i in range(4)], m["dve_rope"] if t else None)
            dve.wait_ge(m["act_ll"], 1)
            s(dve.scalar_tensor_tensor(out=lf, in0=xl[:, :, 0:384], scalar=0.0, in1=ll[:, :, 0:384], op0=ALU.min, op1=ALU.subtract))
            s(dve.scalar_tensor_tensor(out=z[:, :, ZDF:ZDF + 256], in0=xl[:, :, 128:384], scalar=0.0, in1=ll[:, :, 128:384],
                                       op0=ALU.max, op1=ALU.add))
            s(dve.scalar_tensor_tensor(out=g_b, in0=xl[:, :, 384:388], scalar=0.0, in1=ll[:, :, 384:388], op0=ALU.max, op1=ALU.add))
            s(dve.scalar_tensor_tensor(out=beta, in0=xl[:, :, 388:392], scalar=0.0, in1=ll[:, :, 388:392], op0=ALU.min,
                                       op1=ALU.subtract), m["dve_kd"])
            s.fence()
            s(dve.tensor_scalar(lf[:, :, 0:128], lf[:, :, 0:128], 1.0 / 16, None, ALU.mult))
            s(dve.scalar_tensor_tensor(out=g_b, in0=g_b, scalar=-1.0, in1=bc(ea.unsqueeze(1), TT, 4), op0=ALU.mult, op1=ALU.mult))
            dve.wait_ge(m["pe_kdT"], 1)
            s(dve.tensor_copy(kdT, ps[:, 4, :].rearrange("p (a b) -> p a b", b=T)), m["dve_kdT"])
            for side, dst in enumerate((qTA, kTA)):
                dve.wait_ge(m["pe_qkA"], side + 1)
                s(dve.tensor_copy(dst, ps[:, 5 + side, :].rearrange("p (a b) -> p a b", b=T)), m["dve_qkA"])
            s.fence()
            for t in range(TT):
                s(dve.tensor_tensor(qgT[:, 0:2, t * P:(t + 1) * P], qTA[:, :, t * P:(t + 1) * P], K["ret_qdecay"], ALU.mult))
            for t in range(TT):
                keys = z[:, t, ZRK:ZRK + 256].rearrange("p (h c) -> p h c", c=64)
                s(dve.tensor_tensor(keys, keys, bc(K["ret_ktail"].unsqueeze(2), 4, 64), ALU.mult), m["dve_ktA"] if t else None)
            for t in range(TT):
                dve.wait_ge(m["pe_scA"], 1)
                s(dve.tensor_tensor(pTA[:, t].rearrange("p (a b) c -> p a b c", b=2), even_odd(2 * t),
                                    K["ret_decay"].rearrange("p (a b) c -> p a b c", b=2), ALU.mult), m["dve_pA"])
            for t in range(TT):
                dve.wait_ge(m["act_gate"], t + 1)
                gate = z[:, t, ZG + 256:ZG + D].rearrange("p (a h c) -> p a h c", a=3, c=64)
                s(dve.tensor_tensor(gate, gate, bc(R["head_gains"].unsqueeze(2), 3, 4, 64), ALU.mult), m["dve_gate"])
            def faded(unit):
                t, g = unit // 3, unit % 3
                tok = slice(t * P, (t + 1) * P)
                k_ = cqkT[:, 1, tok] if g == 0 else kdT[:, g - 1, tok]
                dve.wait_ge(m["act_fade"], unit + 1)
                s(dve.tensor_tensor(kX[unit % 2], fades[:, 0:6], bc(k_.unsqueeze(1), 6, P), ALU.mult), m["dve_qk"])

            dve.wait_ge(m["pe_o"], 2)
            s.fence()
            faded(0)
            hn = 0
            for unit in range(3 * TT):
                heads_here = 4 if unit % 3 == 0 else 2
                for h in range(heads_here):
                    dve.wait_ge(m["pe_sc"], hn + 1)
                    if hn >= 2:
                        dve.wait_ge(m["pe_o"], 2 + hn - 1)
                    b = 2 + 2 * (hn % 2)
                    s.fence()
                    s(dve.tensor_tensor(pT7, ps[:, b:b + 2].rearrange("p a (b c) -> p (a b) c", c=P)[:, 0:7],
                                        K["levels"], ALU.mult))
                    s.fence()
                    s(dve.tensor_reduce(pT_sum[:, hn % 2], pT7.rearrange("p l c -> p c l"), AX_X, ALU.add), m["dve_pT"])
                    hn += 1
                    if h == heads_here - 2 and unit + 1 < 3 * TT:
                        faded(unit + 1)
            dve.wait_ge(m["pool_qk"], 3 * TT)
            dve.wait_ge(m["pe_o"], 18)
            both = ps[:, 0:2].rearrange("p a b -> p (a b)")[:, 0:768]
            for n in range(NCH - 1):
                dve.wait_ge(m["pe_kv"], n + 1)
                if n == 0:
                    s(dve.tensor_tensor(states[:, 0], both, K["own"], ALU.mult), m["dve_state"])
                    continue
                s.fence()
                s(dve.tensor_tensor(kv_own, both, K["own"], ALU.mult))
                s.fence()
                for g, (a, wd) in enumerate(((0, 128), (128, 128), (256, 256), (512, 128), (640, 128))):
                    cd = K["ret_cdecay"][:, g:g + 1] if g < 2 else cdecay[:, g, n:n + 1]
                    ins = dve.scalar_tensor_tensor(out=states[:, n, a:a + wd], in0=states[:, n - 1, a:a + wd], scalar=cd,
                                                   in1=kv_own[:, a:a + wd], op0=ALU.mult, op1=ALU.add)
                s(ins, m["dve_state"])
            dve.wait_ge(m["act_o"], 3)
            for t in range(TT):
                dve.wait_ge(m["pe_inter"], 1 if t == 0 else 3)
                r = slice(64, 128) if t == 0 else slice(0, 128)
                src = ps[r, 2 + 2 * t:4 + 2 * t].rearrange("p a b -> p (a b)")
                s(dve.tensor_tensor(xn[r, t, 0:256], xn[r, t, 0:256], src[:, 0:256], ALU.add))
                s(dve.tensor_tensor(xn[r, t, 512:1024], xn[r, t, 512:1024], src[:, 256:768], ALU.add), m["dve_inter"])

            dve.wait_ge(m["act_sqB"], 1)
            hs = hstat[:, 0:16].rearrange("p (a b) -> p a b", b=8)
            s(dve.tensor_reduce(hs, squares.rearrange("p a (h c) -> p a h c", c=64), AX_X, ALU.add))
            s.fence()
            s(dve.tensor_scalar(hs, hs, EPS, None, ALU.add))
            s(dve.tensor_copy(g_exp.rearrange("p a (h c) -> p a h c", c=64), bc(g_b.unsqueeze(3), TT, 4, 64)), m["dve_b"])
            dve.wait_ge(m["pool_rsB"], 1)
            rs = hstat[:, 16:32].rearrange("p (a b) -> p a b", b=8)
            s(dve.tensor_scalar(rs[:, :, 0:4], rs[:, :, 0:4], 0.125, None, ALU.mult))
            s.fence()
            for t in range(TT):
                qk = z[:, t, 0:512].rearrange("p (h c) -> p h c", c=64)
                s(dve.tensor_tensor(qk, qk, bc(rs[:, t].unsqueeze(2), 8, 64), ALU.mult))
            s.fence()
            dve.wait_ge(m["act_gB"], 1)

            def heads(ap):
                return ap.rearrange("p (h c) -> p h c", c=64)
            for t in range(TT):
                b4, gm, tl = (bc(a_.unsqueeze(2), 4, 64) for a_ in (beta[:, t], natB[:, t, 0], natB[:, t, 1]))
                s(dve.tensor_tensor(heads(kb[:, t]), heads(z[:, t, 256:512]), b4, ALU.mult))
                s(dve.tensor_tensor(heads(qg[:, t]), heads(z[:, t, 0:256]), gm, ALU.mult))
                s(dve.tensor_tensor(heads(kt[:, t]), heads(z[:, t, 256:512]), tl, ALU.mult))
                s(dve.tensor_tensor(heads(z[:, t, 512:768]), heads(z[:, t, 512:768]), b4, ALU.mult))
                s.fence()
                s(dve.tensor_tensor(heads(kbg[:, t]), heads(kb[:, t]), gm, ALU.mult), m["dve_natB"] if t else None)
            for side, dst in enumerate((qTB, kTB, kbT, qgB)):
                dve.wait_ge(m["pe_tB"], side + 1)
                s(dve.tensor_copy(dst, ps[:, side, :].rearrange("p (a b) -> p a b", b=T)), m["dve_tB"])

            def four(ap):
                return ap.rearrange("p (a b) c -> p a b c", b=2)

            def bank(b):
                return ps[:, b, :].rearrange("p (a b) -> p a b", b=P)
            for t in range(TT):
                for h in range(4):
                    ins = dve.tensor_scalar(xB[:, place(h)], K["sums"][:, 7], g_b[:, t, h:h + 1], None, ALU.mult)
                s(ins, m["dve_xB"])
                dve.wait_ge(m["act_rB"], t + 1)
                s(dve.tensor_tensor(ratio_s, ratio_i, bc(K["strict"].unsqueeze(1), 4, P), ALU.mult))
                s.fence()
                s(dve.tensor_tensor(ratio_i, ratio_i, bc(K["incl"].unsqueeze(1), 4, P), ALU.mult))
                dve.wait_ge(m["pe_kkB"], t + 1)
                s(dve.tensor_tensor(four(nT), even_odd(0), four(ratio_s), ALU.mult))
                s.fence()
                s(dve.tensor_tensor(four(pB[:, t]), even_odd(2), four(ratio_i), ALU.mult))
                if t:
                    dve.wait_ge(m["pe_uvB"], 1)
                s(dve.tensor_tensor(nmT, nT, bc(K["levels"][:, 5].unsqueeze(1), 4, P), ALU.mult))
                s.fence()
                s(dve.tensor_tensor(xBT, bc(K["ident"].unsqueeze(1), 4, P), nmT, ALU.subtract), m["dve_xB"])
                dve.wait_ge(m["pe_xB"], t * 11 + 1)
                s.fence()
                s(dve.tensor_copy(xB, bank(2)))
                s(dve.tensor_tensor(nmT, nT, bc(K["levels"][:, 4].unsqueeze(1), 4, P), ALU.mult), m["dve_xB"])
                for lev in range(5):
                    for pair in range(2):
                        two = slice(2 * pair, 2 * pair + 2)
                        dve.wait_ge(m["pe_xB"], t * 11 + 2 + 2 * lev + pair)
                        s.fence()
                        if lev < 4:
                            s(dve.tensor_tensor(xB[:, two], xB[:, two], bank(pair)[:, 0:2], ALU.subtract))
                            s(dve.tensor_tensor(nmT[:, two], nT[:, two], bc(K["levels"][:, 3 - lev].unsqueeze(1), 2, P), ALU.mult))
                        s(dve.tensor_tensor(xBT[:, two], xBT[:, two], bank(pair)[:, 2:4], ALU.subtract), m["dve_xB"])
                if t == 0:
                    norm(1)
            tsplit(1, 1)
            dve.wait_ge(m["act_uvB"], 2)
            s.fence()
            s(dve.memset(stateB, 0.0), m["dve_sB"])
            for n in range(NCH):
                t, r = n // 2, slice(64 * (n % 2), 64 * (n % 2) + 64)
                dve.wait_ge(m["pe_wB"], n + 1)
                s(dve.tensor_tensor(u_nat[r, t], uv[r, t], ps[r, 0, 0:256], ALU.subtract), m["dve_uB"])
                if n == NCH - 1:
                    dve.wait_ge(m["pe_oB"], n + 1)
                    s(dve.memset(stateB, 0.0), m["dve_sB"])
                else:
                    dve.wait_ge(m["pe_sB"], n + 1)
                    s(dve.tensor_tensor(kuB, ps[:, 1, 0:256], K["own"][:, 0:256], ALU.mult))
                    s.fence()
                    for p in range(2):
                        ins = dve.scalar_tensor_tensor(out=stateB[:, p * P:(p + 1) * P], in0=stateB[:, p * P:(p + 1) * P],
                                                       scalar=decB[:, p, n:n + 1], in1=kuB[:, p * P:(p + 1) * P],
                                                       op0=ALU.mult, op1=ALU.add)
                    s(ins, m["dve_sB"])
                if n:
                    split_now(C_K + n + 1)
            split_now(C_V + 1)
            dve.wait_ge(m["act_osq"], 1)
            hs = hstat[:, 64:96].rearrange("p (a b) -> p a b", b=16)
            s(dve.tensor_reduce(hs, area(4096, TT, D).rearrange("p a (h c) -> p a h c", c=64), AX_X, ALU.add))
            s.fence()
            s(dve.tensor_scalar(hs, hs, 1.0 / 64, EPS, ALU.mult, ALU.add), m["dve_onorm"])
            splits_only(C_V, 4)
            for t in range(TT):
                dve.wait_ge(m["pool_ors"], t + 1)
                o = xn[:, t].rearrange("p (h c) -> p h c", c=64)
                s(dve.tensor_tensor(o, o, bc(hstat[:, 32 + 16 * t:48 + 16 * t].unsqueeze(2), 16, 64), ALU.mult))
                s.fence()
                s(dve.tensor_tensor(xn[:, t], xn[:, t], z[:, t, ZG:ZG + D], ALU.mult), m["dve_on"])

            dve.wait_ge(used, 2 * (C_V + 4))
            tsplit(2, None)
            split_now(C_OUT + 1)
            residual(C_OUT, 3)
            norm(2)
            tsplit(3, 2)
            split_now(C_Q + 1)
            splits_only(C_Q, 4)
            attention(0, CROSS)
            oT_low(0)
            split_now(C_O + 1)
            residual(C_O, 6)
            norm(3)
            tsplit(4, 3)
            split_now(C_FFN + 1)
            ffn(C_FFN, 0, 9)
            norm(4, res, area(2048, D), res_out)
            for l in range(LAYERS):
                b = C_LAYER + l * LAYER_CHUNKS
                norm(5 + 2 * l)
                tsplit(5 + 2 * l, 4 + 2 * l, first_parts(b))
                split_now(b + 1)
                def latents(i):
                    if i == 2:
                        dve.wait_ge(l_["act_ss"], 4 * (l + 1))
                        st = lstat[:, 0:8].rearrange("p (k a b) -> p k a b", k=2, b=2)
                        s(dve.tensor_scalar(st[:, 1, :, 0], st[:, 0, :, 0], 1.0 / 256, EPS, ALU.mult, ALU.add))
                        s(dve.tensor_scalar(st[:, 1, :, 1], st[:, 0, :, 1], 1.0 / 128, EPS, ALU.mult, ALU.add), l_["dve_ms"])
                        dve.wait_ge(l_["pool_rs"], l + 1)
                        for t in range(TT):
                            for j, (c, n) in enumerate(((YCQ, 256), (YKV, 128))):
                                ins = dve.tensor_scalar(z[:, t, c:c + n], z[:, t, c:c + n], lstat[:, 8 + 2 * t + j:9 + 2 * t + j], None, ALU.mult)
                        s(ins, l_["dve_n"])
                    if i == 3:
                        for t in range(TT):
                            dve.wait_ge(l_["pe_lat"], 2 * l + t + 1)
                            s(dve.tensor_tensor(latT[:, :, t * P:(t + 1) * P], ps[:, 4 + t, 0:384].rearrange("p (a b) -> p a b", b=P),
                                                bc(G["g_lat"][:, l].unsqueeze(2), 3, P), ALU.mult), l_["dve_lat"])
                    if i == 5:
                        rotations()

                def rotations():
                    def quad(n, *shape):
                        return [shaped(xn[:].rearrange("p a b -> p (a b)")[:, i * 384:i * 384 + n], shape) for i in range(4)]
                    dve.wait_ge(z_out, IN_CHUNKS + l * IN2_CHUNKS + 6)
                    hd = z[:, :, YDQ:YDQ + 1536].rearrange("p a (h c) -> p a h c", c=64)
                    rotate(hd[:, :, :, 0:8], hd[:, :, :, 8:16], *(bc(K[n].unsqueeze(2), TT, 24, 8) for n in ("cos_h", "sin_h")),
                           quad(384, TT, 24, 8))
                    ix = z[:, :, YQI:YQI + 288].rearrange("p a (h c) -> p a h c", c=32)
                    s.fence()
                    rotate(ix[:, :, :, 0:4], ix[:, :, :, 4:8], *(bc(K[n].unsqueeze(2), TT, 9, 4) for n in ("cos_i", "sin_i")),
                           quad(72, TT, 9, 4))
                    s.fence()
                    kp = z[:, :, YPE:YPE + 32]
                    rotate(kp[:, :, 0:16], kp[:, :, 16:32], K["cos_a"], K["sin_a"], quad(32, TT, 16))
                    dve.wait_ge(l_["act_up"], 2 * (l + 1))
                    s.fence()
                    mq = z[:, :, 3024:3408].rearrange("p a (h c) -> p a h c", c=96)
                    rotate(mq[:, :, :, 64:80], mq[:, :, :, 80:96], *(bc(K[n].unsqueeze(2), TT, 4, 16) for n in ("cos_a", "sin_a")),
                           quad(128, TT, 4, 16))
                    s.fence()
                    s(dve.tensor_copy(z[:, :, 3408:3792].rearrange("p a (h c) -> p a h c", c=96)[:, :, :, 64:96],
                                      bc(kp.unsqueeze(2), TT, 4, 32)))
                    s(dve.tensor_copy(z[:, :, 0:128].rearrange("p a (h c) -> p a h c", c=32),
                                      bc(z[:, :, YKI:YKI + 32].unsqueeze(2), TT, 4, 32)), l_["dve_rope"])

                section(dve, b, IN2_CHUNKS, 0, 0, split, lambda i, slot: None, between=latents)
                dve.wait_ge(z_out, IN_CHUNKS + (l + 1) * IN2_CHUNKS)
                s(dve.tensor_scalar(wis[:], z[:, :, YWI:YWI + 8], 256 ** -0.5, None, ALU.mult))
                for n in range(1, 12, 2):
                    t, g = n // 6, n % 6
                    dve.wait_ge(l_["pe_tT"], 12 * l + n + 1)
                    r, k = 96 if g < 2 else P, 3 if g == 5 else 4
                    s(dve.tensor_copy(tT[0:r, 4 * g:4 * g + k, t * P:(t + 1) * P],
                                      ps[0:r, (n + 4) % 8, 0:k * P].rearrange("p (a b) -> p a b", b=P)), l_["dve_tT"])
                for t in range(TT):
                    n = P * (t + 1)
                    dve.wait_ge(l_["act_relu"], 2 * l + t + 1)
                    for h in range(8):
                        if h:
                            s.fence()
                        s(dve.scalar_tensor_tensor(out=score[t][:, 0:n], in0=relus[t][:, 2 * (h % 4) + h // 4, 0:n], scalar=wis[:, t, h:h + 1],
                                                   in1=K["causal"][:, t, 0:n] if h == 0 else score[t][:, 0:n],
                                                   op0=ALU.mult, op1=ALU.add))
                s.fence()
                rounds = TOPK // 8

                def best_keys(step):
                    t, i = divmod(step, rounds + 1)
                    n = P * (t + 1)
                    src = score[t][:, 0:n] if i == 0 else work[:, 0:n]
                    s.fence()
                    if i < rounds:
                        s(dve.max(best, src))
                        s.fence()
                        s(dve.match_replace(work[:, 0:n], best, src, -3.0e38))
                        return
                    s(dve.tensor_tensor(work[:, 0:n], src, score[t][:, 0:n], ALU.is_equal))
                    s.fence()
                    s(dve.scalar_tensor_tensor(out=dsa_mask[:, t, 0:n], in0=work[:, 0:n], scalar=NEG, in1=K["causal"][:, t, 0:n],
                                               op0=ALU.mult, op1=ALU.add))
                    s.fence()

                def between(i):
                    before, steps = len(LAYER) * 3 // 4, 2 * (rounds + 1)
                    if i < before:
                        for step in range(i * steps // before, (i + 1) * steps // before):
                            best_keys(step)
                attention(first_pair(l), LAYER, between)
                oT_low(4 * (l + 1))
                split_now(b + IN2_CHUNKS + 1)
                residual(b + IN2_CHUNKS, 11 + 5 * l)
                norm(6 + 2 * l)
                tsplit(6 + 2 * l, 5 + 2 * l)
                split_now(b + IN2_CHUNKS + 5)
                ffn(b + IN2_CHUNKS + 4, l + 1, 14 + 5 * l)
            norm(9, xn, area(2048, D), m["dve_out"])


def pack_columns(w, cols):
    n = w.shape[1] // cols
    return np.ascontiguousarray(w.reshape(KT, P, n, cols).transpose(2, 1, 0, 3)).reshape(n, P, KT * cols)


def pack_rows(w):
    return np.ascontiguousarray(w.reshape(4, 2, P, D).transpose(0, 2, 1, 3)).reshape(4, P, 2 * D)


def pack_ffn(up, down):
    u = up.reshape(KT, P, 2, NFT, P).transpose(3, 1, 0, 2, 4).reshape(NFT, P, KT * 2 * P)
    d = down.reshape(NFT, P, D)
    mid = np.concatenate([u[1:], d[:-1]], axis=2)
    last = d[-1].reshape(P, 2, D // 2).transpose(1, 0, 2)
    return u[:1], mid, last


def kernel(**inputs):
    import concourse.bacc as bacc
    from concourse.bass_utils import run_bass_kernel_spmd

    a = {k: np.asarray(v) for k, v in inputs.items()}

    def by_partition(rows_):
        v = rows_.reshape(*rows_.shape[:-1], -1, P)
        return np.moveaxis(v, -1, 0).reshape(P, -1)

    arrays = {
        "x": np.ascontiguousarray(a["x"].reshape(TT, P, D).transpose(1, 0, 2)),
        "mem": np.ascontiguousarray(a["mem"].reshape(TT, P, D).transpose(1, 0, 2)),
        "pos": np.ascontiguousarray(a["positions"].reshape(TT, P).T),
    }
    made = shape_constants()
    arrays["consts"] = np.concatenate([made[n].reshape(P, -1) for n in CONSTS], axis=1)
    gains = np.stack([a["mix_norm_w"][0], a["mem_norm_w"], a["xattn_norm_w"][0], a["ffn_norm_w"][0],
                      a["g_attn_2"][0], a["g_ffn_2"][0], a["g_attn_2"][1], a["g_ffn_2"][1]])
    lat = np.concatenate([a["g_q_lat_2"], a["g_kv_lat_2"]], axis=1)
    convs = np.concatenate([a["ffn_conv_w"], a["conv_w_2"]], axis=0)
    convs = convs.reshape(3, 3, 2, NFT, P).transpose(4, 0, 3, 2, 1).reshape(P, -1)
    bias = np.concatenate([np.zeros((1, 2 * FF), np.float32), a["conv_b_2"]], axis=0)
    bias = bias.reshape(3, 2, NFT, P).transpose(3, 0, 2, 1).reshape(P, -1)
    gdn = a["gdn_conv_w"][0].reshape(4, 6, P).transpose(2, 1, 0).reshape(P, -1)
    arrays["params"] = np.concatenate([by_partition(gains), by_partition(lat), gdn, convs, bias], axis=1)
    arrays["rows"] = np.concatenate([a["gdn_a_log"][0], a["gdn_dt_bias"][0], a["gla_gk_bias"][0], a["gdn_norm_w"][0],
                                     a["gla_norm_w"][0], a["hgrn_norm_w"][0]])
    arrays["gfinal"] = np.stack([a["final_norm_w"], a["g_final_2"]])
    arrays["gkup"] = a["gla_gk_up"][0]
    uq = a["w_uq_2"].reshape(LAYERS, 2, P, 384).transpose(0, 2, 1, 3).reshape(LAYERS, P, 768)
    arrays["lat"] = np.concatenate([uq, a["w_ukv_2"]], axis=2)

    w = a["w_in"][0]
    at = np.cumsum([0, 256, 256, 256, 256, 256, 256, 256, 4, 4, 256, 128, 128, 256, 16, 256, 256, 256, 256, 256])
    names = "rq rk rv rg bq bk bv ba bb bg cq ck cv lr cg dq df di dg".split()
    col = {n: w[:, at[i]:at[i + 1]] for i, n in enumerate(names)}
    order = "bq bk bv cq ck dq df rq rk rv cv di rg bg cg dg lr ba bb".split()
    w = np.concatenate([col[n] for n in order] + [np.zeros((D, ZW - 3864), np.float32)], axis=1)
    arrays["win"] = pack_columns(w, IN_COLS)
    arrays["wk"] = pack_columns(a["xattn_wk"][0], 256)
    arrays["wv"] = pack_rows(a["xattn_wv"][0])
    arrays["wout"] = pack_rows(a["w_out"][0])
    arrays["wq"] = pack_columns(a["xattn_wq"][0], 256)
    arrays["wo"] = pack_rows(a["xattn_wo"][0])
    ffns = [pack_ffn(a["ffn_up"][0], a["ffn_down"][0])]
    ffns += [pack_ffn(a["w_up_2"][l], a["w_down_2"][l]) for l in range(LAYERS)]
    for i, n in enumerate("abc"):
        arrays["ffn_" + n] = np.concatenate([f[i] for f in ffns], axis=0)
    win2 = []
    for l in range(LAYERS):
        w = a["w_in_2"][l]
        dil, dsa, rest = w[:, 416:1952], w[:, 1952:2720], w[:, 2720:]
        w = np.concatenate([w[:, :416], dil[:, :1024], dsa[:, :512], rest[:, :288], dil[:, 1024:], dsa[:, 512:],
                            rest[:, 288:296], np.zeros((D, YW - 3016), np.float32)], axis=1)
        win2.append(pack_columns(w, IN2_COLS))
    arrays["win2"] = np.concatenate(win2)
    arrays["wo2"] = np.concatenate([pack_rows(a["w_o_2"][l]) for l in range(LAYERS)])

    nc = bacc.Bacc("TRN2", target_bir_lowering=False, num_devices=1)
    arrays = {f"in_{k}": np.ascontiguousarray(v) for k, v in arrays.items()}
    aps = {k[3:] + "_d": nc.dram_tensor(k, v.shape, mybir.dt.from_np(v.dtype), kind="ExternalInput").ap()
           for k, v in arrays.items()}
    out = nc.dram_tensor("out", (P, TT, D), F32, kind="ExternalOutput").ap()
    hybrid_two_block_kernel(nc, out_d=out, **aps)
    r = run_bass_kernel_spmd(nc, [arrays], core_ids=[0])
    return np.asarray(r.results[0]["out"]).transpose(1, 0, 2).reshape(1, T, D)
```
